# Optimizing a Trainium2 kernel written in Bass

```python
import math
import jax, jax.numpy as jnp
from jax import lax
import numpy as np

D_MODEL = 1024
BATCH = 1
SEQ = 512
DEPTH = 1

MIX_WIDTH = D_MODEL
MOBA_WIDTH = MIX_WIDTH // 2
MOBA_HEAD_DIM = 64
MOBA_HEADS = MOBA_WIDTH // MOBA_HEAD_DIM
MOBA_BLOCK = 256
MOBA_TOPK = 3
QUERY_CHUNK = 128
GDN_WIDTH = MIX_WIDTH - MOBA_WIDTH
GDN_HEAD_DIM = 128
GDN_HEADS = GDN_WIDTH // GDN_HEAD_DIM
GDN_CONV = 4
GDN_CHUNK = 64
IN_SPLITS = (MOBA_WIDTH,) * 4 + (GDN_WIDTH,) * 4 + (GDN_HEADS, GDN_HEADS)
IN_WIDTH = sum(IN_SPLITS)
RMS_EPS = 1e-6
NEG_INF = -1e30


def rms_norm(x, w):
    xf = x.astype(jnp.float32)
    y = xf * lax.rsqrt(jnp.mean(xf * xf, axis=-1, keepdims=True) + RMS_EPS)
    return (y * w.astype(jnp.float32)).astype(x.dtype)

def alibi_slopes(n_heads):
    start = 2.0 ** (-8.0 / n_heads)
    return jnp.asarray(start ** np.arange(1, n_heads + 1), dtype=jnp.float32)

def moba_attention(q, k, v):
    B, T, H, dh = q.shape
    nb = -(-T // MOBA_BLOCK)
    pad = nb * MOBA_BLOCK - T
    n_qc = T // QUERY_CHUNK
    k_sel = min(MOBA_TOPK, nb - 1)
    scale = dh ** -0.5
    slopes = alibi_slopes(H)
    qh = q.transpose(0, 2, 1, 3)
    pad_cfg = ((0, 0), (0, pad), (0, 0), (0, 0))
    kb = jnp.pad(k, pad_cfg).reshape(B, nb, MOBA_BLOCK, H, dh).transpose(0, 3, 1, 2, 4)
    vb = jnp.pad(v, pad_cfg).reshape(B, nb, MOBA_BLOCK, H, dh).transpose(0, 3, 1, 2, 4)
    kbar = jnp.mean(kb.astype(jnp.float32), axis=3)
    blk_off = jnp.arange(MOBA_BLOCK)
    head_idx = jnp.arange(H)[:, None, None]

    def chunk_attend(step):
        bi = step // n_qc
        q0 = (step % n_qc) * QUERY_CHUNK
        own = q0 // MOBA_BLOCK
        qc = lax.dynamic_slice_in_dim(qh[bi], q0, QUERY_CHUNK, axis=1)
        kb_b, vb_b = kb[bi], vb[bi]
        t_pos = q0 + jnp.arange(QUERY_CHUNK)
        k_own = lax.dynamic_index_in_dim(kb_b, own, axis=1, keepdims=False)
        v_own = lax.dynamic_index_in_dim(vb_b, own, axis=1, keepdims=False)
        dist_own = (t_pos[:, None] - (own * MOBA_BLOCK + blk_off)[None, :]).astype(jnp.float32)
        logit_own = (jnp.einsum('hqd,hkd->hqk', qc, k_own).astype(jnp.float32) * scale
                     - slopes[:, None, None] * dist_own)
        logit_own = jnp.where(dist_own >= 0, logit_own, NEG_INF)
        if k_sel == 0:
            p = jax.nn.softmax(logit_own, axis=-1).astype(v.dtype)
            return jnp.einsum('hqk,hkd->hqd', p, v_own)
        gate = jnp.einsum('hqd,hnd->hqn', qc.astype(jnp.float32), kbar[bi])
        gate = jnp.where(jnp.arange(nb) < own, gate, NEG_INF)
        _, sel = lax.top_k(gate, k_sel)
        k_g = kb_b[head_idx, sel]
        v_g = vb_b[head_idx, sel]
        s_sel = sel[..., None] * MOBA_BLOCK + blk_off
        dist_sel = (t_pos[None, :, None, None] - s_sel).astype(jnp.float32)
        logit_sel = (jnp.einsum('hqd,hqnkd->hqnk', qc, k_g).astype(jnp.float32) * scale
                     - slopes[:, None, None, None] * dist_sel)
        valid = (jnp.arange(k_sel) < own)[None, None, :, None]
        logit_sel = jnp.where(valid, logit_sel, NEG_INF).reshape(H, QUERY_CHUNK, k_sel * MOBA_BLOCK)
        p = jax.nn.softmax(jnp.concatenate([logit_sel, logit_own], axis=-1), axis=-1).astype(v.dtype)
        p_sel = p[..., :k_sel * MOBA_BLOCK].reshape(H, QUERY_CHUNK, k_sel, MOBA_BLOCK)
        p_own = p[..., k_sel * MOBA_BLOCK:]
        return (jnp.einsum('hqnk,hqnkd->hqd', p_sel, v_g)
                + jnp.einsum('hqk,hkd->hqd', p_own, v_own))

    out = lax.map(chunk_attend, jnp.arange(B * n_qc))
    out = out.reshape(B, n_qc, H, QUERY_CHUNK, dh).transpose(0, 1, 3, 2, 4)
    return out.reshape(B, T, H * dh)

def causal_depthwise_conv(x, w):
    K, C = w.shape
    return lax.conv_general_dilated(
        x, w[:, None, :].astype(x.dtype), window_strides=(1,), padding=((K - 1, 0),),
        dimension_numbers=('NWC', 'WIO', 'NWC'), feature_group_count=C)

def l2_normalize(x):
    return x * lax.rsqrt(jnp.sum(x * x, axis=-1, keepdims=True) + RMS_EPS)

def gated_delta_rule(q, k, v, g, beta):
    B, T, H, dk = q.shape
    dv = v.shape[-1]
    C = GDN_CHUNK
    nc = T // C
    q = l2_normalize(q) * (dk ** -0.5)
    k = l2_normalize(k)

    def chunks(t):
        return t.reshape(B, nc, C, H, -1).transpose(1, 0, 3, 2, 4)

    q, k, v = chunks(q), chunks(k), chunks(v)
    beta = beta.reshape(B, nc, C, H).transpose(1, 0, 3, 2)
    gc = jnp.cumsum(g.reshape(B, nc, C, H).transpose(1, 0, 3, 2), axis=-1)
    causal = jnp.tril(jnp.ones((C, C), dtype=bool))
    strict = jnp.tril(jnp.ones((C, C), dtype=bool), -1)
    decay = jnp.exp(jnp.where(causal, gc[..., :, None] - gc[..., None, :], -jnp.inf))
    k_beta = k * beta[..., None]
    a = jnp.where(strict, jnp.einsum('nbhid,nbhjd->nbhij', k_beta, k) * decay, 0.0)
    eye = jnp.eye(C, dtype=jnp.float32)
    t_inv = lax.linalg.triangular_solve(a + eye, jnp.broadcast_to(eye, a.shape),
                                        left_side=True, lower=True, unit_diagonal=True)
    u = t_inv @ (v * beta[..., None])
    w = t_inv @ (k_beta * jnp.exp(gc)[..., None])
    intra = jnp.where(causal, jnp.einsum('nbhid,nbhjd->nbhij', q, k) * decay, 0.0)
    q_dec = q * jnp.exp(gc)[..., None]
    k_dec = k * jnp.exp(gc[..., -1:] - gc)[..., None]
    g_last = jnp.exp(gc[..., -1])

    def step(S, xs):
        q_i, k_i, u_i, w_i, intra_i, gl = xs
        v_new = u_i - w_i @ S
        o = q_i @ S + intra_i @ v_new
        S = S * gl[..., None, None] + jnp.einsum('bhcd,bhce->bhde', k_i, v_new)
        return S, o

    S0 = jnp.zeros((B, H, dk, dv), dtype=jnp.float32)
    _, o = lax.scan(step, S0, (q_dec, k_dec, u, w, intra, g_last))
    return o.transpose(1, 0, 3, 2, 4).reshape(B, T, H, dv)

def hybrid_layer(x, norm_pre_w, w_in, conv_w, a_log, dt_bias, gdn_norm_w, w_out, norm_post_w):
    B, T, _ = x.shape
    h = rms_norm(x, norm_pre_w)
    proj = h @ w_in.astype(x.dtype)
    split_at = list(np.cumsum(IN_SPLITS)[:-1])
    a_q, a_k, a_v, a_z, d_q, d_k, d_v, d_z, d_b, d_a = jnp.split(proj, split_at, axis=-1)

    heads_a = lambda t: t.reshape(B, T, MOBA_HEADS, MOBA_HEAD_DIM)
    moba_out = moba_attention(heads_a(a_q), heads_a(a_k), heads_a(a_v)) * jax.nn.silu(a_z)

    qkv = jax.nn.silu(causal_depthwise_conv(jnp.concatenate([d_q, d_k, d_v], axis=-1), conv_w))
    g_q, g_k, g_v = jnp.split(qkv, 3, axis=-1)
    heads_b = lambda t: t.reshape(B, T, GDN_HEADS, GDN_HEAD_DIM).astype(jnp.float32)
    beta = jax.nn.sigmoid(d_b.astype(jnp.float32))
    g = -jnp.exp(a_log.astype(jnp.float32)) * jax.nn.softplus(
        d_a.astype(jnp.float32) + dt_bias.astype(jnp.float32))
    o = gated_delta_rule(heads_b(g_q), heads_b(g_k), heads_b(g_v), g, beta)
    gdn_out = rms_norm(o, gdn_norm_w).reshape(B, T, GDN_WIDTH).astype(x.dtype) * jax.nn.silu(d_z)

    mixed = jnp.concatenate([moba_out, gdn_out], axis=-1) @ w_out.astype(x.dtype)
    return x + rms_norm(mixed, norm_post_w)

def first_inputs(seed: int = 0) -> dict:
    key = jax.random.key(seed)
    ks = jax.random.split(key, 9)
    f32 = jnp.float32
    x = jax.random.normal(ks[0], (BATCH, SEQ, D_MODEL), f32)
    norm_pre_w = 1.0 + 0.05 * jax.random.normal(ks[1], (DEPTH, D_MODEL), f32)
    w_in = jax.random.normal(ks[2], (DEPTH, D_MODEL, IN_WIDTH), f32) * D_MODEL ** -0.5
    conv_w = jax.random.normal(ks[3], (DEPTH, GDN_CONV, 3 * GDN_WIDTH), f32) * GDN_CONV ** -0.5
    a_log = jnp.log(jax.random.uniform(ks[4], (DEPTH, GDN_HEADS), f32, minval=1.0, maxval=16.0))
    dt = jnp.exp(jax.random.uniform(ks[5], (DEPTH, GDN_HEADS), f32,
                                    minval=math.log(1e-3), maxval=math.log(1e-1)))
    dt_bias = dt + jnp.log(-jnp.expm1(-dt))
    gdn_norm_w = 1.0 + 0.05 * jax.random.normal(ks[6], (DEPTH, GDN_HEAD_DIM), f32)
    w_out = jax.random.normal(ks[7], (DEPTH, MIX_WIDTH, D_MODEL), f32) * MIX_WIDTH ** -0.5
    norm_post_w = 1.0 + 0.05 * jax.random.normal(ks[8], (DEPTH, D_MODEL), f32)
    return {"x": x, "norm_pre_w": norm_pre_w, "w_in": w_in, "conv_w": conv_w,
            "a_log": a_log, "dt_bias": dt_bias, "gdn_norm_w": gdn_norm_w,
            "w_out": w_out, "norm_post_w": norm_post_w}

def first_block(x, norm_pre_w, w_in, conv_w, a_log, dt_bias, gdn_norm_w, w_out, norm_post_w):
    for layer in range(DEPTH):
        x = hybrid_layer(x, norm_pre_w[layer], w_in[layer], conv_w[layer], a_log[layer],
                         dt_bias[layer], gdn_norm_w[layer], w_out[layer], norm_post_w[layer])
    return x


CHUNK = 64
EPS = 1e-6

LRU_WIDTH = D_MODEL
LRU_HEADS = 8
LRU_HEAD_DIM = LRU_WIDTH // LRU_HEADS
LRU_CONV = 4
LRU_C = 8.0

CONV_WIDTH = D_MODEL
CONV_GROUPS = 8
CONV_K = 3

N_BRANCHES = 2
IN_COLS = 2 * LRU_WIDTH + 3 * CONV_WIDTH + N_BRANCHES * D_MODEL

PEER_HEADS = 8
PEER_NKEYS = 128
PEER_N = PEER_NKEYS * PEER_NKEYS
PEER_DKEY = 256
PEER_HALF = PEER_DKEY // 2
PEER_TOPK = 16
PEER_BLOCK = 128


def rmsnorm(x, g):
    xf = x.astype(jnp.float32)
    y = xf * lax.rsqrt(jnp.mean(xf * xf, axis=-1, keepdims=True) + EPS)
    return (y * g.astype(jnp.float32)).astype(x.dtype)

def causal_dwconv(x, w):
    k, c = w.shape
    return lax.conv_general_dilated(
        x, w[:, None, :].astype(x.dtype), window_strides=(1,), padding=[(k - 1, 0)],
        dimension_numbers=("NWC", "WIO", "NWC"), feature_group_count=c)

def rg_lru(x, w_a, b_a, w_x, b_x, lam):
    b, s, _ = x.shape
    xh = x.reshape(b, s, LRU_HEADS, LRU_HEAD_DIM)
    r = jax.nn.sigmoid(jnp.einsum("bshi,hij->bshj", xh, w_a).reshape(b, s, LRU_WIDTH) + b_a)
    i = jax.nn.sigmoid(jnp.einsum("bshi,hij->bshj", xh, w_x).reshape(b, s, LRU_WIDTH) + b_x)
    log_a = (-LRU_C * r.astype(jnp.float32)) * jax.nn.softplus(-lam.astype(jnp.float32))
    a = jnp.exp(log_a)
    mult = jnp.sqrt(-jnp.expm1(2.0 * log_a))
    u = mult * (i * x).astype(jnp.float32)

    def combine(left, right):
        a1, b1 = left
        a2, b2 = right
        return a1 * a2, a2 * b1 + b2

    _, h = lax.associative_scan(combine, (a, u), axis=1)
    return h.astype(x.dtype)

def token_mixers(xn, w_in, conv_a_w, conv_a_b, w_a, b_a, w_x, b_x, lam, conv_b_w, w_out):
    p = xn @ w_in
    splits = [LRU_WIDTH, 2 * LRU_WIDTH, 2 * LRU_WIDTH + CONV_WIDTH,
              2 * LRU_WIDTH + 2 * CONV_WIDTH, 2 * LRU_WIDTH + 3 * CONV_WIDTH,
              2 * LRU_WIDTH + 3 * CONV_WIDTH + D_MODEL]
    xa, ga, vb, bb, cb, ma, mb = jnp.split(p, splits, axis=-1)
    ya = rg_lru(causal_dwconv(xa, conv_a_w) + conv_a_b, w_a, b_a, w_x, b_x, lam) * jax.nn.gelu(ga)
    yb = bb * causal_dwconv(cb * vb, conv_b_w)
    merged = jax.nn.sigmoid(ma) * ya + jax.nn.sigmoid(mb) * yb
    return merged @ w_out

def peer(xn, w_q, sub_keys, u_tab, v_tab):
    b, s, d = xn.shape
    t = xn.reshape(-1, d)
    n_tok = t.shape[0]
    q = (t @ w_q).reshape(n_tok, PEER_HEADS, 2, PEER_HALF)
    sc = jnp.einsum("thpk,hpnk->thpn", q, sub_keys).astype(jnp.float32)
    s_top, i_top = lax.top_k(sc, PEER_TOPK)
    cand = s_top[:, :, 0, :, None] + s_top[:, :, 1, None, :]
    cand_idx = i_top[:, :, 0, :, None] * PEER_NKEYS + i_top[:, :, 1, None, :]
    kk = PEER_TOPK * PEER_TOPK
    best, pos = lax.top_k(cand.reshape(n_tok, PEER_HEADS, kk), PEER_TOPK)
    idx = jnp.take_along_axis(cand_idx.reshape(n_tok, PEER_HEADS, kk), pos, axis=-1)
    g = jax.nn.softmax(best, axis=-1).astype(xn.dtype)

    nb = n_tok // PEER_BLOCK

    def block(args):
        tb, ib, gb = args
        ue = u_tab[ib]
        act = jax.nn.gelu(jnp.einsum("phkd,pd->phk", ue, tb))
        ve = v_tab[ib]
        return jnp.einsum("phk,phkd->pd", gb * act, ve)

    out = lax.map(block, (t.reshape(nb, PEER_BLOCK, d),
                          idx.reshape(nb, PEER_BLOCK, PEER_HEADS, PEER_TOPK),
                          g.reshape(nb, PEER_BLOCK, PEER_HEADS, PEER_TOPK)))
    return out.reshape(b, s, d)

def second_inputs(seed: int = 0) -> dict:
    key = jax.random.key(seed)
    ks = jax.random.split(key, 20)
    f = jnp.float32
    L = DEPTH

    def nrm(k, shape, scale):
        return jax.random.normal(k, shape, f) * scale

    x = nrm(ks[0], (BATCH, SEQ, D_MODEL), 1.0)
    norm1_g = 1.0 + nrm(ks[1], (L, D_MODEL), 0.02)
    w_in = nrm(ks[2], (L, D_MODEL, IN_COLS), D_MODEL ** -0.5)
    conv_a_w = nrm(ks[3], (L, LRU_CONV, LRU_WIDTH), LRU_CONV ** -0.5)
    conv_a_b = nrm(ks[4], (L, LRU_WIDTH), 0.01)
    w_a = nrm(ks[5], (L, LRU_HEADS, LRU_HEAD_DIM, LRU_HEAD_DIM), LRU_HEAD_DIM ** -0.5)
    b_a = nrm(ks[6], (L, LRU_WIDTH), 0.01)
    w_x = nrm(ks[7], (L, LRU_HEADS, LRU_HEAD_DIM, LRU_HEAD_DIM), LRU_HEAD_DIM ** -0.5)
    b_x = nrm(ks[8], (L, LRU_WIDTH), 0.01)
    a_init = jax.random.uniform(ks[9], (L, LRU_WIDTH), f, 0.9, 0.999)
    sig = a_init ** (1.0 / LRU_C)
    lru_lambda = jnp.log(sig) - jnp.log1p(-sig)
    conv_b_w = nrm(ks[10], (L, CONV_K, CONV_WIDTH), CONV_K ** -0.5)
    w_out = nrm(ks[11], (L, D_MODEL, D_MODEL), D_MODEL ** -0.5)
    norm2_g = 1.0 + nrm(ks[12], (L, D_MODEL), 0.02)
    peer_wq = nrm(ks[13], (L, D_MODEL, PEER_HEADS * PEER_DKEY), D_MODEL ** -0.5)
    peer_subkeys = nrm(ks[14], (L, PEER_HEADS, 2, PEER_NKEYS, PEER_HALF), PEER_HALF ** -0.5)
    peer_u = nrm(ks[15], (L, PEER_N, D_MODEL), D_MODEL ** -0.5)
    peer_v = nrm(ks[16], (L, PEER_N, D_MODEL), PEER_HEADS ** -0.5)
    final_g = 1.0 + nrm(ks[17], (D_MODEL,), 0.02)
    return {"x": x, "norm1_g": norm1_g, "w_in": w_in, "conv_a_w": conv_a_w, "conv_a_b": conv_a_b,
            "w_a": w_a, "b_a": b_a, "w_x": w_x, "b_x": b_x, "lru_lambda": lru_lambda,
            "conv_b_w": conv_b_w, "w_out": w_out, "norm2_g": norm2_g, "peer_wq": peer_wq,
            "peer_subkeys": peer_subkeys, "peer_u": peer_u, "peer_v": peer_v, "final_g": final_g}

def second_block(x, norm1_g, w_in, conv_a_w, conv_a_b, w_a, b_a, w_x, b_x, lru_lambda,
              conv_b_w, w_out, norm2_g, peer_wq, peer_subkeys, peer_u, peer_v, final_g):
    h = x
    for l in range(DEPTH):
        xn = rmsnorm(h, norm1_g[l])
        h = h + token_mixers(xn, w_in[l], conv_a_w[l], conv_a_b[l], w_a[l], b_a[l], w_x[l], b_x[l],
                             lru_lambda[l], conv_b_w[l], w_out[l])
        h = h + peer(rmsnorm(h, norm2_g[l]), peer_wq[l], peer_subkeys[l], peer_u[l], peer_v[l])
    return rmsnorm(h, final_g)


def setup_inputs(seed=0):
    out = dict(first_inputs(seed))
    for name, value in second_inputs(seed + 1).items():
        if name != "x":
            out[name + "_2"] = value
    return out


def reference(
    x, norm_pre_w, w_in, conv_w, a_log, dt_bias, gdn_norm_w, w_out, norm_post_w, norm1_g_2,
    w_in_2, conv_a_w_2, conv_a_b_2, w_a_2, b_a_2, w_x_2, b_x_2, lru_lambda_2, conv_b_w_2,
    w_out_2, norm2_g_2, peer_wq_2, peer_subkeys_2, peer_u_2, peer_v_2, final_g_2,
):
    x = first_block(
        x, norm_pre_w, w_in, conv_w, a_log, dt_bias, gdn_norm_w, w_out, norm_post_w,
    )
    return second_block(
        x, norm1_g_2, w_in_2, conv_a_w_2, conv_a_b_2, w_a_2, b_a_2, w_x_2, b_x_2, lru_lambda_2,
        conv_b_w_2, w_out_2, norm2_g_2, peer_wq_2, peer_subkeys_2, peer_u_2, peer_v_2,
        final_g_2,
    )


_drawn_inputs = setup_inputs


def setup_inputs(seed=0):
    import zlib

    import numpy as np

    out = dict(_drawn_inputs(seed))
    spreads = {}
    factors = {'norm1_g_2': 2.831,
     'conv_a_b_2': 15.427,
     'b_a_2': 64.0,
     'b_x_2': 64.0,
     'norm2_g_2': 26.392,
     'final_g_2': 8.077}
    for name, (base, spread) in spreads.items():
        noise = np.random.default_rng([zlib.crc32(name.encode()), seed]).standard_normal(out[name].shape)
        drawn = base * np.exp(spread * noise) if base else spread * noise
        out[name] = __import__('jax').numpy.asarray(drawn.astype(out[name].dtype))
    for name, factor in factors.items():
        out[name] = (out[name] * factor).astype(out[name].dtype)
    return out
```

```python
from contextlib import ExitStack

import concourse.bass as bass
from concourse import mybir

F32 = mybir.dt.float32
F32R = mybir.dt.float32r
BF16 = mybir.dt.bfloat16
U32 = mybir.dt.uint32
ALU = mybir.AluOpType
ACT = mybir.ActivationFunctionType
AX_X = mybir.AxisListType.X

P = 128
T = 512
TT = T // P
D = 1024
DC = D // P
EPS = 1e-6
NEG = -1e30

A_HEADS, A_DH = 8, 64
Q0, K0, V0, Z0 = 0, 4, 8, 12
DQ0, DK0, DV0, DZ0 = 16, 20, 24, 28
PROJ = 32
G_HEADS = 4
G_CONV = 4
BA = 2 * G_HEADS
LEVELS = 7
SEC = 256

L_HEADS = 8
PEER_HEADS, NKEYS, TOPK = 8, 128, 16
GROUPS = 2 * PEER_HEADS

COLS, _at = {}, 0
for _name, _n in (("norm_pre", 8), ("norm1", 8), ("norm2", 8), ("conv", 48), ("conv_a", 32),
                  ("conv_a_b", 8), ("b_a", 8), ("b_x", 8), ("conv_b", 24), ("lam", 8)):
    COLS[_name] = (_at, _n)
    _at += _n
NCOLS = _at
COLS_A = COLS["conv_a"][0]


class Chain:

    def __init__(self, eng, sem, i=None, per=0, done=0):
        self.eng, self.sem, self.i, self.per, self.n, self.done = eng, sem, i, per, 0, done

    def value(self):
        return self.done + self.n if self.i is None else self.i * self.per + (self.done + self.n)

    def add(self, ins):
        self.n += 1
        ins.then_inc(self.sem, 1)

    def wait(self):
        self.eng.wait_ge(self.sem, self.value())

    def __call__(self, ins):
        self.add(ins)
        self.wait()

    def end(self):
        assert self.i is None or self.n == self.per, (self.n, self.per)


def after(count):
    return count + 1


class Kit:

    def __init__(self, nc, ctx):
        self.nc, self.ctx, self.used = nc, ctx, []

    def sb(self, name, shape, dt=F32, ctx=None):
        return (ctx or self.ctx).enter_context(self.nc.sbuf_tensor(name, shape, dt))

    def sem(self, name):
        self.used.append(self.nc.alloc_semaphore(name=name))
        return self.used[-1]

    def credit(self):
        engines = (self.nc.sync, self.nc.scalar, self.nc.vector, self.nc.tensor)
        for n, sem in enumerate(self.used):
            engines[n % len(engines)].sem_inc(sem, 1)
        self.nc.all_engine_barrier()

    def end_stage(self):
        self.nc.clear_and_free_semaphores(self.used)
        self.nc.all_engine_barrier()
        self.used = []

    def sems(self, name, n):
        return [self.sem(f"{name}{i}") for i in range(n)]


def refined_rsqrt(chain, dve, out, root, square_sum, tmp, scale):
    chain(dve.tensor_scalar(square_sum, square_sum, scale, EPS, ALU.mult, ALU.add))
    chain(dve.reciprocal(out, root))
    chain(dve.tensor_tensor(tmp, out, out, ALU.mult))
    chain(dve.tensor_tensor(tmp, tmp, square_sum, ALU.mult))
    chain(dve.tensor_scalar(tmp, tmp, -0.5, 1.5, ALU.mult, ALU.add))
    chain(dve.tensor_tensor(out, out, tmp, ALU.mult))


def load_constants(nc, k, io, w8):
    with ExitStack() as st:
        rows = [k.sb(f"rows{n}", [P, P], ctx=st) for n in range(2)]
        x_in, rows_in, w8_in = k.sem("x_in"), k.sem("rows_in"), k.sem("w8_in")
        ident_zero, ident_done = k.sem("ident_zero"), k.sem("ident_done")
        masks_done = k.sem("masks_done")
        turned, cols_done = k.sem("rows_turned"), k.sem("cols_done")
        na = COLS_A
        nb = NCOLS - na
        with nc.Block() as block:
            @block.sync
            def _(sp):
                sp.dma_start(w8[:, :, :], io["w_in"][0].rearrange("(c p) n -> p c n", p=P)[:, :, PROJ * P:PROJ * P + BA]
                             ).then_inc(w8_in, 16)
                sp.dma_start(k.xh[:, :, :], io["x"][0].rearrange("(t p) d -> p t d", p=P)).then_inc(x_in, 16)
                for name, src in (("norm_pre", io["norm_pre_w"]), ("norm1", io["norm1_g_2"]), ("norm2", io["norm2_g_2"]),
                                  ("conv", io["conv_w"].rearrange("a k c -> a (k c)")),
                                  ("conv_a", io["conv_a_w_2"].rearrange("a k c -> a (k c)")),
                                  ("conv_a_b", io["conv_a_b_2"]), ("b_a", io["b_a_2"]), ("b_x", io["b_x_2"]),
                                  ("conv_b", io["conv_b_w_2"].rearrange("a k c -> a (k c)")), ("lam", io["lru_lambda_2"])):
                    r0, n = COLS[name]
                    tile, r0 = (rows[0], r0) if r0 < na else (rows[1], r0 - na)
                    sp.dma_start(tile[r0:r0 + n, :], src.rearrange("a (c p) -> (a c) p", p=P)).then_inc(rows_in, 16)

            @block.gpsimd
            def _(pool):
                pool.memset(k.ident[:, :], 0.0).then_inc(ident_zero, 1)
                pool.wait_ge(ident_zero, 1)
                pool.affine_select(out=k.ident[:, :], in_=k.ident[:, :], compare_op=ALU.not_equal, fill=1.0,
                                   base=0, pattern=[[-1, P]], channel_multiplier=1).then_inc(ident_done, 1)
                order = Chain(pool, masks_done)
                order(pool.iota(k.row[:, :], [[1, NKEYS]], base=0, channel_multiplier=0,
                                allow_small_or_imprecise_dtypes=True))

            @block.vector
            def _(dve):
                dve.memset(k.eps[:, :], EPS)
                dve.memset(k.ones[:, :], 1.0)
                for n, scale in ((0, P ** -0.5), (1, 1.0)):
                    dve.memset(k.qk_scale[:, 2 * n:2 * n + 2], scale)
                dve.wait_ge(turned, 2)
                dve.tensor_copy(k.cols[:, 0:na], k.ps[0][:, 0:na]).then_inc(cols_done, 1)
                dve.tensor_copy(k.cols[:, na:NCOLS], k.ps[1][:, 0:nb]).then_inc(cols_done, 1)

            @block.tensor
            def _(pe):
                pe.wait_ge(ident_done, 1)
                pe.wait_ge(rows_in, 160)
                pe.transpose(k.ps[0][:, 0:na], rows[0][0:na, :], k.ident[0:na, 0:na]).then_inc(turned, 1)
                pe.transpose(k.ps[1][:, 0:nb], rows[1][0:nb, :], k.ident[0:nb, 0:nb]).then_inc(turned, 1)

            @block.scalar
            def _(act):
                act.wait_ge(x_in, 16)
                act.wait_ge(w8_in, 16)


def norm_and_turn(nc, k, tag, out, weight):
    w0 = COLS[weight][0]
    hi, lo = out
    with ExitStack() as st:
        xs = k.sb(f"{tag}_xs", [P, TT, D], ctx=st)
        stat = k.sb(f"{tag}_stat", [P, 4 * TT], ctx=st)
        vec = k.sem(f"{tag}_vec")
        sq, root, scaled = k.sem(f"{tag}_sq"), k.sem(f"{tag}_root"), k.sem(f"{tag}_scaled")
        turned, his = k.sem(f"{tag}_turned"), k.sem(f"{tag}_hi")
        with nc.Block() as block:
            @block.scalar
            def _(act):
                for t in range(TT):
                    act.activation(xs[:, t, :], k.xh[:, t, :], ACT.Square, accum_out=stat[:, t:t + 1]).then_inc(sq, 1)
                act.wait_ge(sq, TT)
                act.activation(stat[:, TT:2 * TT], stat[:, 0:TT], ACT.Sqrt, scale=1.0 / D,
                               bias=k.eps[:, 0:1]).then_inc(root, 1)
                for c in range(DC):
                    act.wait_ge(turned, c + 1)
                    act.activation(hi[:, c, :], k.ps[c][:, :], ACT.Copy,
                                   scale=k.cols[:, w0 + c:w0 + c + 1]).then_inc(his, 1)

            @block.vector
            def _(dve):
                dve.wait_ge(root, 1)
                refined_rsqrt(Chain(dve, vec), dve, stat[:, 2 * TT:3 * TT], stat[:, TT:2 * TT], stat[:, 0:TT],
                              stat[:, 3 * TT:4 * TT], 1.0 / D)
                for t in range(TT):
                    dve.tensor_scalar(xs[:, t, :], k.xh[:, t, :], stat[:, 2 * TT + t:2 * TT + t + 1], None,
                                      ALU.mult).then_inc(scaled, 1)
                for c in range(DC):
                    dve.wait_ge(his, c + 1)
                    dve.scalar_tensor_tensor(out=lo[:, c, :], in0=k.ps[c][:, :], scalar=k.cols[:, w0 + c:w0 + c + 1],
                                             in1=hi[:, c, :].bitcast(F32), op0=ALU.mult, op1=ALU.subtract)

            @block.tensor
            def _(pe):
                pe.wait_ge(scaled, TT)
                for c in range(DC):
                    for t in range(TT):
                        mm = pe.transpose(k.ps[c][:, t * P:(t + 1) * P], xs[:, t, c * P:(c + 1) * P], k.ident[:, :])
                    mm.then_inc(turned, 1)


def project_first(nc, k, io, src, w8, proj, gates):
    hi, lo = src
    beta, g = gates
    w_dram = io["w_in"][0].rearrange("(c p) n -> p c n", p=P)
    w0, n_ch = COLS["conv"][0], 3 * G_HEADS
    per, sections = SEC // P, 2
    step = per * sections
    steps = PROJ // step
    pairs, unit_pairs = n_ch // 2, G_HEADS
    with ExitStack() as st:
        raw = [k.sb(f"p_raw{b}", [P, DC, SEC], ctx=st) for b in range(sections)]
        whi = [k.sb(f"p_whi{b}", [P, DC, SEC], F32R, ctx=st) for b in range(sections)]
        wlo = [k.sb(f"p_wlo{b}", [P, DC, SEC], F32R, ctx=st) for b in range(sections)]
        w8h, w8l = (k.sb(f"p_w8{n}", [P, DC, BA], F32R, ctx=st) for n in "hl")
        ba = k.sb("p_ba", [P, TT, BA], ctx=st)
        bias = k.sb("p_bias", [P, 2, G_HEADS], ctx=st)
        z = k.sb("p_z", [P, 3, TT, G_HEADS], ctx=st)
        acc, sq, root = ([k.sb(f"p_{n}{b}", [P, T], ctx=st) for b in range(2)] for n in ("acc", "sq", "root"))
        raw_in, w_hi, w_lo = (k.sems(f"p_{n}", sections) for n in ("raw_in", "w_hi", "w_lo"))
        product, kept = k.sems("p_product", step), k.sems("p_kept", step)
        acc_done, silu_done, squared, summed, rooted, unit = (
            k.sems(f"p_{n}", 2) for n in ("acc_done", "silu_done", "squared", "summed", "rooted", "unit"))
        vec, w8_split, w8_product, ba_kept, bias_in, z_made, z_act, decay_rate, gates_done, masks = (
            k.sem(f"p_{n}") for n in ("vec", "w8_split", "w8_product", "ba_kept", "bias_in", "z_made", "z_act",
                                      "decay_rate", "gates_done", "masks"))
        chunk = lambda i: (i * step + DQ0) % PROJ

        def steps_of(eng, body):
            body(0, False, False, False)
            body(1, True, True, False)
            with eng.Fori(2, 2 + unit_pairs) as i:
                body(i, True, True, True)
            for i in range(2 + unit_pairs, steps):
                body(i, i <= pairs, False, False)

        k.credit()
        with nc.Block() as block:
            @block.sync
            def _(sp):
                def load(i, b):
                    sp.dma_start(raw[b][:, :, :], w_dram[:, :, bass.ds(chunk(i) * P + b * SEC, SEC)]).then_inc(raw_in[b], 16)
                for b in range(sections):
                    load(0, b)
                for n, name in enumerate(("a_log", "dt_bias")):
                    sp.dma_start(bias[:, n, :], io[name][0].partition_broadcast(P)).then_inc(bias_in, 16)
                with sp.Fori(1, steps) as i:
                    for b in range(sections):
                        sp.wait_ge(w_lo[b], after(i))
                        load(i, b)

            @block.gpsimd
            def _(pool):
                order = Chain(pool, masks, done=1)
                order(pool.memset(k.upto[:, :], 1.0))
                order(pool.affine_select(out=k.upto[:, :], in_=k.upto[:, :], compare_op=ALU.is_ge, fill=0.0,
                                         base=0, pattern=[[1, P]], channel_multiplier=-1))
                order(pool.memset(k.later[:, :], 0.0))
                order(pool.affine_select(out=k.later[:, :], in_=k.later[:, :], compare_op=ALU.is_ge, fill=NEG,
                                         base=0, pattern=[[1, P]], channel_multiplier=-1))
                order(pool.memset(k.level[:, :, :], 1.0))
                for lv in range(LEVELS):
                    half = 1 << lv
                    m = k.level[:, lv, :].rearrange("p (n s) -> p n s", s=2 * half)
                    n = P // (2 * half)
                    for base, steps, cm in ((0, [-2 * half, 0], 1), (half - 1, [2 * half, 0], -1), (-half, [0, 1], 0)):
                        order(pool.affine_select(out=m, in_=m, compare_op=ALU.is_ge, fill=0.0, base=base,
                                                 pattern=[[steps[0], n], [steps[1], 2 * half]], channel_multiplier=cm))

            @block.tensor
            def _(pe):
                pe.wait_ge(w8_split, after(2))
                for t in range(TT):
                    for c in range(DC):
                        for x, w in ((hi, w8h), (hi, w8l), (lo, w8h)):
                            mm = pe.matmul(k.ps[4 + t][:, 0:BA], x[:, c, t * P:(t + 1) * P], w[:, c, :],
                                           start=(c == 0 and x is hi and w is w8h), stop=(c == DC - 1 and x is lo))
                    mm.then_inc(w8_product, 1)

                def body(i, convolved, square, scaled):
                    for n in range(step):
                        b, j = n // per, n % per
                        if j == 0:
                            pe.wait_ge(w_lo[b], after(i + 1))
                        pe.wait_ge(kept[n], after(i))
                        for c in range(DC):
                            for w, x in ((whi, hi), (whi, lo), (wlo, hi)):
                                mm = pe.matmul(k.ps[n][:, :], w[b][:, c, j * P:(j + 1) * P], x[:, c, :],
                                               start=(c == 0 and w is whi and x is hi), stop=(c == DC - 1 and w is wlo))
                        mm.then_inc(product[n], 1)
                        if n == 0 and scaled:
                            for h in range(2):
                                pe.wait_ge(ba_kept, after(TT))
                                pe.wait_ge(squared[h], after(i - 1))
                                pe.wait_ge(rooted[h], after(i - 2))
                                pe.matmul(k.ps[4 + h][:, :], k.ones[:, :], sq[h][:, :], start=True, stop=True).then_inc(summed[h], 1)
                steps_of(pe, body)

            @block.scalar
            def _(act):
                def high(i, b):
                    act.wait_ge(raw_in[b], after(i * 16 + 16))
                    act.activation(whi[b][:, :, :], raw[b][:, :, :], ACT.Copy).then_inc(w_hi[b], 1)
                for b in range(sections):
                    high(0, b)
                for t in range(TT):
                    act.wait_ge(w8_product, after(t + 1))
                    act.activation(ba[:, t, :], k.ps[4 + t][:, 0:BA], ACT.Copy).then_inc(ba_kept, 1)
                act.wait_ge(ba_kept, after(TT))
                act.activation(beta[:, :, :], ba[:, :, 0:G_HEADS], ACT.Sigmoid)
                act.wait_ge(z_made, after(TT))
                act.activation(z[:, 1, :, :], z[:, 0, :, :], ACT.Abs).then_inc(z_act, 1)
                act.wait_ge(z_act, after(1))
                act.activation(z[:, 1, :, :], z[:, 1, :, :], ACT.Exp, scale=-1.0).then_inc(z_act, 1)
                act.wait_ge(z_act, after(2))
                act.activation(z[:, 2, :, :], z[:, 1, :, :], ACT.Ln, bias=1.0).then_inc(z_act, 1)
                act.wait_ge(bias_in, after(32))
                act.activation(bias[:, 0, :], bias[:, 0, :], ACT.Exp).then_inc(decay_rate, 1)

                def body(i, convolved, square, scaled):
                    for n in range(step):
                        act.wait_ge(product[n], after(i + 1))
                        act.activation(proj[:, chunk(i) + n, :], k.ps[n][:, :], ACT.Copy).then_inc(kept[n], 1)
                        if n % per == per - 1 and not (isinstance(i, int) and i == steps - 1):
                            high(i + 1, n // per)
                        if n == 1 and scaled:
                            for h in range(2):
                                act.wait_ge(summed[h], after(i - 1))
                                act.wait_ge(unit[h], after(i * 2 - 4))
                                act.activation(root[h][:, :], k.ps[4 + h][:, :], ACT.Sqrt, bias=k.eps[:, 0:1]).then_inc(rooted[h], 1)
                    if convolved:
                        for h in range(2):
                            act.wait_ge(acc_done[h], after(i))
                            act.activation(proj[:, i * 2 + (DQ0 + h - 2), :], acc[h][:, :], ACT.Silu).then_inc(silu_done[h], 1)
                    if square:
                        for h in range(2):
                            act.wait_ge(silu_done[h], after(i))
                            act.wait_ge(summed[h], after(i - 1))
                            act.activation(sq[h][:, :], proj[:, (i - 1) * 2 + (DQ0 + h), :], ACT.Square).then_inc(squared[h], 1)
                steps_of(act, body)

            @block.vector
            def _(dve):
                dve.tensor_copy(w8h[:, :, :], w8[:, :, :]).then_inc(w8_split, 1)
                dve.wait_ge(w8_split, after(1))
                dve.tensor_tensor(w8l[:, :, :], w8[:, :, :], w8h[:, :, :].bitcast(F32), ALU.subtract).then_inc(w8_split, 1)

                def low(i, b):
                    dve.wait_ge(w_hi[b], after(i + 1))
                    dve.tensor_tensor(wlo[b][:, :, :], raw[b][:, :, :], whi[b][:, :, :].bitcast(F32),
                                      ALU.subtract).then_inc(w_lo[b], 1)

                def body(i, convolved, square, scaled):
                    low(i, 1)
                    if convolved:
                        chain = Chain(dve, vec, i - 1, 2 * (G_CONV - 1), done=1)
                        for n in range(step):
                            dve.wait_ge(kept[n], after(i))
                        for h in range(2):
                            dve.wait_ge(silu_done[h], after(i - 1))
                            x = lambda upto: proj[:, i * 2 + (DQ0 + h - 2), 0:upto]
                            tap = lambda j: k.cols[:, bass.ds(i * 2 + (w0 + j * n_ch + h - 2), 1)]
                            chain(dve.tensor_scalar(acc[h][:, :], x(T), tap(G_CONV - 1), None, ALU.mult))
                            for j in range(G_CONV - 2, -1, -1):
                                s = G_CONV - 1 - j
                                ins = dve.scalar_tensor_tensor(out=acc[h][:, s:T], in0=x(T - s), scalar=tap(j), in1=acc[h][:, s:T],
                                                               op0=ALU.mult, op1=ALU.add)
                                if j:
                                    chain(ins)
                                else:
                                    ins.then_inc(acc_done[h], 1)
                        chain.end()
                    if not (isinstance(i, int) and i == steps - 1):
                        low(i + 1, 0)
                    if scaled:
                        for h in range(2):
                            dve.wait_ge(rooted[h], after(i - 1))
                            y = proj[:, i * 2 + (DQ0 + h - 4), :]
                            dve.reciprocal(root[h][:, :], root[h][:, :]).then_inc(unit[h], 1)
                            dve.wait_ge(unit[h], after(i * 2 - 3))
                            dve.scalar_tensor_tensor(out=y, in0=y, scalar=k.qk_scale[:, bass.ds(i - 2, 1)], in1=root[h][:, :],
                                                     op0=ALU.mult, op1=ALU.mult).then_inc(unit[h], 1)

                low(0, 0)
                low(0, 1)
                for t in range(TT):
                    dve.wait_ge(ba_kept, after(t + 1))
                    if t == 0:
                        dve.wait_ge(bias_in, after(32))
                    dve.tensor_tensor(z[:, 0, t, :], ba[:, t, G_HEADS:BA], bias[:, 1, :], ALU.add).then_inc(z_made, 1)
                order = Chain(dve, gates_done, done=1)
                dve.wait_ge(decay_rate, after(1))
                dve.wait_ge(z_act, after(3))
                order(dve.tensor_scalar(z[:, 0, :, :], z[:, 0, :, :], 0.0, None, ALU.max))
                order(dve.tensor_tensor(z[:, 0, :, :], z[:, 0, :, :], z[:, 2, :, :], ALU.add))
                for t in range(TT):
                    order(dve.scalar_tensor_tensor(out=g[:, t, :], in0=z[:, 0, t, :], scalar=-1.0, in1=bias[:, 0, :],
                                                   op0=ALU.mult, op1=ALU.mult))
                low(1, 0)
                body(1, True, True, False)
                with dve.Fori(2, 2 + unit_pairs) as i:
                    body(i, True, True, True)
                for i in range(2 + unit_pairs, steps):
                    body(i, i <= pairs, False, False)


def attention(nc, k, proj, mixed):
    with ExitStack() as st:
        vtok = k.sb("a_vtok", [P, TT, A_HEADS * A_DH], ctx=st)
        dist = k.sb("a_dist", [P, T], ctx=st)
        slopes = k.sb("a_slopes", [P, A_HEADS], ctx=st)
        qs = k.sb("a_q", [P, T], ctx=st)
        ks = k.sb("a_k", [P, T], ctx=st)
        logits = k.sb("a_logits", [P, 2, T], ctx=st)
        probs = k.sb("a_probs", [P, 2, T], ctx=st)
        probs_t = k.sb("a_probs_t", [P, 2, T], ctx=st)
        stat = k.sb("a_stat", [P, 4, 8], ctx=st)
        steps = [(b, qt) for b in range(2) for qt in range(TT)]
        n_steps = len(steps)
        dist_made, v_turned, v_kept, slopes_made = (k.sem(f"a_{n}") for n in ("dist_made", "v_turned", "v_kept", "slopes_made"))
        pair_ready, scored, logits_made, max_neg, exped, turned, kept_t, weighted, normed, vec = (
            k.sem(f"a_{n}") for n in ("pair_ready", "scored", "logits_made", "max_neg", "exped", "turned", "kept_t",
                                      "weighted", "normed", "vec"))
        k.credit()
        with nc.Block() as block:
            @block.gpsimd
            def _(pool):
                pool.iota(dist[:, :], [[1, T]], base=-(T - P), channel_multiplier=-1,
                          allow_small_or_imprecise_dtypes=True).then_inc(dist_made, 1)
                pool.wait_ge(dist_made, after(1))
                pool.affine_select(out=dist[:, :], in_=dist[:, :], compare_op=ALU.is_ge, fill=NEG, base=T - P,
                                   pattern=[[-1, T]], channel_multiplier=1).then_inc(dist_made, 1)

            @block.tensor
            def _(pe):
                for t in range(TT):
                    for j in range(4):
                        mm = pe.transpose(k.ps[t][:, j * P:(j + 1) * P], proj[:, V0 + j, t * P:(t + 1) * P], k.ident[:, :])
                    mm.then_inc(v_turned, 1)
                pe.wait_ge(v_kept, after(TT))

                def score(i, n):
                    b, qt = steps[n]
                    if n >= 2:
                        pe.wait_ge(logits_made, after(i * n_steps + n - 1))
                    else:
                        pe.wait_ge(logits_made, after(i * n_steps))
                    if n == 0:
                        pe.wait_ge(pair_ready, after(i * 2 + 2))
                    h = slice(b * A_DH, (b + 1) * A_DH)
                    w = (qt + 1) * P
                    pe.matmul(k.ps[n % 2][:, 0:w], qs[h, qt * P:w], ks[h, 0:w], start=True, stop=True).then_inc(scored, 1)

                def weigh(i, n):
                    b, qt = steps[n]
                    pe.wait_ge(exped, after(i * n_steps + n + 1))
                    if n >= 2:
                        pe.wait_ge(kept_t, after(i * n_steps + n - 1))
                    for kt in range(qt + 1):
                        mm = pe.transpose(k.ps[2 + n % 2][:, kt * P:(kt + 1) * P], probs[:, n % 2, kt * P:(kt + 1) * P], k.ident[:, :])
                    mm.then_inc(turned, 1)
                    pe.wait_ge(kept_t, after(i * n_steps + n + 1))
                    if n >= 2:
                        pe.wait_ge(normed, after(i * n_steps + n - 1))
                    else:
                        pe.wait_ge(normed, after(i * n_steps))
                    for kt in range(qt + 1):
                        mm = pe.matmul(k.ps[4 + n % 2][:, 0:A_DH], probs_t[:, n % 2, kt * P:(kt + 1) * P],
                                       vtok[:, kt, bass.ds(i * P + b * A_DH, A_DH)], start=(kt == 0), stop=(kt == qt))
                    mm.then_inc(weighted, 1)

                with pe.Fori(0, A_HEADS // 2) as i:
                    score(i, 0)
                    for n in range(n_steps):
                        if n + 1 < n_steps:
                            score(i, n + 1)
                        weigh(i, n)

            @block.vector
            def _(dve):
                for h in range(A_HEADS):
                    ins = dve.memset(slopes[:, h:h + 1], 2.0 ** -(h + 1))
                ins.then_inc(slopes_made, 1)
                dve.wait_ge(slopes_made, after(1))
                dve.wait_ge(dist_made, after(2))
                for t in range(TT):
                    dve.wait_ge(v_turned, after(t + 1))
                    dve.tensor_copy(vtok[:, t, :], k.ps[t][:, :]).then_inc(v_kept, 1)

                def normalise(i, n):
                    b, qt = steps[n]
                    dve.wait_ge(exped, after(i * n_steps + n + 1))
                    dve.wait_ge(weighted, after(i * n_steps + n + 1))
                    chain(dve.reciprocal(stat[:, 3, n:n + 1], stat[:, 2, n:n + 1]))
                    dve.tensor_scalar(mixed[:, qt, bass.ds(i * P + b * A_DH, A_DH)], k.ps[4 + n % 2][:, 0:A_DH],
                                      stat[:, 3, n:n + 1], None, ALU.mult).then_inc(normed, 1)

                with dve.Fori(0, A_HEADS // 2) as i:
                    chain = Chain(dve, vec, i, 2 * n_steps, done=1)
                    dve.wait_ge(scored, after(i * n_steps))
                    dve.tensor_scalar(qs[:, :], proj[:, i + Q0, :], A_DH ** -0.5, None, ALU.mult).then_inc(pair_ready, 1)
                    dve.tensor_copy(ks[:, :], proj[:, i + K0, :]).then_inc(pair_ready, 1)
                    for n, (b, qt) in enumerate(steps):
                        w = (qt + 1) * P
                        dve.wait_ge(scored, after(i * n_steps + n + 1))
                        if n >= 2:
                            dve.wait_ge(exped, after(i * n_steps + n - 1))
                        dve.scalar_tensor_tensor(out=logits[:, n % 2, 0:w], in0=dist[:, T - w:T],
                                                 scalar=slopes[:, bass.ds(i * 2 + b, 1)], in1=k.ps[n % 2][:, 0:w],
                                                 op0=ALU.mult, op1=ALU.add).then_inc(logits_made, 1)
                        dve.wait_ge(logits_made, after(i * n_steps + n + 1))
                        chain(dve.tensor_reduce(stat[:, 0, n:n + 1], logits[:, n % 2, 0:w], AX_X, ALU.max))
                        dve.tensor_scalar(stat[:, 1, n:n + 1], stat[:, 0, n:n + 1], -1.0, None, ALU.mult).then_inc(max_neg, 1)
                        if n >= 1:
                            normalise(i, n - 1)
                    normalise(i, n_steps - 1)
                    chain.end()

            @block.scalar
            def _(act):
                with act.Fori(0, A_HEADS // 2) as i:
                    for n, (b, qt) in enumerate(steps):
                        w = (qt + 1) * P
                        act.wait_ge(max_neg, after(i * n_steps + n + 1))
                        if n >= 2:
                            act.wait_ge(turned, after(i * n_steps + n - 1))
                        act.activation(probs[:, n % 2, 0:w], logits[:, n % 2, 0:w], ACT.Exp, bias=stat[:, 1, n:n + 1],
                                       accum_out=stat[:, 2, n:n + 1]).then_inc(exped, 1)
                        act.wait_ge(turned, after(i * n_steps + n + 1))
                        if n >= 2:
                            act.wait_ge(weighted, after(i * n_steps + n - 1))
                        act.activation(probs_t[:, n % 2, 0:w], k.ps[2 + n % 2][:, 0:w], ACT.Copy).then_inc(kept_t, 1)


def delta_prepare(nc, k, qkv, gates, kept):
    beta, g = gates
    H = G_HEADS
    heads = lambda ap: ap.rearrange("p (h n) -> p h n", h=H)
    with ExitStack() as st:
        two = lambda name: [k.sb(f"d_{name}{a}", [P, H, P], ctx=st) for a in range(2)]
        qst, kst, vst, dec, at, m, mt, x, tmp = (two(n) for n in ("q", "k", "v", "dec", "at", "m", "mt", "x", "tmp"))
        ot = [k.sb(f"d_ot{a}", [P, LEVELS, H, P], ctx=st) for a in range(2)]
        small = [k.sb(f"d_small{a}", [P, 4, H], ctx=st) for a in range(2)]
        gb = two("gb")
        names = ("staged", "gc_ready", "gc_kept", "diff", "decay", "rates", "kk_ready", "qk_ready", "at_done", "intra_done",
                 "k_turned", "k_kept", "v_turned", "v_kept", "ot_done", "mt_done", "m_turned", "m_done", "x_ready",
                 "x_kept", "dm_ready", "rate_diff")
        s = {n: k.sems(f"d_{n}", 2) for n in names}
        last = LEVELS - 1
        k.credit()
        with nc.Block() as block:
            @block.vector
            def _(dve):
                with dve.Fori(0, TT // 2) as i:
                    for a in range(2):
                        c = i * 2 + a
                        dve.wait_ge(s["v_turned"][a], after(i))
                        for n, dst in enumerate((qst, kst, vst)):
                            dve.tensor_copy(dst[a][:, :, :], qkv[:, n * H:(n + 1) * H, bass.ds(i * (2 * P) + a * P, P)]
                                            ).then_inc(s["staged"][a], 1)
                        for h in range(H):
                            dve.tensor_scalar(gb[a][:, h, :], k.ones[:, :], g[:, c, h:h + 1], None, ALU.mult
                                              ).then_inc(s["staged"][a], 1)
                    for a in range(2):
                        c = i * 2 + a
                        b0, b3 = heads(k.ps[4 * a][:, :]), k.ps[4 * a + 3]
                        dve.wait_ge(s["gc_ready"][a], after(i + 1))
                        dve.wait_ge(s["decay"][a], after(i))
                        dve.tensor_copy(small[a][:, 0, :], b3[:, 0:H]).then_inc(s["gc_kept"][a], 1)
                        dve.tensor_copy(small[a][:, 1, :], b0[:, :, P - 1]).then_inc(s["gc_kept"][a], 1)
                        dve.wait_ge(s["gc_kept"][a], after(i * 2 + 2))
                        dve.tensor_tensor(small[a][:, 2, :], small[a][:, 1, :], small[a][:, 0, :],
                                          ALU.subtract).then_inc(s["rate_diff"][a], 1)
                        for h in range(H):
                            dve.scalar_tensor_tensor(out=tmp[a][:, h, :], in0=b0[:, h, :], scalar=small[a][:, 0, h:h + 1],
                                                     in1=k.later[:, :], op0=ALU.subtract, op1=ALU.add).then_inc(s["diff"][a], 1)
                    for a in range(2):
                        c = i * 2 + a
                        b1, b2 = heads(k.ps[4 * a + 1][:, :]), heads(k.ps[4 * a + 2][:, :])
                        dve.wait_ge(s["kk_ready"][a], after(i + 1))
                        dve.wait_ge(s["decay"][a], after(i + 1))
                        dve.wait_ge(s["ot_done"][a], after(i * LEVELS))
                        for h in range(H):
                            dve.scalar_tensor_tensor(out=at[a][:, h, :], in0=b1[:, h, :], scalar=beta[:, c, h:h + 1],
                                                     in1=dec[a][:, h, :], op0=ALU.mult, op1=ALU.mult).then_inc(s["at_done"][a], 1)
                        dve.wait_ge(s["qk_ready"][a], after(i + 1))
                        dve.tensor_tensor(kept["intra"][:, c, :, :], b2, dec[a][:, :, :], ALU.mult).then_inc(s["intra_done"][a], 1)
                    for a in range(2):
                        dve.wait_ge(s["ot_done"][a], after(i * LEVELS + 1))
                        dve.wait_ge(s["dm_ready"][a], after(i * last))
                        for h in range(H):
                            dve.tensor_tensor(mt[a][:, h, :], k.ident[:, :], ot[a][:, 0, h, :], ALU.subtract
                                              ).then_inc(s["mt_done"][a], 1)
                    for lv in range(1, LEVELS):
                        for a in range(2):
                            c = i * 2 + a
                            b1, b2 = heads(k.ps[4 * a + 1][:, :]), heads(k.ps[4 * a + 2][:, :])
                            dve.wait_ge(s["dm_ready"][a], after(i * last + lv))
                            if lv < last:
                                dve.tensor_tensor(mt[a][:, :, :], mt[a][:, :, :], b2, ALU.subtract).then_inc(s["mt_done"][a], 1)
                                dve.wait_ge(s["m_done"][a], after(i * last + lv))
                                dve.tensor_tensor(m[a][:, :, :], m[a][:, :, :], b1, ALU.subtract).then_inc(s["m_done"][a], 1)
                            else:
                                dve.tensor_tensor(kept["inv"][:, c, :, :], mt[a][:, :, :], b2, ALU.subtract)

            MT = H + last - 1

            @block.gpsimd
            def _(pool):
                with pool.Fori(0, TT // 2) as i:
                    for lv in range(LEVELS):
                        for a in range(2):
                            if lv == 0:
                                pool.wait_ge(s["at_done"][a], after(i * H + H))
                                pool.wait_ge(s["dm_ready"][a], after(i * last))
                            for h in range(H):
                                ins = pool.tensor_tensor(ot[a][:, lv, h, :], at[a][:, h, :], k.level[:, lv, :], ALU.mult)
                            ins.then_inc(s["ot_done"][a], 1)

            @block.scalar
            def _(act):
                with act.Fori(0, TT // 2) as i:
                    for a in range(2):
                        c = i * 2 + a
                        act.wait_ge(s["diff"][a], after(i * H + H))
                        act.wait_ge(s["intra_done"][a], after(i))
                        act.activation(dec[a][:, :, :], tmp[a][:, :, :], ACT.Exp).then_inc(s["decay"][a], 1)
                        act.wait_ge(s["rate_diff"][a], after(i + 1))
                        act.activation(kept["rates"][:, c, 0, :], small[a][:, 0, :], ACT.Exp)
                        act.activation(kept["rates"][:, c, 1, :], small[a][:, 1, :], ACT.Exp)
                        act.activation(small[a][:, 3, :], small[a][:, 2, :], ACT.Exp).then_inc(s["rates"][a], 1)
                    for a in range(2):
                        c = i * 2 + a
                        b3 = heads(k.ps[4 * a + 3][:, :])
                        act.wait_ge(s["k_turned"][a], after(i + 1))
                        act.wait_ge(s["rates"][a], after(i + 1))
                        for h in range(H):
                            act.activation(kept["kdec"][:, c, h, :], b3[:, h, :], ACT.Copy,
                                           scale=small[a][:, 3, h:h + 1]).then_inc(s["k_kept"][a], 1)
                        act.wait_ge(s["v_turned"][a], after(i + 1))
                        act.activation(kept["v"][:, c, :, :], b3, ACT.Copy).then_inc(s["v_kept"][a], 1)
                    for a in range(2):
                        act.wait_ge(s["m_turned"][a], after(i + 1))
                        act.activation(m[a][:, :, :], heads(k.ps[4 * a][:, :]), ACT.Copy).then_inc(s["m_done"][a], 1)
                    for lv in range(1, LEVELS):
                        for a in range(2):
                            act.wait_ge(s["x_ready"][a], after(i * last + lv))
                            act.activation(x[a][:, :, :], heads(k.ps[4 * a][:, :]), ACT.Copy).then_inc(s["x_kept"][a], 1)

            @block.tensor
            def _(pe):
                with pe.Fori(0, TT // 2) as i:
                    for a in range(2):
                        c = i * 2 + a
                        b0, b3 = heads(k.ps[4 * a][:, :]), k.ps[4 * a + 3]
                        pe.wait_ge(s["v_kept"][a], after(i))
                        pe.wait_ge(s["x_kept"][a], after(i * last))
                        pe.matmul(b3[:, 0:H], k.upto[:, :], g[:, c, :], start=True, stop=True)
                        for h in range(H):
                            pe.wait_ge(s["staged"][a], after(i * (3 + H) + (3 + H)))
                            mm = pe.matmul(b0[:, h, :], gb[a][:, h, :], k.upto[:, :], start=True, stop=True)
                        mm.then_inc(s["gc_ready"][a], 1)
                    for a in range(2):
                        b1, b2, b3 = (heads(k.ps[4 * a + n][:, :]) for n in (1, 2, 3))
                        if True:
                            pe.wait_ge(s["m_done"][a], after(i * last))
                        for h in range(H):
                            mm = pe.matmul(b1[:, h, :], kst[a][:, h, :], kst[a][:, h, :], start=True, stop=True)
                        mm.then_inc(s["kk_ready"][a], 1)
                        for h in range(H):
                            mm = pe.matmul(b2[:, h, :], kst[a][:, h, :], qst[a][:, h, :], start=True, stop=True)
                        mm.then_inc(s["qk_ready"][a], 1)
                        pe.wait_ge(s["gc_kept"][a], after(i * 2 + 2))
                        for h in range(H):
                            mm = pe.transpose(b3[:, h, :], kst[a][:, h, :], k.ident[:, :])
                        mm.then_inc(s["k_turned"][a], 1)
                        pe.wait_ge(s["k_kept"][a], after(i * H + H))
                        for h in range(H):
                            mm = pe.transpose(b3[:, h, :], vst[a][:, h, :], k.ident[:, :])
                        mm.then_inc(s["v_turned"][a], 1)
                    for a in range(2):
                        b0 = heads(k.ps[4 * a][:, :])
                        pe.wait_ge(s["mt_done"][a], after(i * MT + H))
                        pe.wait_ge(s["diff"][a], after(i * H + H))
                        for h in range(H):
                            mm = pe.transpose(b0[:, h, :], mt[a][:, h, :], k.ident[:, :])
                        mm.then_inc(s["m_turned"][a], 1)
                    for lv in range(1, LEVELS):
                        for a in range(2):
                            b0 = heads(k.ps[4 * a][:, :])
                            pe.wait_ge(s["m_done"][a], after(i * last + lv))
                            pe.wait_ge(s["ot_done"][a], after(i * LEVELS + lv + 1))
                            for h in range(H):
                                mm = pe.matmul(b0[:, h, :], ot[a][:, lv, h, :], m[a][:, h, :], start=True, stop=True)
                            mm.then_inc(s["x_ready"][a], 1)
                        for a in range(2):
                            b1, b2 = (heads(k.ps[4 * a + n][:, :]) for n in (1, 2))
                            pe.wait_ge(s["x_kept"][a], after(i * last + lv))
                            pe.wait_ge(s["mt_done"][a], after(i * MT + (H + lv - 1)))
                            if lv == 1:
                                pe.wait_ge(s["at_done"][a], after(i * H + H))
                                pe.wait_ge(s["intra_done"][a], after(i + 1))
                            for h in range(H):
                                if lv < last:
                                    pe.matmul(b1[:, h, :], mt[a][:, h, :], x[a][:, h, :], start=True, stop=True)
                                mm = pe.matmul(b2[:, h, :], x[a][:, h, :], mt[a][:, h, :], start=True, stop=True)
                            mm.then_inc(s["dm_ready"][a], 1)


def delta_scan(nc, k, gates, kept, qkv, o):
    beta, _ = gates
    H = G_HEADS
    heads = lambda ap: ap.rearrange("p (h n) -> p h n", h=H)
    with ExitStack() as st:
        S = k.sb("s_S", [P, H, P], ctx=st)
        z, vn = (k.sb(f"s_{n}", [P, H, P], ctx=st) for n in ("z", "vn"))
        neg = k.sb("s_neg", [P, TT, H], ctx=st)
        ks, qs, tz, intra, upd, z_done, vn_done, o_kept, o_done, s_done, neg_done = (
            k.sem(f"s_{n}") for n in ("ks", "qs", "tz", "intra", "upd", "z_done", "vn_done", "o_kept", "o_done", "s_done", "neg_done"))
        b = [heads(k.ps[n][:, :]) for n in range(5)]
        with nc.Block() as block:
            @block.tensor
            def _(pe):
                for c in range(TT):
                    tok = slice(c * P, (c + 1) * P)
                    if c:
                        pe.wait_ge(s_done, 1 + c * H)
                        for h in range(H):
                            mm = pe.matmul(b[0][:, h, :], qkv[:, H + h, tok], S[:, h, :], start=True, stop=True)
                        mm.then_inc(ks, 1)
                        pe.wait_ge(o_done, c * H - H)
                        for h in range(H):
                            mm = pe.matmul(b[1][:, h, :], qkv[:, h, tok], S[:, h, :], start=True, stop=True)
                        mm.then_inc(qs, 1)
                        pe.wait_ge(z_done, c * H)
                    for h in range(H):
                        src = z[:, h, :] if c else kept["v"][:, 0, h, :]
                        mm = pe.matmul(b[2][:, h, :], kept["inv"][:, c, h, :], src, start=True, stop=True)
                    mm.then_inc(tz, 1)
                    pe.wait_ge(vn_done, (c + 1) * H)
                    if c < TT - 1:
                        for h in range(H):
                            mm = pe.matmul(b[4][:, h, :], kept["kdec"][:, c, h, :], vn[:, h, :], start=True, stop=True)
                        mm.then_inc(upd, 1)
                    if c:
                        pe.wait_ge(o_kept, c)
                    for h in range(H):
                        mm = pe.matmul(b[3][:, h, :], kept["intra"][:, c, h, :], vn[:, h, :], start=True, stop=True)
                    mm.then_inc(intra, 1)

            @block.vector
            def _(dve):
                dve.memset(S[:, :, :], 0.0).then_inc(s_done, 1)
                dve.tensor_scalar(neg[:, :, :], kept["rates"][:, :, 0, :], -1.0, None, ALU.mult).then_inc(neg_done, 1)
                dve.wait_ge(neg_done, 1)
                dve.wait_ge(s_done, 1)
                for c in range(TT):
                    if c:
                        dve.wait_ge(ks, c)
                        dve.wait_ge(tz, c)
                        for h in range(H):
                            dve.scalar_tensor_tensor(out=z[:, h, :], in0=b[0][:, h, :], scalar=neg[:, c, h:h + 1],
                                                     in1=kept["v"][:, c, h, :], op0=ALU.mult, op1=ALU.add).then_inc(z_done, 1)
                    dve.wait_ge(tz, c + 1)
                    if c:
                        dve.wait_ge(intra, c)
                    for h in range(H):
                        dve.tensor_scalar(vn[:, h, :], b[2][:, h, :], beta[:, c, h:h + 1], None, ALU.mult).then_inc(vn_done, 1)
                    if c < TT - 1:
                        dve.wait_ge(upd, c + 1)
                        if c:
                            dve.wait_ge(qs, c)
                        for h in range(H):
                            dve.scalar_tensor_tensor(out=S[:, h, :], in0=S[:, h, :], scalar=kept["rates"][:, c, 1, h:h + 1],
                                                     in1=b[4][:, h, :], op0=ALU.mult, op1=ALU.add).then_inc(s_done, 1)
                    if c:
                        dve.wait_ge(o_kept, c + 1)
                        for h in range(H):
                            dve.scalar_tensor_tensor(out=o[:, c, h * P:(h + 1) * P], in0=b[1][:, h, :],
                                                     scalar=kept["rates"][:, c, 0, h:h + 1], in1=o[:, c, h * P:(h + 1) * P],
                                                     op0=ALU.mult, op1=ALU.add).then_inc(o_done, 1)

            @block.scalar
            def _(act):
                for c in range(TT):
                    act.wait_ge(intra, c + 1)
                    act.activation(o[:, c, :], k.ps[3][:, :], ACT.Copy).then_inc(o_kept, 1)


def gate_and_turn(nc, k, io, mixed, proj, out):
    hi, lo = out
    H, half = G_HEADS, A_HEADS * A_DH
    with ExitStack() as st:
        sq = k.sb("m_sq", [P, TT, H, P], ctx=st)
        stat = k.sb("m_stat", [P, 4, TT * H], ctx=st)
        norm_w = k.sb("m_norm_w", [P, 1], ctx=st)
        m32 = k.sb("m_m32", [P, 2, T], ctx=st)
        names = ("w_in", "sq_done", "summed", "rooted", "vec", "scaled", "gated", "turned", "m32_done", "hi_done", "lo_done")
        s = {n: k.sem(f"m_{n}") for n in names}
        with nc.Block() as block:
            @block.sync
            def _(sp):
                sp.dma_start(norm_w[:, :], io["gdn_norm_w"].rearrange("a p -> p a")).then_inc(s["w_in"], 16)

            @block.scalar
            def _(act):
                for t in range(TT):
                    act.activation(sq[:, t, :, :].rearrange("p h n -> p (h n)"), mixed[:, t, half:D], ACT.Square
                                   ).then_inc(s["sq_done"], 1)
                act.wait_ge(s["summed"], TT)
                act.activation(stat[:, 1, :], stat[:, 0, :], ACT.Sqrt, scale=1.0 / P, bias=k.eps[:, 0:1]).then_inc(s["rooted"], 1)
                for z in (Z0, DZ0):
                    for c in range(4):
                        act.activation(proj[:, z + c, :], proj[:, z + c, :], ACT.Silu).then_inc(s["gated"], 1)
                for c in range(DC):
                    act.wait_ge(s["m32_done"], c + 1)
                    act.activation(hi[:, c, :], m32[:, c % 2, :], ACT.Copy).then_inc(s["hi_done"], 1)

            @block.vector
            def _(dve):
                for t in range(TT):
                    dve.wait_ge(s["sq_done"], t + 1)
                    dve.tensor_reduce(stat[:, 0, t * H:(t + 1) * H], sq[:, t, :, :], AX_X, ALU.add).then_inc(s["summed"], 1)
                dve.wait_ge(s["rooted"], 1)
                refined_rsqrt(Chain(dve, s["vec"]), dve, stat[:, 2, :], stat[:, 1, :], stat[:, 0, :], stat[:, 3, :], 1.0 / P)
                for t in range(TT):
                    for h in range(H):
                        v = mixed[:, t, half + h * P:half + (h + 1) * P]
                        dve.tensor_scalar(v, v, stat[:, 2, t * H + h:t * H + h + 1], None, ALU.mult).then_inc(s["scaled"], 1)
                dve.wait_ge(s["w_in"], 16)
                for c in range(DC):
                    z = Z0 + c if c < 4 else DZ0 + c - 4
                    dve.wait_ge(s["turned"], c + 1)
                    dve.wait_ge(s["gated"], c + 1)
                    if c >= 2:
                        dve.wait_ge(s["lo_done"], c - 1)
                    dve.scalar_tensor_tensor(out=m32[:, c % 2, :], in0=k.ps[c][:, :], scalar=1.0 if c < 4 else norm_w[:, 0:1],
                                             in1=proj[:, z, :], op0=ALU.mult, op1=ALU.mult).then_inc(s["m32_done"], 1)
                    dve.wait_ge(s["hi_done"], c + 1)
                    dve.tensor_tensor(lo[:, c, :], m32[:, c % 2, :], hi[:, c, :].bitcast(F32), ALU.subtract).then_inc(s["lo_done"], 1)

            @block.tensor
            def _(pe):
                for c in range(DC):
                    if c == DC // 2:
                        pe.wait_ge(s["scaled"], TT * H)
                    for t in range(TT):
                        mm = pe.transpose(k.ps[c][:, t * P:(t + 1) * P], mixed[:, t, c * P:(c + 1) * P], k.ident[:, :])
                    mm.then_inc(s["turned"], 1)


def project_out(nc, k, tag, weight, src, post=None):
    hi, lo = src
    with ExitStack() as st:
        raw, whi, wlo = ([k.sb(f"{tag}_{n}{b}", [P, D], dt, ctx=st) for b in range(2)]
                         for n, dt in (("raw", F32), ("whi", F32R), ("wlo", F32R)))
        raw_in, w_hi, w_lo = k.sems(f"{tag}_raw_in", 2), k.sems(f"{tag}_w_hi", 2), k.sems(f"{tag}_w_lo", 2)
        used, summed = k.sem(f"{tag}_used"), k.sem(f"{tag}_summed")
        if post is not None:
            stat = k.sb(f"{tag}_stat", [P, 5, TT], ctx=st)
            halves = k.sb(f"{tag}_halves", [P, TT, 2], ctx=st)
            post_w = k.sb(f"{tag}_post_w", [P, D], ctx=st)
            junk = k.sb(f"{tag}_junk", [P, 2, T], ctx=st)
            normed = k.sb(f"{tag}_normed", [P, 2, T], ctx=st)
            post_in, sq_done, sums_done, rooted, vec, normed_done, added = (
                k.sem(f"{tag}_{n}") for n in ("post_in", "sq_done", "sums_done", "rooted", "vec", "normed_done", "added"))
        with nc.Block() as block:
            @block.sync
            def _(sp):
                if post is not None:
                    sp.dma_start(post_w[:, :], post.partition_broadcast(P)).then_inc(post_in, 16)
                for c in range(DC):
                    if c >= 2:
                        sp.wait_ge(w_lo[c % 2], c // 2)
                    sp.dma_start(raw[c % 2][:, :], weight[c * P:(c + 1) * P, :]).then_inc(raw_in[c % 2], 16)

            @block.vector
            def _(dve):
                for c in range(DC):
                    b = c % 2
                    dve.wait_ge(raw_in[b], 16 * (c // 2 + 1))
                    if c >= 2:
                        dve.wait_ge(used, c - 1)
                    dve.tensor_copy(whi[b][:, :], raw[b][:, :]).then_inc(w_hi[b], 1)
                    dve.wait_ge(w_hi[b], c // 2 + 1)
                    dve.tensor_tensor(wlo[b][:, :], raw[b][:, :], whi[b][:, :].bitcast(F32), ALU.subtract).then_inc(w_lo[b], 1)
                if post is None:
                    for n in range(2 * TT):
                        t, f = n // 2, slice(n % 2 * T, n % 2 * T + T)
                        if n == 0:
                            dve.wait_ge(summed, 1)
                        dve.tensor_tensor(k.xh[:, t, f], k.xh[:, t, f], k.ps[n][:, :], ALU.add)
                    return
                chain = Chain(dve, vec)
                dve.wait_ge(sq_done, 2 * TT)
                dve.tensor_tensor(stat[:, 0, :], halves[:, :, 0], halves[:, :, 1], ALU.add).then_inc(sums_done, 1)
                dve.wait_ge(rooted, 1)
                refined_rsqrt(chain, dve, stat[:, 2, :], stat[:, 1, :], stat[:, 0, :], stat[:, 3, :], 1.0 / D)
                dve.wait_ge(post_in, 16)
                for n in range(2 * TT):
                    t, f = n // 2, slice(n % 2 * T, n % 2 * T + T)
                    if n >= 2:
                        dve.wait_ge(added, n - 1)
                    dve.scalar_tensor_tensor(out=normed[:, n % 2, :], in0=k.ps[n][:, :], scalar=stat[:, 2, t:t + 1],
                                             in1=post_w[:, f], op0=ALU.mult, op1=ALU.mult).then_inc(normed_done, 1)
                    dve.wait_ge(normed_done, n + 1)
                    dve.tensor_tensor(k.xh[:, t, f], k.xh[:, t, f], normed[:, n % 2, :], ALU.add).then_inc(added, 1)

            @block.tensor
            def _(pe):
                for c in range(DC):
                    b = c % 2
                    pe.wait_ge(w_lo[b], c // 2 + 1)
                    for n in range(2 * TT):
                        t, f = n // 2, slice(n % 2 * T, n % 2 * T + T)
                        for x, w in ((hi, whi), (hi, wlo), (lo, whi)):
                            mm = pe.matmul(k.ps[n][:, :], x[:, c, t * P:(t + 1) * P], w[b][:, f],
                                           start=(c == 0 and x is hi and w is whi), stop=(c == DC - 1 and x is lo))
                    if c < DC - 1:
                        mm.then_inc(used, 1)
                mm.then_inc(summed, 1)

            if post is not None:
                @block.scalar
                def _(act):
                    act.wait_ge(summed, 1)
                    for n in range(2 * TT):
                        if n >= 2:
                            act.wait_ge(sq_done, n - 1)
                        act.activation(junk[:, n % 2, :], k.ps[n][:, :], ACT.Square,
                                       accum_out=halves[:, n // 2, n % 2:n % 2 + 1]).then_inc(sq_done, 1)
                    act.wait_ge(sums_done, 1)
                    act.activation(stat[:, 1, :], stat[:, 0, :], ACT.Sqrt, scale=1.0 / D, bias=k.eps[:, 0:1]).then_inc(rooted, 1)


XA, VB, CB, BB, GA, MA, MB = range(7)
W_COLUMNS = {XA: 0, GA: 1, VB: 2, BB: 3, CB: 4, MA: 5, MB: 6}
ATANH_TERMS = 9


def mixers(nc, k, io, src, out):
    hi, lo = src
    mhi, mlo = out
    w_dram = io["w_in_2"][0].rearrange("(c p) n -> p c n", p=P)
    last = L_HEADS - 1
    with ExitStack() as st:
        raw, whi, wlo = ([k.sb(f"x_{n}{s}", [P, DC, P], dt, ctx=st) for s in range(7)]
                         for n, dt in (("raw", F32), ("whi", F32R), ("wlo", F32R)))
        w_gate = k.sb("x_w_gate", [P, 2, P], ctx=st)
        tile = lambda n: k.sb(f"x_{n}", [P, T], ctx=st)
        xc, r, ig, tau, den, e, a, mult, h, ge, vb, cv, yb, sa, sb_ = (
            tile(n) for n in ("xc", "r", "ig", "tau", "den", "e", "a", "mult", "h", "ge", "vb", "cv", "yb", "sa", "sb"))
        rate = k.sb("x_rate", [P, 4, L_HEADS], ctx=st)
        raw_in, w_hi, w_lo, product = (k.sems(f"x_{n}", 7) for n in ("raw_in", "w_hi", "w_lo", "product"))
        names = ("gate_in", "rate_act", "rate_done", "xc_done", "r_ready", "i_ready", "r_done", "i_done", "tau_done",
                 "sqrt_in", "mult_done", "vb_kept", "ge_done", "sa_done", "sb_done", "m_done", "hi_done", "lo_done", "vec")
        s = {n: k.sem(f"x_{n}") for n in names}
        lam0, nl = COLS["lam"]
        col = lambda name, i, j=0, per=L_HEADS: k.cols[:, bass.ds(i + (COLS[name][0] + j * per), 1)]
        VEC = 19

        k.credit()
        with nc.Block() as block:
            @block.sync
            def _(sp):
                def load(i, first):
                    for n in range(7):
                        if not first:
                            sp.wait_ge(w_lo[n], after(i))
                        sp.dma_start(raw[n][:, :, :], w_dram[:, :, bass.ds(i * P + W_COLUMNS[n] * D, P)]).then_inc(raw_in[n], 16)
                        if n == XA:
                            if not first:
                                sp.wait_ge(s["i_ready"], after(i))
                            for j, name in enumerate(("w_a_2", "w_x_2")):
                                sp.dma_start(w_gate[:, j, :], io[name][0, bass.ds(i, 1), :, :].rearrange("a i j -> (a i) j")
                                             ).then_inc(s["gate_in"], 16)
                load(0, True)
                with sp.Fori(1, L_HEADS) as i:
                    load(i, False)

            @block.vector
            def _(dve):
                def split(i, n, first=False):
                    dve.wait_ge(raw_in[n], after(i * 16 + 16))
                    if not first:
                        dve.wait_ge(product[n], after(i))
                    dve.tensor_copy(whi[n][:, :, :], raw[n][:, :, :]).then_inc(w_hi[n], 1)
                    dve.wait_ge(w_hi[n], after(i + 1))
                    dve.tensor_tensor(wlo[n][:, :, :], raw[n][:, :, :], whi[n][:, :, :].bitcast(F32), ALU.subtract).then_inc(w_lo[n], 1)

                for n in range(7):
                    split(0, n, True)
                order = Chain(dve, s["rate_done"], done=1)
                dve.wait_ge(s["rate_act"], after(2))
                order(dve.tensor_scalar(rate[:, 1, :], rate[:, 0, :], 2.0, None, ALU.add))
                order(dve.reciprocal(rate[:, 1, :], rate[:, 1, :]))
                order(dve.tensor_tensor(rate[:, 0, :], rate[:, 0, :], rate[:, 1, :], ALU.mult))
                order(dve.tensor_tensor(rate[:, 1, :], rate[:, 0, :], rate[:, 0, :], ALU.mult))
                order(dve.tensor_scalar(rate[:, 2, :], rate[:, 1, :], 1.0 / (2 * ATANH_TERMS - 1), 1.0 / (2 * ATANH_TERMS - 3), ALU.mult, ALU.add))
                for n in range(ATANH_TERMS - 3, -1, -1):
                    order(dve.tensor_tensor(rate[:, 2, :], rate[:, 2, :], rate[:, 1, :], ALU.mult))
                    order(dve.tensor_scalar(rate[:, 2, :], rate[:, 2, :], 1.0 / (2 * n + 1), None, ALU.add))
                order(dve.tensor_tensor(rate[:, 2, :], rate[:, 2, :], rate[:, 0, :], ALU.mult))
                order(dve.tensor_scalar(rate[:, 1, :], k.cols[:, lam0:lam0 + nl], -1.0, 0.0, ALU.mult, ALU.max))
                order(dve.tensor_scalar(rate[:, 2, :], rate[:, 2, :], -8.0, None, ALU.mult))
                order(dve.tensor_scalar(rate[:, 1, :], rate[:, 1, :], -4.0, None, ALU.mult))
                order(dve.tensor_tensor(rate[:, 3, :], rate[:, 2, :], rate[:, 1, :], ALU.add))
                rate_steps = order.n

                def head(i, more):
                    chain = Chain(dve, s["vec"], i, VEC, done=1)
                    nxt = (lambda n: split(i + 1, n)) if more else (lambda n: None)
                    dve.wait_ge(product[XA], after(i + 1))
                    dve.wait_ge(s["i_ready"], after(i))
                    p = k.ps[0]
                    chain(dve.tensor_scalar(xc[:, :], p[:, :], col("conv_a", i, 3), col("conv_a_b", i), ALU.mult, ALU.add))
                    for j in (2, 1, 0):
                        d = 3 - j
                        ins = dve.scalar_tensor_tensor(out=xc[:, d:T], in0=p[:, 0:T - d], scalar=col("conv_a", i, j),
                                                       in1=xc[:, d:T], op0=ALU.mult, op1=ALU.add)
                        if j:
                            chain(ins)
                        else:
                            ins.then_inc(s["xc_done"], 1)
                    nxt(XA)
                    dve.wait_ge(product[CB], after(i + 1))
                    dve.wait_ge(s["vb_kept"], after(i + 1))
                    chain(dve.tensor_tensor(cv[:, :], vb[:, :], k.ps[2][:, :], ALU.mult))
                    chain(dve.tensor_scalar(yb[:, :], cv[:, :], col("conv_b", i, 2), None, ALU.mult))
                    for j in (1, 0):
                        d = 2 - j
                        chain(dve.scalar_tensor_tensor(out=yb[:, d:T], in0=cv[:, 0:T - d], scalar=col("conv_b", i, j),
                                                       in1=yb[:, d:T], op0=ALU.mult, op1=ALU.add))
                    nxt(VB)
                    nxt(CB)
                    dve.wait_ge(product[BB], after(i + 1))
                    chain(dve.tensor_tensor(yb[:, :], yb[:, :], k.ps[3][:, :], ALU.mult))
                    nxt(BB)
                    dve.wait_ge(s["tau_done"], after(i + 1))
                    chain(dve.tensor_scalar(den[:, :], tau[:, :], -1.0, 1.0, ALU.mult, ALU.add))
                    chain(dve.reciprocal(den[:, :], den[:, :]))
                    chain(dve.scalar_tensor_tensor(out=e[:, :], in0=tau[:, :], scalar=2.0, in1=den[:, :], op0=ALU.mult, op1=ALU.mult))
                    dve.scalar_tensor_tensor(out=den[:, :], in0=e[:, :], scalar=2.0, in1=e[:, :], op0=ALU.add, op1=ALU.mult
                                             ).then_inc(s["sqrt_in"], 1)
                    chain(dve.tensor_scalar(a[:, :], e[:, :], 1.0, None, ALU.add))
                    dve.wait_ge(s["i_done"], after(i + 1))
                    chain(dve.tensor_tensor(ig[:, :], ig[:, :], xc[:, :], ALU.mult))
                    dve.wait_ge(s["mult_done"], after(i + 1))
                    chain(dve.tensor_tensor(ig[:, :], ig[:, :], mult[:, :], ALU.mult))
                    chain(dve.tensor_tensor_scan(h[:, :], a[:, :], ig[:, :], 0.0, ALU.mult, ALU.add))
                    nxt(GA)
                    dve.wait_ge(s["ge_done"], after(i + 1))
                    chain(dve.tensor_tensor(h[:, :], h[:, :], ge[:, :], ALU.mult))
                    dve.wait_ge(s["sa_done"], after(i + 1))
                    chain(dve.tensor_tensor(h[:, :], h[:, :], sa[:, :], ALU.mult))
                    nxt(MA)
                    if more:
                        nxt(MB)
                    dve.wait_ge(s["sb_done"], after(i + 1))
                    chain(dve.tensor_tensor(yb[:, :], yb[:, :], sb_[:, :], ALU.mult))
                    dve.tensor_tensor(h[:, :], h[:, :], yb[:, :], ALU.add).then_inc(s["m_done"], 1)
                    dve.wait_ge(s["hi_done"], after(i + 1))
                    chain(dve.tensor_tensor(mlo[:, i, :], h[:, :], mhi[:, i, :].bitcast(F32), ALU.subtract))
                    assert chain.n == VEC, chain.n

                with dve.Fori(0, last) as i:
                    head(i, True)
                head(last, False)

            @block.tensor
            def _(pe):
                def section(i, n):
                    pe.wait_ge(w_lo[n], after(i + 1))
                    for c in range(DC):
                        for w, x in ((whi, hi), (whi, lo), (wlo, hi)):
                            mm = pe.matmul(k.ps[n][:, :], w[n][:, c, :], x[:, c, :], start=(c == 0 and w is whi and x is hi),
                                           stop=(c == DC - 1 and w is wlo))
                    mm.then_inc(product[n], 1)

                with pe.Fori(0, L_HEADS) as i:
                    pe.wait_ge(s["i_done"], after(i))
                    section(i, XA)
                    pe.wait_ge(s["vb_kept"], after(i))
                    section(i, VB)
                    pe.wait_ge(s["m_done"], after(i))
                    section(i, CB)
                    section(i, BB)
                    pe.wait_ge(s["gate_in"], after(i * 32 + 32))
                    pe.wait_ge(s["xc_done"], after(i + 1))
                    pe.wait_ge(s["r_done"], after(i))
                    pe.matmul(k.ps[7][:, :], w_gate[:, 0, :], xc[:, :], start=True, stop=True).then_inc(s["r_ready"], 1)
                    pe.matmul(k.ps[0][:, :], w_gate[:, 1, :], xc[:, :], start=True, stop=True).then_inc(s["i_ready"], 1)
                    pe.wait_ge(s["ge_done"], after(i))
                    section(i, GA)
                    pe.wait_ge(s["sa_done"], after(i))
                    section(i, MA)
                    pe.wait_ge(s["sb_done"], after(i))
                    section(i, MB)

            @block.scalar
            def _(act):
                act.activation(rate[:, 3, :], k.cols[:, lam0:lam0 + nl], ACT.Abs).then_inc(s["rate_act"], 1)
                act.wait_ge(s["rate_act"], after(1))
                act.activation(rate[:, 0, :], rate[:, 3, :], ACT.Exp, scale=-1.0).then_inc(s["rate_act"], 1)
                act.wait_ge(s["rate_done"], after(4 + 1 + 2 * (ATANH_TERMS - 2) + 5))
                with act.Fori(0, L_HEADS) as i:
                    act.wait_ge(product[VB], after(i + 1))
                    act.wait_ge(s["m_done"], after(i))
                    act.activation(vb[:, :], k.ps[1][:, :], ACT.Copy).then_inc(s["vb_kept"], 1)
                    act.wait_ge(s["r_ready"], after(i + 1))
                    act.activation(r[:, :], k.ps[7][:, :], ACT.Sigmoid, bias=col("b_a", i)).then_inc(s["r_done"], 1)
                    act.wait_ge(s["i_ready"], after(i + 1))
                    act.activation(ig[:, :], k.ps[0][:, :], ACT.Sigmoid, bias=col("b_x", i)).then_inc(s["i_done"], 1)
                    act.wait_ge(s["r_done"], after(i + 1))
                    act.activation(tau[:, :], r[:, :], ACT.Tanh, scale=rate[:, 3, bass.ds(i, 1)]).then_inc(s["tau_done"], 1)
                    act.wait_ge(s["sqrt_in"], after(i + 1))
                    act.activation(mult[:, :], den[:, :], ACT.Sqrt, scale=-1.0).then_inc(s["mult_done"], 1)
                    act.wait_ge(product[GA], after(i + 1))
                    act.activation(ge[:, :], k.ps[4][:, :], ACT.Gelu_apprx_tanh).then_inc(s["ge_done"], 1)
                    act.wait_ge(product[MA], after(i + 1))
                    act.activation(sa[:, :], k.ps[5][:, :], ACT.Sigmoid).then_inc(s["sa_done"], 1)
                    act.wait_ge(product[MB], after(i + 1))
                    act.activation(sb_[:, :], k.ps[6][:, :], ACT.Sigmoid).then_inc(s["sb_done"], 1)
                    act.wait_ge(s["m_done"], after(i + 1))
                    act.activation(mhi[:, i, :], h[:, :], ACT.Copy).then_inc(s["hi_done"], 1)


def choose_experts(nc, k, io, src, chosen, residual):
    H, K, LOW = PEER_HEADS, TOPK, -3.0e38
    hi, lo = src
    keys = io["peer_subkeys_2"][0].rearrange("h s n c -> n (h s) c")
    w_dram = io["peer_wq_2"][0].rearrange("(c p) n -> p c n", p=P)
    steps = 4
    per = GROUPS // steps
    heads = H // steps
    sections = 2 * steps
    pairs = TT * heads
    ROW0, MID, CAND = K, K + 7 * 8, K + 7 * 8 + 8
    with ExitStack() as st:
        raw = [k.sb(f"k_raw{b}", [P, DC, SEC], ctx=st) for b in range(2)]
        whi = [k.sb(f"k_whi{b}", [P, DC, SEC], F32R, ctx=st) for b in range(4)]
        wlo = [k.sb(f"k_wlo{b}", [P, DC, SEC], F32R, ctx=st) for b in range(4)]
        qt = k.sb("k_qt", [P, per, T], ctx=st)
        sc = [k.sb(f"k_sc{b}", [P, TT * per, NKEYS], ctx=st) for b in range(2)]
        kt = k.sb("k_t", [P, GROUPS, P], ctx=st)
        rest = k.sb("k_rest", [P, TT * per, NKEYS], ctx=st)
        top = k.sb("k_top", [P, TT * per, K], ctx=st)
        top_i = k.sb("k_top_i", [P, TT * per, K], U32, ctx=st)
        top_f = [k.sb(f"k_top_f{b}", [P, TT * per, K], ctx=st) for b in range(2)]
        cand = k.sb("k_cand", [P, pairs, CAND], ctx=st)
        rest2 = k.sb("k_rest2", [P, pairs, CAND], ctx=st)
        best = k.sb("k_best", [P, steps, pairs, K], ctx=st)
        largest = k.sb("k_largest", [P, steps, pairs], ctx=st)
        total = k.sb("k_total", [P, 2, steps, pairs], ctx=st)
        pos = k.sb("k_pos", [P, pairs, K], U32, ctx=st)
        part = k.sb("k_part", [P, 2, pairs, K], U32, ctx=st)
        eighth = k.sb("k_eighth", [P, 3, pairs, K], ctx=st)
        rank = k.sb("k_rank", [P, 2, pairs, K], ctx=st)
        flat = k.xh[:, :, :].rearrange("p t d -> p (t d)")
        eq = [flat[:, n * pairs * K * K:(n + 1) * pairs * K * K].rearrange("p (m a c) -> p m a c", m=pairs, a=K) for n in range(2)]
        sel = k.sb("k_sel", [P, 3, steps, pairs, K], ctx=st)
        raw_in, w_hi, w_lo = k.sems("k_raw_in", 2), k.sems("k_w_hi", 4), k.sems("k_w_lo", 4)
        product, q_kept, scored = k.sems("k_product", per), k.sems("k_q_kept", per), k.sems("k_scored", per)
        names = ("residual_out", "keys_in", "keys_turned", "sc_kept", "read", "vec", "matched",
                 "reduced", "shifted", "exped", "sel_done", "turned", "pool")
        s = {n: k.sem(f"k_{n}") for n in names}
        keys_of = lambda i: top_f[i % 2][:, :, :].rearrange("p (m s) a -> p s m a", s=2)

        def pick(eng, i, n):
            return eng.tensor_tensor(eq[n][:, :, :, :], eq[n][:, :, :, :],
                                     keys_of(i)[:, n, :, :].unsqueeze(2).to_broadcast([P, pairs, K, K]), ALU.mult)

        def low(eng, sec):
            b = sec % 4
            eng.wait_ge(w_hi[b], after(sec // 4 + 1))
            eng.tensor_tensor(wlo[b][:, :, :], raw[sec % 2][:, :, :], whi[b][:, :, :].bitcast(F32), ALU.subtract
                              ).then_inc(w_lo[b], 1)

        k.credit()
        with nc.Block() as block:
            @block.sync
            def _(sp):
                for sec in range(sections):
                    if sec >= 2:
                        sp.wait_ge(w_lo[(sec - 2) % 4], after((sec - 2) // 4 + 1))
                    sp.dma_start(raw[sec % 2][:, :, :], w_dram[:, :, sec * SEC:(sec + 1) * SEC]).then_inc(raw_in[sec % 2], 16)
                    if sec == 1:
                        sp.dma_start(sc[1][:, :, :], keys).then_inc(s["keys_in"], 16)
                        sp.dma_start(residual, k.xh[:, :, :]).then_inc(s["residual_out"], 16)
                sp.wait_ge(s["residual_out"], after(16))

            @block.tensor
            def _(pe):
                def queries(pair, half, n):
                    b = 2 * half + n // 2
                    if n % 2 == 0:
                        pe.wait_ge(w_lo[b], after(pair + 1))
                    for c in range(DC):
                        for w, x in ((whi, hi), (whi, lo), (wlo, hi)):
                            mm = pe.matmul(k.ps[n][:, :], w[b][:, c, n % 2 * P:(n % 2 + 1) * P], x[:, c, :],
                                           start=(c == 0 and w is whi and x is hi), stop=(c == DC - 1 and w is wlo))
                    return mm

                def scores(i, n):
                    pe.wait_ge(q_kept[n], after(i + 1))
                    for t in range(TT):
                        mm = pe.matmul(k.ps[4 + t][:, n * P:(n + 1) * P], qt[:, n, t * P:(t + 1) * P],
                                       kt[:, i * per + n, :], start=True, stop=True)
                    mm.then_inc(scored[n], 1)

                pe.wait_ge(s["keys_in"], after(16))
                for g in range(GROUPS):
                    mm = pe.transpose(k.ps[4 + g // 4][:, g % 4 * P:(g % 4 + 1) * P], sc[1][:, g, :], k.ident[:, :])
                    if g % 4 == 3:
                        mm.then_inc(s["keys_turned"], 1)
                with pe.Fori(0, steps // 2) as pair:
                    for half in range(2):
                        i = pair * 2 + half
                        for n in range(per):
                            pe.wait_ge(q_kept[n], after(i))
                            queries(pair, half, n).then_inc(product[n], 1)
                            if n == 1:
                                pe.wait_ge(s["sc_kept"], after(i * 4 + 4))
                            if n:
                                scores(i, n - 1)
                        scores(i, per - 1)
                pe.wait_ge(s["sel_done"], after(1))
                for t in range(TT):
                    for n in range(3):
                        mm = pe.transpose(k.ps[t][:, n * P:(n + 1) * P],
                                          flat[:, (t * 3 + n) * P:(t * 3 + n + 1) * P], k.ident[:, :])
                    mm.then_inc(s["turned"], 1)

            @block.scalar
            def _(act):
                def high(sec):
                    b = sec % 4
                    act.wait_ge(raw_in[sec % 2], after(16 * (sec // 2 + 1)))
                    if sec >= 4:
                        act.wait_ge(product[2 * (sec % 2) + 1], after(sec // 2 - 1))
                    act.activation(whi[b][:, :, :], raw[sec % 2][:, :, :], ACT.Copy).then_inc(w_hi[b], 1)
                high(0)
                high(1)
                for n in range(4):
                    act.wait_ge(s["keys_turned"], after(n + 1))
                    act.activation(kt[:, 4 * n:4 * n + 4, :].rearrange("p g n -> p (g n)"), k.ps[4 + n][:, :], ACT.Copy
                                   ).then_inc(s["sc_kept"], 1)
                high(2)
                high(3)
                for i in range(steps):
                    for n in range(per):
                        act.wait_ge(product[n], after(i + 1))
                        if i:
                            act.wait_ge(scored[n], after(i))
                        act.activation(qt[:, n, :], k.ps[n][:, :], ACT.Copy).then_inc(q_kept[n], 1)
                        if n % 2 and i + 2 < steps:
                            high(2 * (i + 2) + n // 2)
                    for n in range(per):
                        act.wait_ge(scored[n], after(i + 1))
                    if i >= 2:
                        act.wait_ge(s["read"], after(i - 1))
                    for t in range(TT):
                        act.activation(sc[i % 2][:, per * t:per * (t + 1), :].rearrange("p g n -> p (g n)"), k.ps[4 + t][:, :],
                                       ACT.Copy).then_inc(s["sc_kept"], 1)
                act.wait_ge(s["shifted"], after(steps))
                act.activation(best[:, :, :, :], best[:, :, :, :], ACT.Exp).then_inc(s["exped"], 1)
                for t in range(TT):
                    act.wait_ge(s["turned"], after(t + 1))
                    act.activation(chosen[:, :, t * P:(t + 1) * P], k.ps[t][:, 0:3 * P].rearrange("p (n t) -> p n t", n=3), ACT.Copy)

            @block.gpsimd
            def _(pool):
                order = Chain(pool, s["pool"], done=1)

                def select(i):
                    for n in range(2):
                        pool.wait_ge(s["matched"], after(2 * i + n + 1))
                        order(pick(pool, i, n))
                        for w in (8, 4, 2):
                            order(pool.tensor_tensor(eq[n][:, :, :, 0:w], eq[n][:, :, :, 0:w], eq[n][:, :, :, w:2 * w], ALU.add))
                        pool.tensor_tensor(sel[:, n, i, :, :], eq[n][:, :, :, 0], eq[n][:, :, :, 1], ALU.add
                                           ).then_inc(s["reduced"], 1)
                low(pool, 4)
                low(pool, 5)
                low(pool, 6)
                select(0)
                low(pool, 7)
                select(1)
                select(2)

            @block.vector
            def _(dve):
                order = Chain(dve, s["vec"], done=1)

                for sec in range(4):
                    low(dve, sec)
                for i in range(steps):
                    b, tops = i % 2, top[:, :, :].rearrange("p (m s) a -> p s m a", s=2)
                    if i >= 2:
                        dve.wait_ge(s["reduced"], after(2 * (i - 1)))
                    for t in range(TT):
                        dve.wait_ge(s["sc_kept"], after(4 * (i + 1) + t + 1))
                        for g in range(per * t, per * (t + 1)):
                            order.add(dve.max(top[:, g, 0:8], sc[b][:, g, :]))
                    order.wait()
                    for g in range(TT * per):
                        order.add(dve.max_index(top_i[:, g, 0:8], top[:, g, 0:8], sc[b][:, g, :]))
                        order.add(dve.match_replace(rest[:, g, :], top[:, g, 0:8], sc[b][:, g, :], LOW))
                    order.wait()
                    dve.sem_inc(s["read"], 1)
                    for g in range(TT * per):
                        order.add(dve.max(top[:, g, 8:16], rest[:, g, :]))
                    order.wait()
                    for g in range(TT * per):
                        order.add(dve.max_index(top_i[:, g, 8:16], top[:, g, 8:16], rest[:, g, :]))
                    order.wait()
                    order.add(dve.tensor_copy(top_f[b][:, :, :], top_i[:, :, :]))
                    first = lambda a0, a1, n: tops[:, 0, :, a0:a1].unsqueeze(3).to_broadcast([P, pairs, a1 - a0, n])
                    second = lambda rows, n: tops[:, 1, :, 0:n].unsqueeze(2).to_broadcast([P, pairs, rows, n])
                    for at, a0, a1, n in ((0, 0, 1, K), (ROW0, 1, 8, 8), (MID, 8, K, 1)):
                        order.add(dve.tensor_tensor(cand[:, :, at:at + (a1 - a0) * n].rearrange("p m (a c) -> p m a c", c=n),
                                                    first(a0, a1, n), second(a1 - a0, n), ALU.add))
                    order.wait()
                    for m in range(pairs):
                        order.add(dve.max(best[:, i, m, 0:8], cand[:, m, :]))
                    order.wait()
                    for m in range(pairs):
                        order.add(dve.max_index(pos[:, m, 0:8], best[:, i, m, 0:8], cand[:, m, :]))
                        order.add(dve.match_replace(rest2[:, m, :], best[:, i, m, 0:8], cand[:, m, :], LOW))
                    order.wait()
                    for m in range(pairs):
                        order.add(dve.max(best[:, i, m, 8:16], rest2[:, m, :]))
                    order.wait()
                    for m in range(pairs):
                        order.add(dve.max_index(pos[:, m, 8:16], best[:, i, m, 8:16], rest2[:, m, :]))
                    order.wait()
                    order.add(dve.tensor_copy(largest[:, i, :], best[:, i, :, 0]))
                    order.add(dve.tensor_scalar(part[:, 0, :, :], pos[:, :, :], 3, None, ALU.logical_shift_right))
                    order(dve.tensor_scalar(part[:, 1, :, :], pos[:, :, :], 7, None, ALU.bitwise_and))
                    dve.tensor_tensor(best[:, i, :, :], best[:, i, :, :], largest[:, i, :].unsqueeze(2).to_broadcast([P, pairs, K]),
                                      ALU.subtract).then_inc(s["shifted"], 1)
                    order(dve.tensor_copy(eighth[:, 0:2, :, :], part[:, :, :, :]))
                    q, r, last = (eighth[:, n, :, :] for n in range(3))
                    order.add(dve.tensor_scalar(rank[:, 0, :, :], q, 1.0, 0.0, ALU.subtract, ALU.max))
                    order.add(dve.tensor_scalar(rank[:, 1, :, :], q, 1.0, 8.0, ALU.is_equal, ALU.mult))
                    order(dve.scalar_tensor_tensor(out=last, in0=q, scalar=float(MID // 8), in1=r, op0=ALU.is_equal, op1=ALU.mult))
                    order.add(dve.tensor_tensor(rank[:, 0, :, :], rank[:, 0, :, :], last, ALU.add))
                    order(dve.tensor_tensor(r, r, last, ALU.subtract))
                    order(dve.tensor_tensor(rank[:, 1, :, :], rank[:, 1, :, :], r, ALU.add))
                    if i:
                        dve.wait_ge(s["reduced"], after(2 * i))
                    else:
                        dve.wait_ge(s["residual_out"], after(16))
                    for n in range(2):
                        dve.tensor_tensor(eq[n][:, :, :, :], rank[:, n, :, :].unsqueeze(3).to_broadcast([P, pairs, K, K]),
                                          k.row[:, 0:K].unsqueeze(1).unsqueeze(1).to_broadcast([P, pairs, K, K]), ALU.is_equal
                                          ).then_inc(s["matched"], 1)
                for n in range(2):
                    dve.wait_ge(s["matched"], after(2 * steps - 1 + n))
                    order(pick(dve, steps - 1, n))
                    dve.tensor_reduce(sel[:, n, steps - 1, :, :], eq[n][:, :, :, :], AX_X, ALU.add).then_inc(s["reduced"], 1)
                dve.wait_ge(s["exped"], after(1))
                order(dve.tensor_reduce(total[:, 0, :, :], best[:, :, :, :], AX_X, ALU.add))
                order(dve.reciprocal(total[:, 1, :, :], total[:, 0, :, :]))
                order(dve.tensor_tensor(sel[:, 2, :, :, :].rearrange("p i m a -> p (i m) a"),
                                        best[:, :, :, :].rearrange("p i m a -> p (i m) a"),
                                        total[:, 1, :, :].rearrange("p i m -> p (i m)").unsqueeze(2).to_broadcast([P, steps * pairs, K]), ALU.mult))
                dve.wait_ge(s["reduced"], after(2 * steps))
                for t in range(TT):
                    for n in range(3):
                        ins = dve.tensor_copy(flat[:, (t * 3 + n) * P:(t * 3 + n + 1) * P].rearrange("p (i r) -> p i r", i=steps),
                                              sel[:, n, :, heads * t:heads * (t + 1), :].rearrange("p i h a -> p i (h a)"))
                        if t == TT - 1 and n == 2:
                            order.wait()
                            ins.then_inc(s["sel_done"], 1)
                        else:
                            order.add(ins)


EXPERT_TILES = NKEYS
PER = 4
TOK_TILE = T // EXPERT_TILES
CHUNK_TILES = P // TOK_TILE


def first_products(nc, k, io, src, chosen, acts, weights):
    hi, lo = src
    u_dram = io["peer_u_2"][0].rearrange("(p c) d -> p c d", c=NKEYS)
    chunks = T // P
    pieces = 16
    with ExitStack() as st:
        raw = [k.xh[:, b, :] for b in range(2)]
        ga = [k.xh[:, 2, b * T:(b + 1) * T] for b in range(2)]
        one = [k.xh[:, 3, b * T:(b + 1) * T].rearrange("p (q n) -> p q n", q=TOK_TILE) for b in range(2)]
        two = [k.sb(f"u_two{s}", [P, TOK_TILE, P], ctx=st) for s in range(2)]
        uhi = [k.sb(f"u_hi{s}", [P, DC, P], F32R, ctx=st) for s in range(2)]
        ulo = [k.sb(f"u_lo{s}", [P, DC, P], F32R, ctx=st) for s in range(2)]
        spread = k.sb("u_spread", [P, 2, NKEYS, P], ctx=st)
        names = ("raw_in", "turned", "hi_done", "lo_done", "product", "ga_done", "ga_out", "one_done", "spread_ready",
                 "spread_kept", "stored")
        s = {n: k.sems(f"u_{n}", 2) for n in names}
        rounds = CHUNK_TILES // PER
        half = PER // 2

        def loop(eng, body, chunk=lambda pair, parity: None):
            with eng.Fori(0, chunks // 2) as pair:
                for parity in range(2):
                    chunk(pair, parity)
                    with eng.Fori(0, rounds) as r:
                        body(pair * (2 * rounds) + (r + parity * rounds), parity, r)

        def place(n, u):
            return u % 2, n * half + u // 2

        k.credit()
        piece_out = k.sems("u_piece_out", 2)
        with nc.Block() as block:
            @block.sync
            def _(sp):
                def load(n, u):
                    b, before = place(n, u)
                    sp.wait_ge(s["turned"][b], after(before * 2))
                    sp.dma_start(raw[b], u_dram[:, bass.ds((n * PER + u) % EXPERT_TILES, 1), :].rearrange("p a d -> p (a d)")
                                 ).then_inc(s["raw_in"][b], 16)

                def body(n, parity, r):
                    for u in range(PER):
                        load(n, u + 1)
                load(0, 0)
                loop(sp, body)

            @block.gpsimd
            def _(pool):
                step = NKEYS // pieces
                with pool.Fori(0, chunks // 2) as pair:
                    for parity in range(2):
                        for b in range(2):
                            pool.wait_ge(s["spread_kept"][b], after(pair * CHUNK_TILES + (parity + 1) * (CHUNK_TILES // 2)))
                        for at in range(0, NKEYS, step):
                            pool.dma_start(weights[at:at + step, :, bass.ds(pair * (2 * P) + parity * P, P)].rearrange("n p t -> p n t"),
                                           spread[:, parity, at:at + step, :]).then_inc(piece_out[parity], 16)
                        pool.wait_ge(piece_out[parity], pair * (16 * pieces) + 16 * pieces)
                        pool.sem_inc(s["stored"][parity], 1)

            @block.tensor
            def _(pe):
                def turn(n, u):
                    b, before = place(n, u)
                    pe.wait_ge(s["raw_in"][b], after(before * 16 + 16))
                    pe.wait_ge(s["lo_done"][b], after(before * 2))
                    for f in range(2):
                        for c in range(4 * f, 4 * f + 4):
                            mm = pe.transpose(k.ps[2 * b + f][:, c % 4 * P:(c % 4 + 1) * P], raw[b][:, c * P:(c + 1) * P], k.ident[:, :])
                        mm.then_inc(s["turned"][b], 1)

                def multiply(n, u):
                    b, before = place(n, u)
                    pe.wait_ge(s["ga_done"][b], after(before))
                    for c in range(DC):
                        if c % 4 == 0:
                            pe.wait_ge(s["lo_done"][b], after(before * 2 + (c // 4 + 1)))
                        for w, x in ((uhi, hi), (uhi, lo), (ulo, hi)):
                            mm = pe.matmul(k.ps[4 + b][:, :], w[b][:, c, :], x[:, c, :], start=(c == 0 and w is uhi and x is hi),
                                           stop=(c == DC - 1 and w is ulo))
                    mm.then_inc(s["product"][b], 1)
                    pe.wait_ge(s["one_done"][b], after(before * (2 * TOK_TILE) + 2 * TOK_TILE))
                    pe.wait_ge(s["spread_kept"][b], after(before))
                    for q in range(TOK_TILE):
                        mm = pe.matmul(k.ps[6 + b][:, q * P:(q + 1) * P], one[b][:, q, :], two[b][:, q, :], start=True, stop=True)
                    mm.then_inc(s["spread_ready"][b], 1)

                def body(n, parity, r):
                    for u in range(PER):
                        turn(n, u + 1)
                        multiply(n, u)
                turn(0, 0)
                loop(pe, body)

            @block.vector
            def _(dve):
                def low(n, u):
                    b, before = place(n, u)
                    for f in range(2):
                        dve.wait_ge(s["hi_done"][b], after(before * 2 + (f + 1)))
                        dve.tensor_tensor(ulo[b][:, 4 * f:4 * f + 4, :], k.ps[2 * b + f][:, :].rearrange("p (c n) -> p c n", c=4),
                                          uhi[b][:, 4 * f:4 * f + 4, :].bitcast(F32), ALU.subtract).then_inc(s["lo_done"][b], 1)

                def onehots(n, u):
                    b, before = place(n, u)
                    dve.wait_ge(s["spread_ready"][b], after(before))
                    for q in range(TOK_TILE):
                        at = bass.ds(n * (PER * TOK_TILE) + (u * TOK_TILE + q), 1)
                        dve.tensor_scalar(one[b][:, q, :], k.row[:, :], chosen[:, 0, at], None, ALU.is_equal
                                          ).then_inc(s["one_done"][b], 1)
                        dve.tensor_scalar(two[b][:, q, :], k.row[:, :], chosen[:, 1, at], chosen[:, 2, at],
                                          ALU.is_equal, ALU.mult).then_inc(s["one_done"][b], 1)

                def body(n, parity, r):
                    for u in range(PER):
                        low(n, u + 1)
                        onehots(n, u)
                low(0, 0)
                loop(dve, body)

            @block.scalar
            def _(act):
                def high(n, u):
                    b, before = place(n, u)
                    act.wait_ge(s["product"][b], after(before))
                    for f in range(2):
                        act.wait_ge(s["turned"][b], after(before * 2 + (f + 1)))
                        act.activation(uhi[b][:, 4 * f:4 * f + 4, :], k.ps[2 * b + f][:, :].rearrange("p (c n) -> p c n", c=4),
                                       ACT.Copy).then_inc(s["hi_done"][b], 1)

                def keep(n, u, parity, r):
                    b, before = place(n, u)
                    act.wait_ge(s["product"][b], after(before + 1))
                    act.wait_ge(s["ga_out"][b], after(before * 16))
                    act.activation(ga[b], k.ps[4 + b][:, :], ACT.Gelu_apprx_tanh).then_inc(s["ga_done"][b], 1)
                    act.wait_ge(s["spread_ready"][b], after(before + 1))
                    act.activation(spread[:, parity, :, bass.ds(r * (PER * TOK_TILE) + u * TOK_TILE, TOK_TILE)],
                                   k.ps[6 + b][:, :].rearrange("p (q n) -> p n q", q=TOK_TILE), ACT.Copy
                                   ).then_inc(s["spread_kept"][b], 1)
                    act.wait_ge(s["ga_done"][b], after(before + 1))
                    act.dma_start(acts[bass.ds(n * PER + u, 1), :, :].rearrange("a p t -> (a p) t"), ga[b]
                                  ).then_inc(s["ga_out"][b], 16)

                def body(n, parity, r):
                    for u in range(PER):
                        high(n, u + 1)
                        keep(n, u, parity, r)

                def chunk(pair, parity):
                    act.wait_ge(s["stored"][parity], after(pair))
                high(0, 0)
                loop(act, body, chunk)
                for b in range(2):
                    act.wait_ge(s["ga_out"][b], after(16 * EXPERT_TILES // 2))


def second_products(nc, k, io, acts, weights):
    v_dram = io["peer_v_2"][0].rearrange("(p c) d -> p c d", c=NKEYS)
    with ExitStack() as st:
        raw = [k.sb(f"v_raw{u}", [P, D], ctx=st) for u in range(PER)]
        ga = [k.sb(f"v_ga{u}", [P, T], ctx=st) for u in range(PER)]
        gg = [k.sb(f"v_gg{u}", [P, T], ctx=st) for u in range(PER)]
        h32 = [k.sb(f"v_h{b}", [P, T], ctx=st) for b in range(2)]
        vhi, vlo = ([k.sb(f"v_{n}{b}", [P, D], F32R, ctx=st) for b in range(2)] for n in ("vhi", "vlo"))
        hhi, hlo = ([k.sb(f"v_{n}{b}", [P, T], F32R, ctx=st) for b in range(2)] for n in ("hhi", "hlo"))
        zero = k.sb("v_zero", [P, T], ctx=st)
        v_in, ga_in, gg_in = (k.sems(f"v_{n}", PER) for n in ("in", "ga_in", "gg_in"))
        slot_v, slot_h = k.sems("v_split_slot", PER), k.sems("v_weighted_slot", PER)
        s = {n: k.sems(f"v_{n}", 2) for n in ("vhi_done", "hhi_done", "hlo_done", "used")}
        zeroed = k.sem("v_zeroed")
        rounds, half = EXPERT_TILES // PER, PER // 2
        place = lambda n, u: (u % 2, n * half + u // 2)
        k.credit()
        with nc.Block() as block:
            @block.sync
            def _(sp):
                with sp.Fori(0, rounds) as n:
                    for u in range(PER):
                        at = bass.ds(n * PER + u, 1)
                        sp.wait_ge(slot_v[u], after(n))
                        sp.dma_start(raw[u][:, :], v_dram[:, at, :].rearrange("p a d -> p (a d)")).then_inc(v_in[u], 16)
                        sp.wait_ge(slot_h[u], after(n))
                        sp.dma_start(ga[u][:, :], acts[at, :, :].rearrange("a p t -> (a p) t")).then_inc(ga_in[u], 16)
                        sp.dma_start(gg[u][:, :], weights[at, :, :].rearrange("a p t -> (a p) t")).then_inc(gg_in[u], 16)

            @block.vector
            def _(dve):
                dve.memset(zero[:, :], 0.0).then_inc(zeroed, 1)
                with dve.Fori(0, rounds) as n:
                    for u in range(PER):
                        b, before = place(n, u)
                        dve.wait_ge(ga_in[u], after(n * 16 + 16))
                        dve.wait_ge(gg_in[u], after(n * 16 + 16))
                        dve.wait_ge(s["hlo_done"][b], after(before))
                        dve.tensor_tensor(h32[b][:, :], ga[u][:, :], gg[u][:, :], ALU.mult).then_inc(slot_h[u], 1)
                        dve.wait_ge(s["vhi_done"][b], after(before + 1))
                        dve.tensor_tensor(vlo[b][:, :], raw[u][:, :], vhi[b][:, :].bitcast(F32), ALU.subtract).then_inc(slot_v[u], 1)
                        dve.wait_ge(s["hhi_done"][b], after(before + 1))
                        dve.wait_ge(slot_h[u], after(n + 1))
                        dve.tensor_tensor(hlo[b][:, :], h32[b][:, :], hhi[b][:, :].bitcast(F32), ALU.subtract).then_inc(s["hlo_done"][b], 1)

            @block.scalar
            def _(act):
                with act.Fori(0, rounds) as n:
                    for u in range(PER):
                        b, before = place(n, u)
                        act.wait_ge(v_in[u], after(n * 16 + 16))
                        act.wait_ge(s["used"][b], after(before))
                        act.activation(vhi[b][:, :], raw[u][:, :], ACT.Copy).then_inc(s["vhi_done"][b], 1)
                        act.wait_ge(slot_h[u], after(n + 1))
                        act.activation(hhi[b][:, :], h32[b][:, :], ACT.Copy).then_inc(s["hhi_done"][b], 1)

            @block.tensor
            def _(pe):
                pe.wait_ge(zeroed, after(1))
                for q in range(2 * TT):
                    pe.matmul(k.ps[q][:, :], zero[:, 0:P], zero[:, :], start=True, stop=False, skip_group_check=True)
                with pe.Fori(0, rounds) as n:
                    for u in range(PER):
                        b, before = place(n, u)
                        pe.wait_ge(slot_v[u], after(n + 1))
                        pe.wait_ge(s["hlo_done"][b], after(before + 1))
                        for q in range(2 * TT):
                            t, f = q // 2, slice(q % 2 * T, q % 2 * T + T)
                            for h, v in ((hhi, vhi), (hhi, vlo), (hlo, vhi)):
                                mm = pe.matmul(k.ps[q][:, :], h[b][:, t * P:(t + 1) * P], v[b][:, f], start=False, stop=False,
                                               skip_group_check=True)
                        mm.then_inc(s["used"][b], 1)
                for q in range(2 * TT):
                    pe.matmul(k.ps[q][:, :], zero[:, 0:P], zero[:, :], start=False, stop=True, skip_group_check=True)


def finish(nc, k, io, residual, out):
    out_t = out[0].rearrange("(t p) d -> t p d", p=P)
    with ExitStack() as st:
        gain = k.sb("f_gain", [P, D], ctx=st)
        y = k.sb("f_y", [P, TT, D], ctx=st)
        junk = k.sb("f_junk", [P, 2, D], ctx=st)
        stat = k.sb("f_stat", [P, 4, TT], ctx=st)
        gain_in, res_in, added, squared, rooted, vec, done, stored = (
            k.sem(f"f_{n}") for n in ("gain_in", "res_in", "added", "squared", "rooted", "vec", "done", "stored"))
        with nc.Block() as block:
            @block.sync
            def _(sp):
                sp.dma_start(k.xh[:, :, :], residual).then_inc(res_in, 16)
                sp.dma_start(gain[:, :], io["final_g_2"].partition_broadcast(P)).then_inc(gain_in, 16)
                for t in range(TT):
                    sp.wait_ge(done, t + 1)
                    sp.dma_start(out_t[t], y[:, t, :]).then_inc(stored, 16)
                sp.wait_ge(stored, 16 * TT)

            @block.vector
            def _(dve):
                dve.wait_ge(res_in, 16)
                for q in range(2 * TT):
                    t, f = q // 2, slice(q % 2 * T, q % 2 * T + T)
                    dve.tensor_tensor(k.xh[:, t, f], k.xh[:, t, f], k.ps[q][:, :], ALU.add).then_inc(added, 1)
                dve.wait_ge(rooted, 1)
                refined_rsqrt(Chain(dve, vec), dve, stat[:, 2, :], stat[:, 1, :], stat[:, 0, :], stat[:, 3, :], 1.0 / D)
                dve.wait_ge(gain_in, 16)
                dve.wait_ge(added, 2 * TT)
                for t in range(TT):
                    dve.scalar_tensor_tensor(out=y[:, t, :], in0=k.xh[:, t, :], scalar=stat[:, 2, t:t + 1], in1=gain[:, :],
                                             op0=ALU.mult, op1=ALU.mult).then_inc(done, 1)

            @block.scalar
            def _(act):
                for t in range(TT):
                    act.wait_ge(added, 2 * t + 2)
                    if t >= 2:
                        act.wait_ge(squared, t - 1)
                    act.activation(junk[:, t % 2, :], k.xh[:, t, :], ACT.Square, accum_out=stat[:, 0, t:t + 1]).then_inc(squared, 1)
                act.wait_ge(squared, TT)
                act.activation(stat[:, 1, :], stat[:, 0, :], ACT.Sqrt, scale=1.0 / D, bias=k.eps[:, 0:1]).then_inc(rooted, 1)


def build(nc, io, out):
    with ExitStack() as ctx:
        k = Kit(nc, ctx)
        k.ps = [ctx.enter_context(nc.psum_tensor(f"bank{b}", [P, T], F32)) for b in range(8)]
        k.ident = k.sb("ident", [P, P])
        k.cols = k.sb("cols", [P, NCOLS])
        k.eps = k.sb("eps", [P, 1])
        k.row = k.sb("row", [P, NKEYS])
        k.xh = k.sb("xh", [P, TT, D])
        with ExitStack() as st:
            k.ones = k.sb("ones", [P, P], ctx=st)
            k.upto, k.later = k.sb("upto", [P, P], ctx=st), k.sb("later", [P, P], ctx=st)
            k.level = k.sb("level", [P, LEVELS, P], ctx=st)
            k.qk_scale = k.sb("qk_scale", [P, G_HEADS], ctx=st)
            w8 = k.sb("w8", [P, DC, BA], ctx=st)
            load_constants(nc, k, io, w8)
            k.end_stage()
            mixed = k.sb("mixed", [P, TT, D], ctx=st)
            proj = k.sb("proj", [P, PROJ, T], ctx=st)
            gates = (k.sb("beta", [P, TT, G_HEADS], ctx=st), k.sb("g", [P, TT, G_HEADS], ctx=st))
            with ExitStack() as st2:
                xt = (k.sb("xt_hi", [P, DC, T], F32R, ctx=st2), k.sb("xt_lo", [P, DC, T], F32R, ctx=st2))
                norm_and_turn(nc, k, "n1", xt, "norm_pre")
                k.end_stage()
                project_first(nc, k, io, xt, w8, proj, gates)
                k.end_stage()
            attention(nc, k, proj, mixed)
            k.end_stage()
            o = mixed[:, :, A_HEADS * A_DH:D]
            with ExitStack() as st2:
                qkv = proj[:, DQ0:DZ0, :]
                kept = {n: proj[:, at:at + TT, :].rearrange("p c (h n) -> p c h n", h=G_HEADS)
                        for n, at in (("intra", Q0), ("inv", K0), ("kdec", V0))}
                kept["v"] = k.sb("kept_v", [P, TT, G_HEADS, P], ctx=st2)
                kept["rates"] = k.sb("kept_rates", [P, TT, 2, G_HEADS], ctx=st2)
                delta_prepare(nc, k, qkv, gates, kept)
                k.end_stage()
                delta_scan(nc, k, gates, kept, qkv, o)
                k.end_stage()
            with ExitStack() as st2:
                xt = (k.sb("mt_hi", [P, DC, T], F32R, ctx=st2), k.sb("mt_lo", [P, DC, T], F32R, ctx=st2))
                gate_and_turn(nc, k, io, mixed, proj, xt)
                k.end_stage()
                project_out(nc, k, "o1", io["w_out"][0], xt, post=io["norm_post_w"][0])
                k.end_stage()
        with ExitStack() as st:
            mt = (k.sb("g_hi", [P, DC, T], F32R, ctx=st), k.sb("g_lo", [P, DC, T], F32R, ctx=st))
            with ExitStack() as st2:
                xt = (k.sb("xt2_hi", [P, DC, T], F32R, ctx=st2), k.sb("xt2_lo", [P, DC, T], F32R, ctx=st2))
                norm_and_turn(nc, k, "n2", xt, "norm1")
                k.end_stage()
                mixers(nc, k, io, xt, mt)
                k.end_stage()
            project_out(nc, k, "o2", io["w_out_2"][0], mt)
            k.end_stage()
        residual = nc.dram_tensor("residual", (P, TT, D), F32, kind="Internal").ap()
        acts = nc.dram_tensor("acts", (EXPERT_TILES, P, T), F32, kind="Internal").ap()
        weights = nc.dram_tensor("weights", (EXPERT_TILES, P, T), F32, kind="Internal").ap()
        with ExitStack() as st:
            chosen = k.sb("chosen", [P, 3, T], ctx=st)
            xt = (k.sb("xt3_hi", [P, DC, T], F32R, ctx=st), k.sb("xt3_lo", [P, DC, T], F32R, ctx=st))
            norm_and_turn(nc, k, "n3", xt, "norm2")
            k.end_stage()
            choose_experts(nc, k, io, xt, chosen, residual)
            k.end_stage()
            first_products(nc, k, io, xt, chosen, acts, weights)
            k.end_stage()
        second_products(nc, k, io, acts, weights)
        k.end_stage()
        finish(nc, k, io, residual, out)
        k.end_stage()


_INS = ["x", "norm_pre_w", "w_in", "conv_w", "a_log", "dt_bias", "gdn_norm_w", "w_out", "norm_post_w", "norm1_g_2",
        "w_in_2", "conv_a_w_2", "conv_a_b_2", "w_a_2", "b_a_2", "w_x_2", "b_x_2", "lru_lambda_2", "conv_b_w_2",
        "w_out_2", "norm2_g_2", "peer_wq_2", "peer_subkeys_2", "peer_u_2", "peer_v_2", "final_g_2"]


def kernel(**inputs):
    import numpy as _np
    import concourse.bacc as _bacc
    from concourse.bass_utils import run_bass_kernel_spmd as _run

    nc = _bacc.Bacc("TRN2", target_bir_lowering=False, num_devices=1)
    arrays, io = {}, {}
    for name in _INS:
        a = _np.ascontiguousarray(inputs[name])
        arrays[f"in_{name}_dram"] = a
        io[name] = nc.dram_tensor(f"in_{name}_dram", a.shape, mybir.dt.from_np(a.dtype), kind="ExternalInput").ap()
    out = nc.dram_tensor("out_dram", (1, T, D), F32, kind="ExternalOutput").ap()
    build(nc, io, out)
    r = _run(nc, [arrays], core_ids=[0])
    return r.results[0]["out_dram"]
```

```python
from contextlib import ExitStack

import concourse.bass as bass
from concourse import mybir

F32 = mybir.dt.float32
F32R = mybir.dt.float32r
BF16 = mybir.dt.bfloat16
U32 = mybir.dt.uint32
ALU = mybir.AluOpType
ACT = mybir.ActivationFunctionType
AX_X = mybir.AxisListType.X

P = 128
T = 512
TT = T // P
D = 1024
DC = D // P
EPS = 1e-6
NEG = -1e30

A_HEADS, A_DH = 8, 64
Q0, K0, V0, Z0 = 0, 4, 8, 12
DQ0, DK0, DV0, DZ0 = 16, 20, 24, 28
PROJ = 32
G_HEADS = 4
G_CONV = 4
BA = 2 * G_HEADS
LEVELS = 7
SEC = 256

L_HEADS = 8
PEER_HEADS, NKEYS, TOPK = 8, 128, 16
EXPERT_TILES = NKEYS
EARLY = 8
GROUPS = 2 * PEER_HEADS

COLS, _at = {}, 0
for _name, _n in (("norm_pre", 8), ("norm1", 8), ("norm2", 8), ("conv", 48), ("conv_a", 32),
                  ("conv_a_b", 8), ("b_a", 8), ("b_x", 8), ("conv_b", 24), ("lam", 8)):
    COLS[_name] = (_at, _n)
    _at += _n
NCOLS = _at
COLS_A = COLS["conv_a"][0]


class Chain:

    def __init__(self, eng, sem, i=None, per=0, done=0):
        self.eng, self.sem, self.i, self.per, self.n, self.done = eng, sem, i, per, 0, done

    def value(self):
        return self.done + self.n if self.i is None else self.i * self.per + (self.done + self.n)

    def add(self, ins):
        self.n += 1
        ins.then_inc(self.sem, 1)

    def wait(self):
        self.eng.wait_ge(self.sem, self.value())

    def __call__(self, ins):
        self.add(ins)
        self.wait()

    def end(self):
        assert self.i is None or self.n == self.per, (self.n, self.per)


def after(count):
    return count + 1


class Kit:

    def __init__(self, nc, ctx):
        self.nc, self.ctx, self.used = nc, ctx, []

    def sb(self, name, shape, dt=F32, ctx=None):
        return (ctx or self.ctx).enter_context(self.nc.sbuf_tensor(name, shape, dt))

    def sem(self, name):
        self.used.append(self.nc.alloc_semaphore(name=name))
        return self.used[-1]

    def credit(self):
        engines = (self.nc.sync, self.nc.scalar, self.nc.vector, self.nc.tensor)
        for n, sem in enumerate(self.used):
            engines[n % len(engines)].sem_inc(sem, 1)
        self.nc.all_engine_barrier()

    def end_stage(self):
        self.nc.clear_and_free_semaphores(self.used)
        self.nc.all_engine_barrier()
        self.used = []

    def sems(self, name, n):
        return [self.sem(f"{name}{i}") for i in range(n)]


def refined_rsqrt(chain, dve, out, root, square_sum, tmp, scale):
    chain(dve.tensor_scalar(square_sum, square_sum, scale, EPS, ALU.mult, ALU.add))
    chain(dve.reciprocal(out, root))
    chain(dve.tensor_tensor(tmp, out, out, ALU.mult))
    chain(dve.tensor_tensor(tmp, tmp, square_sum, ALU.mult))
    chain(dve.tensor_scalar(tmp, tmp, -0.5, 1.5, ALU.mult, ALU.add))
    chain(dve.tensor_tensor(out, out, tmp, ALU.mult))


def load_constants(nc, k, io, w8):
    with ExitStack() as st:
        rows = [k.sb(f"rows{n}", [P, P], ctx=st) for n in range(2)]
        x_in, rows_in, w8_in = k.sem("x_in"), k.sem("rows_in"), k.sem("w8_in")
        ident_zero, ident_done = k.sem("ident_zero"), k.sem("ident_done")
        masks_done = k.sem("masks_done")
        turned, cols_done = k.sem("rows_turned"), k.sem("cols_done")
        na = COLS_A
        nb = NCOLS - na
        with nc.Block() as block:
            @block.sync
            def _(sp):
                sp.dma_start(w8[:, :, :], io["w_in"][0].rearrange("(c p) n -> p c n", p=P)[:, :, PROJ * P:PROJ * P + BA]
                             ).then_inc(w8_in, 16)
                sp.dma_start(k.xh[:, :, :], io["x"][0].rearrange("(t p) d -> p t d", p=P)).then_inc(x_in, 16)
                for name, src in (("norm_pre", io["norm_pre_w"]), ("norm1", io["norm1_g_2"]), ("norm2", io["norm2_g_2"]),
                                  ("conv", io["conv_w"].rearrange("a k c -> a (k c)")),
                                  ("conv_a", io["conv_a_w_2"].rearrange("a k c -> a (k c)")),
                                  ("conv_a_b", io["conv_a_b_2"]), ("b_a", io["b_a_2"]), ("b_x", io["b_x_2"]),
                                  ("conv_b", io["conv_b_w_2"].rearrange("a k c -> a (k c)")), ("lam", io["lru_lambda_2"])):
                    r0, n = COLS[name]
                    tile, r0 = (rows[0], r0) if r0 < na else (rows[1], r0 - na)
                    sp.dma_start(tile[r0:r0 + n, :], src.rearrange("a (c p) -> (a c) p", p=P)).then_inc(rows_in, 16)

            @block.gpsimd
            def _(pool):
                pool.memset(k.ident[:, :], 0.0).then_inc(ident_zero, 1)
                pool.wait_ge(ident_zero, 1)
                pool.affine_select(out=k.ident[:, :], in_=k.ident[:, :], compare_op=ALU.not_equal, fill=1.0,
                                   base=0, pattern=[[-1, P]], channel_multiplier=1).then_inc(ident_done, 1)
                order = Chain(pool, masks_done)
                order(pool.iota(k.row[:, :], [[1, NKEYS]], base=0, channel_multiplier=0,
                                allow_small_or_imprecise_dtypes=True))

            @block.vector
            def _(dve):
                dve.memset(k.eps[:, :], EPS)
                dve.memset(k.ones[:, :], 1.0)
                for n, scale in ((0, P ** -0.5), (1, 1.0)):
                    dve.memset(k.qk_scale[:, 2 * n:2 * n + 2], scale)
                dve.wait_ge(turned, 2)
                dve.tensor_copy(k.cols[:, 0:na], k.ps[0][:, 0:na]).then_inc(cols_done, 1)
                dve.tensor_copy(k.cols[:, na:NCOLS], k.ps[1][:, 0:nb]).then_inc(cols_done, 1)

            @block.tensor
            def _(pe):
                pe.wait_ge(ident_done, 1)
                pe.wait_ge(rows_in, 160)
                pe.transpose(k.ps[0][:, 0:na], rows[0][0:na, :], k.ident[0:na, 0:na]).then_inc(turned, 1)
                pe.transpose(k.ps[1][:, 0:nb], rows[1][0:nb, :], k.ident[0:nb, 0:nb]).then_inc(turned, 1)

            @block.scalar
            def _(act):
                act.wait_ge(x_in, 16)
                act.wait_ge(w8_in, 16)


def norm_and_turn(nc, k, tag, out, weight):
    with ExitStack() as st:
        xs = k.sb(f"{tag}_xs", [P, TT, D], ctx=st)
        stat = k.sb(f"{tag}_stat", [P, 4 * TT], ctx=st)
        norm = NormAndTurn(nc, k, tag, out, weight, [xs[:, t, :] for t in range(TT)], stat)
        with nc.Block() as block:
            @block.scalar
            def _(act):
                norm.squares(act)
                norm.highs(act)

            @block.vector
            def _(dve):
                norm.scale(dve)
                norm.lows(dve)

            @block.tensor
            def _(pe):
                norm.tensor(pe)


class NormAndTurn:

    def __init__(self, nc, k, tag, out, weight, xs, stat):
        self.k, self.out, self.w0, self.xs, self.stat = k, out, COLS[weight][0], xs, stat
        self.vec, self.sq, self.root, self.scaled, self.turned, self.his, self.los = (
            k.sem(f"{tag}_{n}") for n in ("vec", "sq", "root", "scaled", "turned", "hi", "lo"))

    def squares(self, act):
        k, stat = self.k, self.stat
        for t in range(TT):
            act.activation(self.xs[t], k.xh[:, t, :], ACT.Square, accum_out=stat[:, t:t + 1]).then_inc(self.sq, 1)
        act.wait_ge(self.sq, TT)
        act.activation(stat[:, TT:2 * TT], stat[:, 0:TT], ACT.Sqrt, scale=1.0 / D, bias=k.eps[:, 0:1]).then_inc(self.root, 1)

    def highs(self, act):
        k = self.k
        for c in range(DC):
            act.wait_ge(self.turned, c + 1)
            act.activation(self.out[0][:, c, :], k.ps[c][:, :], ACT.Copy, scale=k.cols[:, self.w0 + c:self.w0 + c + 1]
                           ).then_inc(self.his, 1)

    def scale(self, dve):
        k, stat = self.k, self.stat
        dve.wait_ge(self.root, 1)
        refined_rsqrt(Chain(dve, self.vec), dve, stat[:, 2 * TT:3 * TT], stat[:, TT:2 * TT], stat[:, 0:TT],
                      stat[:, 3 * TT:4 * TT], 1.0 / D)
        for t in range(TT):
            dve.tensor_scalar(self.xs[t], k.xh[:, t, :], stat[:, 2 * TT + t:2 * TT + t + 1], None, ALU.mult
                              ).then_inc(self.scaled, 1)

    def lows(self, dve):
        k = self.k
        hi, lo = self.out
        for c in range(DC):
            dve.wait_ge(self.his, c + 1)
            dve.scalar_tensor_tensor(out=lo[:, c, :], in0=k.ps[c][:, :], scalar=k.cols[:, self.w0 + c:self.w0 + c + 1],
                                     in1=hi[:, c, :].bitcast(F32), op0=ALU.mult, op1=ALU.subtract).then_inc(self.los, 1)

    def tensor(self, pe):
        k = self.k
        pe.wait_ge(self.scaled, TT)
        for c in range(DC):
            for t in range(TT):
                mm = pe.transpose(k.ps[c][:, t * P:(t + 1) * P], self.xs[t][:, c * P:(c + 1) * P], k.ident[:, :])
            mm.then_inc(self.turned, 1)
        pe.wait_ge(self.los, DC)


def project_first(nc, k, io, src, w8, proj, gates):
    hi, lo = src
    beta, g = gates
    w_dram = io["w_in"][0].rearrange("(c p) n -> p c n", p=P)
    w0, n_ch = COLS["conv"][0], 3 * G_HEADS
    per, sections = SEC // P, 2
    step = per * sections
    steps = PROJ // step
    pairs, unit_pairs = n_ch // 2, G_HEADS
    with ExitStack() as st:
        raw = [k.sb(f"p_raw{b}", [P, DC, SEC], ctx=st) for b in range(sections)]
        whi = [k.sb(f"p_whi{b}", [P, DC, SEC], F32R, ctx=st) for b in range(sections)]
        wlo = [k.sb(f"p_wlo{b}", [P, DC, SEC], F32R, ctx=st) for b in range(sections)]
        w8h, w8l = (k.sb(f"p_w8{n}", [P, DC, BA], F32R, ctx=st) for n in "hl")
        ba_t = k.sb("p_ba_t", [BA, T], ctx=st)
        ba = k.sb("p_ba", [P, TT, BA], ctx=st)
        bias = k.sb("p_bias", [P, 2, G_HEADS], ctx=st)
        z = k.sb("p_z", [P, 3, TT, G_HEADS], ctx=st)
        acc, sq, root = ([k.sb(f"p_{n}{b}", [P, T], ctx=st) for b in range(2)] for n in ("acc", "sq", "root"))
        raw_in, w_hi, w_lo = (k.sems(f"p_{n}", sections) for n in ("raw_in", "w_hi", "w_lo"))
        product, kept = k.sems("p_product", step), k.sems("p_kept", step)
        acc_done, silu_done, squared, summed, rooted, unit = (
            k.sems(f"p_{n}", 2) for n in ("acc_done", "silu_done", "squared", "summed", "rooted", "unit"))
        vec, w8_split, w8_product, ba_kept, bias_in, z_made, z_act, decay_rate, gates_done, masks = (
            k.sem(f"p_{n}") for n in ("vec", "w8_split", "w8_product", "ba_kept", "bias_in", "z_made", "z_act",
                                      "decay_rate", "gates_done", "masks"))
        chunk = lambda i: (i * step + DQ0) % PROJ

        def steps_of(eng, body):
            body(0, False, False, False)
            body(1, True, True, False)
            with eng.Fori(2, 2 + unit_pairs) as i:
                body(i, True, True, True)
            for i in range(2 + unit_pairs, steps):
                body(i, i <= pairs, False, False)

        stat = k.sb("p_stat", [P, 4 * TT], ctx=st)
        k.credit()
        late = proj[:, Q0:Q0 + DC, :].rearrange("p (t a) n -> p t (a n)", t=TT)
        norm = NormAndTurn(nc, k, "p_norm", src, "norm_pre", [late[:, t, :] for t in range(TT)], stat)
        with nc.Block() as block:
            @block.sync
            def _(sp):
                def load(i, b):
                    sp.dma_start(raw[b][:, :, :], w_dram[:, :, bass.ds(chunk(i) * P + b * SEC, SEC)]).then_inc(raw_in[b], 16)
                for b in range(sections):
                    load(0, b)
                for n, name in enumerate(("a_log", "dt_bias")):
                    sp.dma_start(bias[:, n, :], io[name][0].partition_broadcast(P)).then_inc(bias_in, 16)
                with sp.Fori(1, steps) as i:
                    for b in range(sections):
                        sp.wait_ge(w_lo[b], after(i))
                        load(i, b)

            @block.gpsimd
            def _(pool):
                order = Chain(pool, masks, done=1)
                order(pool.memset(k.upto[:, :], 1.0))
                order(pool.affine_select(out=k.upto[:, :], in_=k.upto[:, :], compare_op=ALU.is_ge, fill=0.0,
                                         base=0, pattern=[[1, P]], channel_multiplier=-1))
                order(pool.memset(k.later[:, :], 0.0))
                order(pool.affine_select(out=k.later[:, :], in_=k.later[:, :], compare_op=ALU.is_ge, fill=NEG,
                                         base=0, pattern=[[1, P]], channel_multiplier=-1))
                order(pool.memset(k.level[:, :, :], 1.0))
                for lv in range(LEVELS):
                    half = 1 << lv
                    m = k.level[:, lv, :].rearrange("p (n s) -> p n s", s=2 * half)
                    n = P // (2 * half)
                    for base, steps, cm in ((0, [-2 * half, 0], 1), (half - 1, [2 * half, 0], -1), (-half, [0, 1], 0)):
                        order(pool.affine_select(out=m, in_=m, compare_op=ALU.is_ge, fill=0.0, base=base,
                                                 pattern=[[steps[0], n], [steps[1], 2 * half]], channel_multiplier=cm))

            @block.tensor
            def _(pe):
                norm.tensor(pe)
                pe.wait_ge(w8_split, after(2))
                for c in range(DC):
                    for w, x in ((w8h, hi), (w8h, lo), (w8l, hi)):
                        mm = pe.matmul(k.ps[4][0:BA, :], w[:, c, :], x[:, c, :], start=(c == 0 and w is w8h and x is hi),
                                       stop=(c == DC - 1 and w is w8l))
                mm.then_inc(w8_product, 1)

                def turn_gates():
                    pe.wait_ge(ba_kept, after(1))
                    for t in range(TT):
                        mm = pe.transpose(k.ps[5][:, t * BA:(t + 1) * BA], ba_t[:, t * P:(t + 1) * P], k.ident[0:BA, 0:BA])
                    mm.then_inc(w8_product, 1)

                def body(i, convolved, square, scaled):
                    for n in range(step):
                        b, j = n // per, n % per
                        if j == 0:
                            pe.wait_ge(w_lo[b], after(i + 1))
                        pe.wait_ge(kept[n], after(i))
                        for c in range(DC):
                            for w, x in ((whi, hi), (whi, lo), (wlo, hi)):
                                mm = pe.matmul(k.ps[n][:, :], w[b][:, c, j * P:(j + 1) * P], x[:, c, :],
                                               start=(c == 0 and w is whi and x is hi), stop=(c == DC - 1 and w is wlo))
                        mm.then_inc(product[n], 1)
                        if n == 0 and isinstance(i, int) and i == 0:
                            turn_gates()
                        if n == 0 and scaled:
                            for h in range(2):
                                pe.wait_ge(ba_kept, after(2))
                                pe.wait_ge(squared[h], after(i - 1))
                                pe.wait_ge(rooted[h], after(i - 2))
                                pe.matmul(k.ps[4 + h][:, :], k.ones[:, :], sq[h][:, :], start=True, stop=True).then_inc(summed[h], 1)
                steps_of(pe, body)

            @block.scalar
            def _(act):
                def high(i, b):
                    act.wait_ge(raw_in[b], after(i * 16 + 16))
                    act.activation(whi[b][:, :, :], raw[b][:, :, :], ACT.Copy).then_inc(w_hi[b], 1)
                norm.squares(act)
                for b in range(sections):
                    high(0, b)
                norm.highs(act)
                act.wait_ge(w8_product, after(1))
                act.activation(ba_t[:, :], k.ps[4][0:BA, :], ACT.Copy).then_inc(ba_kept, 1)
                act.wait_ge(w8_product, after(2))
                act.activation(ba[:, :, :], k.ps[5][:, 0:TT * BA].rearrange("p (t n) -> p t n", t=TT), ACT.Copy
                               ).then_inc(ba_kept, 1)
                act.wait_ge(ba_kept, after(2))
                act.activation(beta[:, :, :], ba[:, :, 0:G_HEADS], ACT.Sigmoid)
                act.wait_ge(z_made, after(TT))
                act.activation(z[:, 1, :, :], z[:, 0, :, :], ACT.Abs).then_inc(z_act, 1)
                act.wait_ge(z_act, after(1))
                act.activation(z[:, 1, :, :], z[:, 1, :, :], ACT.Exp, scale=-1.0).then_inc(z_act, 1)
                act.wait_ge(z_act, after(2))
                act.activation(z[:, 2, :, :], z[:, 1, :, :], ACT.Ln, bias=1.0).then_inc(z_act, 1)
                act.wait_ge(bias_in, after(32))
                act.activation(bias[:, 0, :], bias[:, 0, :], ACT.Exp).then_inc(decay_rate, 1)

                def body(i, convolved, square, scaled):
                    for n in range(step):
                        act.wait_ge(product[n], after(i + 1))
                        act.activation(proj[:, chunk(i) + n, :], k.ps[n][:, :], ACT.Copy).then_inc(kept[n], 1)
                        if n % per == per - 1 and not (isinstance(i, int) and i == steps - 1):
                            high(i + 1, n // per)
                        if n == 1 and scaled:
                            for h in range(2):
                                act.wait_ge(summed[h], after(i - 1))
                                act.wait_ge(unit[h], after(i * 2 - 4))
                                act.activation(root[h][:, :], k.ps[4 + h][:, :], ACT.Sqrt, bias=k.eps[:, 0:1]).then_inc(rooted[h], 1)
                    if convolved:
                        for h in range(2):
                            act.wait_ge(acc_done[h], after(i))
                            act.activation(proj[:, i * 2 + (DQ0 + h - 2), :], acc[h][:, :], ACT.Silu).then_inc(silu_done[h], 1)
                    if square:
                        for h in range(2):
                            act.wait_ge(silu_done[h], after(i))
                            act.wait_ge(summed[h], after(i - 1))
                            act.activation(sq[h][:, :], proj[:, (i - 1) * 2 + (DQ0 + h), :], ACT.Square).then_inc(squared[h], 1)
                steps_of(act, body)

            @block.vector
            def _(dve):
                dve.tensor_copy(w8h[:, :, :], w8[:, :, :]).then_inc(w8_split, 1)
                dve.wait_ge(w8_split, after(1))
                dve.tensor_tensor(w8l[:, :, :], w8[:, :, :], w8h[:, :, :].bitcast(F32), ALU.subtract).then_inc(w8_split, 1)

                def low(i, b):
                    dve.wait_ge(w_hi[b], after(i + 1))
                    dve.tensor_tensor(wlo[b][:, :, :], raw[b][:, :, :], whi[b][:, :, :].bitcast(F32),
                                      ALU.subtract).then_inc(w_lo[b], 1)

                def body(i, convolved, square, scaled):
                    low(i, 1)
                    if convolved:
                        chain = Chain(dve, vec, i - 1, 2 * (G_CONV - 1), done=1)
                        for n in range(step):
                            dve.wait_ge(kept[n], after(i))
                        for h in range(2):
                            dve.wait_ge(silu_done[h], after(i - 1))
                            x = lambda upto: proj[:, i * 2 + (DQ0 + h - 2), 0:upto]
                            tap = lambda j: k.cols[:, bass.ds(i * 2 + (w0 + j * n_ch + h - 2), 1)]
                            chain(dve.tensor_scalar(acc[h][:, :], x(T), tap(G_CONV - 1), None, ALU.mult))
                            for j in range(G_CONV - 2, -1, -1):
                                s = G_CONV - 1 - j
                                ins = dve.scalar_tensor_tensor(out=acc[h][:, s:T], in0=x(T - s), scalar=tap(j), in1=acc[h][:, s:T],
                                                               op0=ALU.mult, op1=ALU.add)
                                if j:
                                    chain(ins)
                                else:
                                    ins.then_inc(acc_done[h], 1)
                        chain.end()
                    if not (isinstance(i, int) and i == steps - 1):
                        low(i + 1, 0)
                    if scaled:
                        for h in range(2):
                            dve.wait_ge(rooted[h], after(i - 1))
                            y = proj[:, i * 2 + (DQ0 + h - 4), :]
                            dve.reciprocal(root[h][:, :], root[h][:, :]).then_inc(unit[h], 1)
                            dve.wait_ge(unit[h], after(i * 2 - 3))
                            dve.scalar_tensor_tensor(out=y, in0=y, scalar=k.qk_scale[:, bass.ds(i - 2, 1)], in1=root[h][:, :],
                                                     op0=ALU.mult, op1=ALU.mult).then_inc(unit[h], 1)

                norm.scale(dve)
                low(0, 0)
                low(0, 1)
                norm.lows(dve)
                for t in range(TT):
                    if t == 0:
                        dve.wait_ge(ba_kept, after(2))
                        dve.wait_ge(bias_in, after(32))
                    dve.tensor_tensor(z[:, 0, t, :], ba[:, t, G_HEADS:BA], bias[:, 1, :], ALU.add).then_inc(z_made, 1)
                order = Chain(dve, gates_done, done=1)
                dve.wait_ge(decay_rate, after(1))
                dve.wait_ge(z_act, after(3))
                order(dve.tensor_scalar(z[:, 0, :, :], z[:, 0, :, :], 0.0, None, ALU.max))
                order(dve.tensor_tensor(z[:, 0, :, :], z[:, 0, :, :], z[:, 2, :, :], ALU.add))
                for t in range(TT):
                    order(dve.scalar_tensor_tensor(out=g[:, t, :], in0=z[:, 0, t, :], scalar=-1.0, in1=bias[:, 0, :],
                                                   op0=ALU.mult, op1=ALU.mult))
                low(1, 0)
                body(1, True, True, False)
                with dve.Fori(2, 2 + unit_pairs) as i:
                    body(i, True, True, True)
                for i in range(2 + unit_pairs, steps):
                    body(i, i <= pairs, False, False)


def attention(nc, k, proj, mixed):
    with ExitStack() as st:
        vtok = k.sb("a_vtok", [P, TT, A_HEADS * A_DH], ctx=st)
        dist = k.sb("a_dist", [P, T], ctx=st)
        slopes = k.sb("a_slopes", [P, A_HEADS], ctx=st)
        qs = [k.sb(f"a_q{p}", [P, T], ctx=st) for p in range(2)]
        ks = [k.sb(f"a_k{p}", [P, T], ctx=st) for p in range(2)]
        logits = k.sb("a_logits", [P, 3, T], ctx=st)
        probs = k.sb("a_probs", [P, 3, T], ctx=st)
        probs_t = k.sb("a_probs_t", [P, 2, T], ctx=st)
        stat = k.sb("a_stat", [P, 4, 4 * TT], ctx=st)
        steps = [(p, b, qt) for p in range(2) for b in range(2) for qt in range(TT)]
        n_steps = len(steps)
        score_bank = [k.ps[0], k.ps[1], k.ps[6]]

        def before(i, n, depth):
            return after(i * n_steps + max(n - depth + 1, 0))

        dist_made, v_turned, v_kept, slopes_made = (k.sem(f"a_{n}") for n in ("dist_made", "v_turned", "v_kept", "slopes_made"))
        pair_ready, scored, logits_made, max_neg, exped, turned, kept_t, weighted, normed, vec = (
            k.sem(f"a_{n}") for n in ("pair_ready", "scored", "logits_made", "max_neg", "exped", "turned", "kept_t",
                                      "weighted", "normed", "vec"))
        k.credit()
        with nc.Block() as block:
            @block.gpsimd
            def _(pool):
                pool.iota(dist[:, :], [[1, T]], base=-(T - P), channel_multiplier=-1,
                          allow_small_or_imprecise_dtypes=True).then_inc(dist_made, 1)
                pool.wait_ge(dist_made, after(1))
                pool.affine_select(out=dist[:, :], in_=dist[:, :], compare_op=ALU.is_ge, fill=NEG, base=T - P,
                                   pattern=[[-1, T]], channel_multiplier=1).then_inc(dist_made, 1)

            @block.tensor
            def _(pe):
                for t in range(TT):
                    for j in range(4):
                        mm = pe.transpose(k.ps[t][:, j * P:(j + 1) * P], proj[:, V0 + j, t * P:(t + 1) * P], k.ident[:, :])
                    mm.then_inc(v_turned, 1)
                pe.wait_ge(v_kept, after(TT))

                def score(i, n):
                    p, b, qt = steps[n]
                    pe.wait_ge(logits_made, before(i, n, 3))
                    if b == 0 and qt == 0:
                        pe.wait_ge(pair_ready, after(i * 4 + 2 * p + 2))
                    h = slice(b * A_DH, (b + 1) * A_DH)
                    w = (qt + 1) * P
                    pe.matmul(score_bank[n % 3][:, 0:w], qs[p][h, qt * P:w], ks[p][h, 0:w], start=True, stop=True).then_inc(scored, 1)

                def turn(i, n):
                    p, b, qt = steps[n]
                    pe.wait_ge(exped, after(i * n_steps + n + 1))
                    pe.wait_ge(kept_t, before(i, n, 2))
                    for kt in range(qt + 1):
                        mm = pe.transpose(k.ps[2 + n % 2][:, kt * P:(kt + 1) * P], probs[:, n % 3, kt * P:(kt + 1) * P], k.ident[:, :])
                    mm.then_inc(turned, 1)

                def weigh(i, n):
                    p, b, qt = steps[n]
                    pe.wait_ge(kept_t, after(i * n_steps + n + 1))
                    pe.wait_ge(normed, before(i, n, 2))
                    for kt in range(qt + 1):
                        mm = pe.matmul(k.ps[4 + n % 2][:, 0:A_DH], probs_t[:, n % 2, kt * P:(kt + 1) * P],
                                       vtok[:, kt, bass.ds(i * (2 * P) + p * P + b * A_DH, A_DH)], start=(kt == 0), stop=(kt == qt))
                    mm.then_inc(weighted, 1)

                with pe.Fori(0, A_HEADS // 4) as i:
                    score(i, 0)
                    score(i, 1)
                    turn(i, 0)
                    for n in range(n_steps):
                        if n + 2 < n_steps:
                            score(i, n + 2)
                        if n + 1 < n_steps:
                            turn(i, n + 1)
                        weigh(i, n)

            @block.vector
            def _(dve):
                for h in range(A_HEADS):
                    ins = dve.memset(slopes[:, h:h + 1], 2.0 ** -(h + 1))
                ins.then_inc(slopes_made, 1)
                dve.wait_ge(slopes_made, after(1))
                dve.wait_ge(dist_made, after(2))
                for t in range(TT):
                    dve.wait_ge(v_turned, after(t + 1))
                    dve.tensor_copy(vtok[:, t, :], k.ps[t][:, :]).then_inc(v_kept, 1)

                def normalise(i, n):
                    p, b, qt = steps[n]
                    dve.wait_ge(exped, after(i * n_steps + n + 1))
                    dve.wait_ge(weighted, after(i * n_steps + n + 1))
                    chain(dve.reciprocal(stat[:, 3, n:n + 1], stat[:, 2, n:n + 1]))
                    dve.tensor_scalar(mixed[:, qt, bass.ds(i * (2 * P) + p * P + b * A_DH, A_DH)], k.ps[4 + n % 2][:, 0:A_DH],
                                      stat[:, 3, n:n + 1], None, ALU.mult).then_inc(normed, 1)

                with dve.Fori(0, A_HEADS // 4) as i:
                    chain = Chain(dve, vec, i, 2 * n_steps, done=1)
                    dve.wait_ge(scored, after(i * n_steps))
                    for p in range(2):
                        dve.tensor_scalar(qs[p][:, :], proj[:, i * 2 + (Q0 + p), :], A_DH ** -0.5, None, ALU.mult
                                          ).then_inc(pair_ready, 1)
                        dve.tensor_copy(ks[p][:, :], proj[:, i * 2 + (K0 + p), :]).then_inc(pair_ready, 1)
                    for n, (p, b, qt) in enumerate(steps):
                        w = (qt + 1) * P
                        dve.wait_ge(scored, after(i * n_steps + n + 1))
                        dve.wait_ge(exped, before(i, n, 3))
                        dve.scalar_tensor_tensor(out=logits[:, n % 3, 0:w], in0=dist[:, T - w:T],
                                                 scalar=slopes[:, bass.ds(i * 4 + (2 * p + b), 1)], in1=score_bank[n % 3][:, 0:w],
                                                 op0=ALU.mult, op1=ALU.add).then_inc(logits_made, 1)
                        dve.wait_ge(logits_made, after(i * n_steps + n + 1))
                        chain(dve.tensor_reduce(stat[:, 0, n:n + 1], logits[:, n % 3, 0:w], AX_X, ALU.max))
                        dve.tensor_scalar(stat[:, 1, n:n + 1], stat[:, 0, n:n + 1], -1.0, None, ALU.mult).then_inc(max_neg, 1)
                        if n >= 2:
                            normalise(i, n - 2)
                    normalise(i, n_steps - 2)
                    normalise(i, n_steps - 1)
                    chain.end()

            @block.scalar
            def _(act):
                def keep(i, n):
                    w = (steps[n][2] + 1) * P
                    act.wait_ge(turned, after(i * n_steps + n + 1))
                    act.wait_ge(weighted, before(i, n, 2))
                    act.activation(probs_t[:, n % 2, 0:w], k.ps[2 + n % 2][:, 0:w], ACT.Copy).then_inc(kept_t, 1)

                with act.Fori(0, A_HEADS // 4) as i:
                    for n, (p, b, qt) in enumerate(steps):
                        w = (qt + 1) * P
                        act.wait_ge(max_neg, after(i * n_steps + n + 1))
                        act.wait_ge(turned, before(i, n, 3))
                        act.activation(probs[:, n % 3, 0:w], logits[:, n % 3, 0:w], ACT.Exp, bias=stat[:, 1, n:n + 1],
                                       accum_out=stat[:, 2, n:n + 1]).then_inc(exped, 1)
                        if n:
                            keep(i, n - 1)
                    keep(i, n_steps - 1)


def delta_prepare(nc, k, qkv, gates, kept):
    beta, g = gates
    H = G_HEADS
    heads = lambda ap: ap.rearrange("p (h n) -> p h n", h=H)
    with ExitStack() as st:
        two = lambda name: [k.sb(f"d_{name}{a}", [P, H, P], ctx=st) for a in range(2)]
        qst, kst, vst, dec, at, m, mt, x, tmp = (two(n) for n in ("q", "k", "v", "dec", "at", "m", "mt", "x", "tmp"))
        ot = [k.sb(f"d_ot{a}", [P, LEVELS, H, P], ctx=st) for a in range(2)]
        small = [k.sb(f"d_small{a}", [P, 4, H], ctx=st) for a in range(2)]
        gb = two("gb")
        names = ("staged", "gc_ready", "gc_kept", "diff", "decay", "rates", "kk_ready", "qk_ready", "at_done", "intra_done",
                 "k_turned", "k_kept", "v_turned", "v_kept", "ot_done", "mt_done", "m_turned", "m_done", "x_ready",
                 "x_kept", "dm_ready", "rate_diff")
        s = {n: k.sems(f"d_{n}", 2) for n in names}
        last = LEVELS - 1
        k.credit()
        with nc.Block() as block:
            @block.vector
            def _(dve):
                with dve.Fori(0, TT // 2) as i:
                    for a in range(2):
                        c = i * 2 + a
                        dve.wait_ge(s["v_turned"][a], after(i))
                        for n, dst in enumerate((qst, kst, vst)):
                            dve.tensor_copy(dst[a][:, :, :], qkv[:, n * H:(n + 1) * H, bass.ds(i * (2 * P) + a * P, P)]
                                            ).then_inc(s["staged"][a], 1)
                        for h in range(H):
                            dve.tensor_scalar(gb[a][:, h, :], k.ones[:, :], g[:, c, h:h + 1], None, ALU.mult
                                              ).then_inc(s["staged"][a], 1)
                    for a in range(2):
                        c = i * 2 + a
                        b0, b3 = heads(k.ps[4 * a][:, :]), k.ps[4 * a + 3]
                        dve.wait_ge(s["gc_ready"][a], after(i + 1))
                        dve.wait_ge(s["decay"][a], after(i))
                        dve.tensor_copy(small[a][:, 0, :], b3[:, 0:H]).then_inc(s["gc_kept"][a], 1)
                        dve.tensor_copy(small[a][:, 1, :], b0[:, :, P - 1]).then_inc(s["gc_kept"][a], 1)
                        dve.wait_ge(s["gc_kept"][a], after(i * 2 + 2))
                        dve.tensor_tensor(small[a][:, 2, :], small[a][:, 1, :], small[a][:, 0, :],
                                          ALU.subtract).then_inc(s["rate_diff"][a], 1)
                        for h in range(H):
                            dve.scalar_tensor_tensor(out=tmp[a][:, h, :], in0=b0[:, h, :], scalar=small[a][:, 0, h:h + 1],
                                                     in1=k.later[:, :], op0=ALU.subtract, op1=ALU.add).then_inc(s["diff"][a], 1)
                    for a in range(2):
                        c = i * 2 + a
                        b1, b2 = heads(k.ps[4 * a + 1][:, :]), heads(k.ps[4 * a + 2][:, :])
                        dve.wait_ge(s["kk_ready"][a], after(i + 1))
                        dve.wait_ge(s["decay"][a], after(i + 1))
                        dve.wait_ge(s["ot_done"][a], after(i * LEVELS))
                        for h in range(H):
                            dve.scalar_tensor_tensor(out=at[a][:, h, :], in0=b1[:, h, :], scalar=beta[:, c, h:h + 1],
                                                     in1=dec[a][:, h, :], op0=ALU.mult, op1=ALU.mult).then_inc(s["at_done"][a], 1)
                        dve.wait_ge(s["qk_ready"][a], after(i + 1))
                        dve.tensor_tensor(kept["intra"][:, c, :, :], b2, dec[a][:, :, :], ALU.mult).then_inc(s["intra_done"][a], 1)
                    for a in range(2):
                        dve.wait_ge(s["ot_done"][a], after(i * LEVELS + 1))
                        dve.wait_ge(s["dm_ready"][a], after(i * last))
                        for h in range(H):
                            dve.tensor_tensor(mt[a][:, h, :], k.ident[:, :], ot[a][:, 0, h, :], ALU.subtract
                                              ).then_inc(s["mt_done"][a], 1)
                    for lv in range(1, LEVELS):
                        for a in range(2):
                            c = i * 2 + a
                            b1, b2 = heads(k.ps[4 * a + 1][:, :]), heads(k.ps[4 * a + 2][:, :])
                            dve.wait_ge(s["dm_ready"][a], after(i * last + lv))
                            if lv < last:
                                dve.tensor_tensor(mt[a][:, :, :], mt[a][:, :, :], b2, ALU.subtract).then_inc(s["mt_done"][a], 1)
                                dve.wait_ge(s["m_done"][a], after(i * last + lv))
                                dve.tensor_tensor(m[a][:, :, :], m[a][:, :, :], b1, ALU.subtract).then_inc(s["m_done"][a], 1)
                            else:
                                dve.tensor_tensor(kept["inv"][:, c, :, :], mt[a][:, :, :], b2, ALU.subtract)

            MT = H + last - 1

            @block.gpsimd
            def _(pool):
                with pool.Fori(0, TT // 2) as i:
                    for lv in range(LEVELS):
                        for a in range(2):
                            if lv == 0:
                                pool.wait_ge(s["at_done"][a], after(i * H + H))
                                pool.wait_ge(s["dm_ready"][a], after(i * last))
                            for h in range(H):
                                ins = pool.tensor_tensor(ot[a][:, lv, h, :], at[a][:, h, :], k.level[:, lv, :], ALU.mult)
                            ins.then_inc(s["ot_done"][a], 1)

            @block.scalar
            def _(act):
                with act.Fori(0, TT // 2) as i:
                    for a in range(2):
                        c = i * 2 + a
                        act.wait_ge(s["diff"][a], after(i * H + H))
                        act.wait_ge(s["intra_done"][a], after(i))
                        act.activation(dec[a][:, :, :], tmp[a][:, :, :], ACT.Exp).then_inc(s["decay"][a], 1)
                        act.wait_ge(s["rate_diff"][a], after(i + 1))
                        act.activation(kept["rates"][:, c, 0, :], small[a][:, 0, :], ACT.Exp)
                        act.activation(kept["rates"][:, c, 1, :], small[a][:, 1, :], ACT.Exp)
                        act.activation(small[a][:, 3, :], small[a][:, 2, :], ACT.Exp).then_inc(s["rates"][a], 1)
                    for a in range(2):
                        c = i * 2 + a
                        b3 = heads(k.ps[4 * a + 3][:, :])
                        act.wait_ge(s["k_turned"][a], after(i + 1))
                        act.wait_ge(s["rates"][a], after(i + 1))
                        for h in range(H):
                            act.activation(kept["kdec"][:, c, h, :], b3[:, h, :], ACT.Copy,
                                           scale=small[a][:, 3, h:h + 1]).then_inc(s["k_kept"][a], 1)
                        act.wait_ge(s["v_turned"][a], after(i + 1))
                        act.activation(kept["v"][:, c, :, :], b3, ACT.Copy).then_inc(s["v_kept"][a], 1)
                    for a in range(2):
                        act.wait_ge(s["m_turned"][a], after(i + 1))
                        act.activation(m[a][:, :, :], heads(k.ps[4 * a][:, :]), ACT.Copy).then_inc(s["m_done"][a], 1)
                    for lv in range(1, LEVELS):
                        for a in range(2):
                            act.wait_ge(s["x_ready"][a], after(i * last + lv))
                            act.activation(x[a][:, :, :], heads(k.ps[4 * a][:, :]), ACT.Copy).then_inc(s["x_kept"][a], 1)

            @block.tensor
            def _(pe):
                with pe.Fori(0, TT // 2) as i:
                    for a in range(2):
                        c = i * 2 + a
                        b0, b3 = heads(k.ps[4 * a][:, :]), k.ps[4 * a + 3]
                        pe.wait_ge(s["v_kept"][a], after(i))
                        pe.wait_ge(s["x_kept"][a], after(i * last))
                        pe.matmul(b3[:, 0:H], k.upto[:, :], g[:, c, :], start=True, stop=True)
                        for h in range(H):
                            pe.wait_ge(s["staged"][a], after(i * (3 + H) + (3 + H)))
                            mm = pe.matmul(b0[:, h, :], gb[a][:, h, :], k.upto[:, :], start=True, stop=True)
                        mm.then_inc(s["gc_ready"][a], 1)
                    for a in range(2):
                        b1, b2, b3 = (heads(k.ps[4 * a + n][:, :]) for n in (1, 2, 3))
                        pe.wait_ge(s["m_done"][a], after(i * last))
                        for h in range(H):
                            mm = pe.matmul(b1[:, h, :], kst[a][:, h, :], kst[a][:, h, :], start=True, stop=True)
                        mm.then_inc(s["kk_ready"][a], 1)
                        for h in range(H):
                            mm = pe.matmul(b2[:, h, :], kst[a][:, h, :], qst[a][:, h, :], start=True, stop=True)
                        mm.then_inc(s["qk_ready"][a], 1)
                        pe.wait_ge(s["gc_kept"][a], after(i * 2 + 2))
                        for h in range(H):
                            mm = pe.transpose(b3[:, h, :], kst[a][:, h, :], k.ident[:, :])
                        mm.then_inc(s["k_turned"][a], 1)
                        pe.wait_ge(s["k_kept"][a], after(i * H + H))
                        for h in range(H):
                            mm = pe.transpose(b3[:, h, :], vst[a][:, h, :], k.ident[:, :])
                        mm.then_inc(s["v_turned"][a], 1)
                    for a in range(2):
                        b0 = heads(k.ps[4 * a][:, :])
                        pe.wait_ge(s["mt_done"][a], after(i * MT + H))
                        pe.wait_ge(s["diff"][a], after(i * H + H))
                        for h in range(H):
                            mm = pe.transpose(b0[:, h, :], mt[a][:, h, :], k.ident[:, :])
                        mm.then_inc(s["m_turned"][a], 1)
                    for lv in range(1, LEVELS):
                        for a in range(2):
                            b0 = heads(k.ps[4 * a][:, :])
                            pe.wait_ge(s["m_done"][a], after(i * last + lv))
                            pe.wait_ge(s["ot_done"][a], after(i * LEVELS + lv + 1))
                            for h in range(H):
                                mm = pe.matmul(b0[:, h, :], ot[a][:, lv, h, :], m[a][:, h, :], start=True, stop=True)
                            mm.then_inc(s["x_ready"][a], 1)
                        for a in range(2):
                            b1, b2 = (heads(k.ps[4 * a + n][:, :]) for n in (1, 2))
                            pe.wait_ge(s["x_kept"][a], after(i * last + lv))
                            pe.wait_ge(s["mt_done"][a], after(i * MT + (H + lv - 1)))
                            if lv == 1:
                                pe.wait_ge(s["at_done"][a], after(i * H + H))
                                pe.wait_ge(s["intra_done"][a], after(i + 1))
                            for h in range(H):
                                if lv < last:
                                    pe.matmul(b1[:, h, :], mt[a][:, h, :], x[a][:, h, :], start=True, stop=True)
                                mm = pe.matmul(b2[:, h, :], x[a][:, h, :], mt[a][:, h, :], start=True, stop=True)
                            mm.then_inc(s["dm_ready"][a], 1)


def delta_scan(nc, k, gates, kept, qkv, o):
    beta, _ = gates
    H = G_HEADS
    heads = lambda ap: ap.rearrange("p (h n) -> p h n", h=H)
    with ExitStack() as st:
        S = k.sb("s_S", [P, H, P], ctx=st)
        z, vn = (k.sb(f"s_{n}", [P, H, P], ctx=st) for n in ("z", "vn"))
        neg = k.sb("s_neg", [P, TT, H], ctx=st)
        ks, qs, tz, intra, upd, z_done, vn_done, o_kept, o_done, s_done, neg_done = (
            k.sem(f"s_{n}") for n in ("ks", "qs", "tz", "intra", "upd", "z_done", "vn_done", "o_kept", "o_done", "s_done", "neg_done"))
        b = [heads(k.ps[n][:, :]) for n in range(5)]
        with nc.Block() as block:
            @block.tensor
            def _(pe):
                for c in range(TT):
                    tok = slice(c * P, (c + 1) * P)
                    if c:
                        pe.wait_ge(s_done, 1 + c * H)
                        for h in range(H):
                            mm = pe.matmul(b[0][:, h, :], qkv[:, H + h, tok], S[:, h, :], start=True, stop=True)
                        mm.then_inc(ks, 1)
                        pe.wait_ge(o_done, c * H - H)
                        for h in range(H):
                            mm = pe.matmul(b[1][:, h, :], qkv[:, h, tok], S[:, h, :], start=True, stop=True)
                        mm.then_inc(qs, 1)
                        pe.wait_ge(z_done, c * H)
                    for h in range(H):
                        src = z[:, h, :] if c else kept["v"][:, 0, h, :]
                        mm = pe.matmul(b[2][:, h, :], kept["inv"][:, c, h, :], src, start=True, stop=True)
                    mm.then_inc(tz, 1)
                    pe.wait_ge(vn_done, (c + 1) * H)
                    if c < TT - 1:
                        for h in range(H):
                            mm = pe.matmul(b[4][:, h, :], kept["kdec"][:, c, h, :], vn[:, h, :], start=True, stop=True)
                        mm.then_inc(upd, 1)
                    if c:
                        pe.wait_ge(o_kept, c)
                    for h in range(H):
                        mm = pe.matmul(b[3][:, h, :], kept["intra"][:, c, h, :], vn[:, h, :], start=True, stop=True)
                    mm.then_inc(intra, 1)

            @block.vector
            def _(dve):
                dve.memset(S[:, :, :], 0.0).then_inc(s_done, 1)
                dve.tensor_scalar(neg[:, :, :], kept["rates"][:, :, 0, :], -1.0, None, ALU.mult).then_inc(neg_done, 1)
                dve.wait_ge(neg_done, 1)
                dve.wait_ge(s_done, 1)
                for c in range(TT):
                    if c:
                        dve.wait_ge(ks, c)
                        dve.wait_ge(tz, c)
                        for h in range(H):
                            dve.scalar_tensor_tensor(out=z[:, h, :], in0=b[0][:, h, :], scalar=neg[:, c, h:h + 1],
                                                     in1=kept["v"][:, c, h, :], op0=ALU.mult, op1=ALU.add).then_inc(z_done, 1)
                    dve.wait_ge(tz, c + 1)
                    if c:
                        dve.wait_ge(intra, c)
                    for h in range(H):
                        dve.tensor_scalar(vn[:, h, :], b[2][:, h, :], beta[:, c, h:h + 1], None, ALU.mult).then_inc(vn_done, 1)
                    if c < TT - 1:
                        dve.wait_ge(upd, c + 1)
                        if c:
                            dve.wait_ge(qs, c)
                        for h in range(H):
                            dve.scalar_tensor_tensor(out=S[:, h, :], in0=S[:, h, :], scalar=kept["rates"][:, c, 1, h:h + 1],
                                                     in1=b[4][:, h, :], op0=ALU.mult, op1=ALU.add).then_inc(s_done, 1)
                    if c:
                        dve.wait_ge(o_kept, c + 1)
                        for h in range(H):
                            dve.scalar_tensor_tensor(out=o[:, c, h * P:(h + 1) * P], in0=b[1][:, h, :],
                                                     scalar=kept["rates"][:, c, 0, h:h + 1], in1=o[:, c, h * P:(h + 1) * P],
                                                     op0=ALU.mult, op1=ALU.add).then_inc(o_done, 1)

            @block.scalar
            def _(act):
                for c in range(TT):
                    act.wait_ge(intra, c + 1)
                    act.activation(o[:, c, :], k.ps[3][:, :], ACT.Copy).then_inc(o_kept, 1)


def gate_and_turn(nc, k, io, mixed, proj, out):
    hi, lo = out
    H, half = G_HEADS, A_HEADS * A_DH
    with ExitStack() as st:
        sq = k.sb("m_sq", [P, TT, H, P], ctx=st)
        stat = k.sb("m_stat", [P, 4, TT * H], ctx=st)
        norm_w = k.sb("m_norm_w", [P, 1], ctx=st)
        m32 = k.sb("m_m32", [P, 2, T], ctx=st)
        names = ("w_in", "sq_done", "summed", "rooted", "vec", "scaled", "gated", "turned", "m32_done", "hi_done", "lo_done")
        s = {n: k.sem(f"m_{n}") for n in names}
        with nc.Block() as block:
            @block.sync
            def _(sp):
                sp.dma_start(norm_w[:, :], io["gdn_norm_w"].rearrange("a p -> p a")).then_inc(s["w_in"], 16)

            @block.scalar
            def _(act):
                for t in range(TT):
                    act.activation(sq[:, t, :, :].rearrange("p h n -> p (h n)"), mixed[:, t, half:D], ACT.Square
                                   ).then_inc(s["sq_done"], 1)
                act.wait_ge(s["summed"], TT)
                act.activation(stat[:, 1, :], stat[:, 0, :], ACT.Sqrt, scale=1.0 / P, bias=k.eps[:, 0:1]).then_inc(s["rooted"], 1)
                for z in (Z0, DZ0):
                    for c in range(4):
                        act.activation(proj[:, z + c, :], proj[:, z + c, :], ACT.Silu).then_inc(s["gated"], 1)
                for c in range(DC):
                    act.wait_ge(s["m32_done"], c + 1)
                    act.activation(hi[:, c, :], m32[:, c % 2, :], ACT.Copy).then_inc(s["hi_done"], 1)

            @block.vector
            def _(dve):
                for t in range(TT):
                    dve.wait_ge(s["sq_done"], t + 1)
                    dve.tensor_reduce(stat[:, 0, t * H:(t + 1) * H], sq[:, t, :, :], AX_X, ALU.add).then_inc(s["summed"], 1)
                dve.wait_ge(s["rooted"], 1)
                refined_rsqrt(Chain(dve, s["vec"]), dve, stat[:, 2, :], stat[:, 1, :], stat[:, 0, :], stat[:, 3, :], 1.0 / P)
                for t in range(TT):
                    for h in range(H):
                        v = mixed[:, t, half + h * P:half + (h + 1) * P]
                        dve.tensor_scalar(v, v, stat[:, 2, t * H + h:t * H + h + 1], None, ALU.mult).then_inc(s["scaled"], 1)
                dve.wait_ge(s["w_in"], 16)
                for c in range(DC):
                    z = Z0 + c if c < 4 else DZ0 + c - 4
                    dve.wait_ge(s["turned"], c + 1)
                    dve.wait_ge(s["gated"], c + 1)
                    if c >= 2:
                        dve.wait_ge(s["lo_done"], c - 1)
                    dve.scalar_tensor_tensor(out=m32[:, c % 2, :], in0=k.ps[c][:, :], scalar=1.0 if c < 4 else norm_w[:, 0:1],
                                             in1=proj[:, z, :], op0=ALU.mult, op1=ALU.mult).then_inc(s["m32_done"], 1)
                    dve.wait_ge(s["hi_done"], c + 1)
                    dve.tensor_tensor(lo[:, c, :], m32[:, c % 2, :], hi[:, c, :].bitcast(F32), ALU.subtract).then_inc(s["lo_done"], 1)

            @block.tensor
            def _(pe):
                for c in range(DC):
                    if c == DC // 2:
                        pe.wait_ge(s["scaled"], TT * H)
                    for t in range(TT):
                        mm = pe.transpose(k.ps[c][:, t * P:(t + 1) * P], mixed[:, t, c * P:(c + 1) * P], k.ident[:, :])
                    mm.then_inc(s["turned"], 1)


def project_out(nc, k, tag, weight, src, post=None):
    hi, lo = src
    with ExitStack() as st:
        raw, whi, wlo = ([k.sb(f"{tag}_{n}{b}", [P, D], dt, ctx=st) for b in range(2)]
                         for n, dt in (("raw", F32), ("whi", F32R), ("wlo", F32R)))
        raw_in, w_hi, w_lo = k.sems(f"{tag}_raw_in", 2), k.sems(f"{tag}_w_hi", 2), k.sems(f"{tag}_w_lo", 2)
        used, summed = k.sem(f"{tag}_used"), k.sem(f"{tag}_summed")
        if post is not None:
            stat = k.sb(f"{tag}_stat", [P, 5, TT], ctx=st)
            halves = k.sb(f"{tag}_halves", [P, TT, 2], ctx=st)
            post_w = k.sb(f"{tag}_post_w", [P, D], ctx=st)
            junk = k.sb(f"{tag}_junk", [P, 2, T], ctx=st)
            normed = k.sb(f"{tag}_normed", [P, 2, T], ctx=st)
            post_in, sq_done, sums_done, rooted, vec, normed_done, added = (
                k.sem(f"{tag}_{n}") for n in ("post_in", "sq_done", "sums_done", "rooted", "vec", "normed_done", "added"))
        with nc.Block() as block:
            @block.sync
            def _(sp):
                if post is not None:
                    sp.dma_start(post_w[:, :], post.partition_broadcast(P)).then_inc(post_in, 16)
                for c in range(DC):
                    if c >= 2:
                        sp.wait_ge(w_lo[c % 2], c // 2)
                    sp.dma_start(raw[c % 2][:, :], weight[c * P:(c + 1) * P, :]).then_inc(raw_in[c % 2], 16)

            @block.vector
            def _(dve):
                for c in range(DC):
                    b = c % 2
                    dve.wait_ge(raw_in[b], 16 * (c // 2 + 1))
                    if c >= 2:
                        dve.wait_ge(used, c - 1)
                    dve.tensor_copy(whi[b][:, :], raw[b][:, :]).then_inc(w_hi[b], 1)
                    dve.wait_ge(w_hi[b], c // 2 + 1)
                    dve.tensor_tensor(wlo[b][:, :], raw[b][:, :], whi[b][:, :].bitcast(F32), ALU.subtract).then_inc(w_lo[b], 1)
                if post is None:
                    for n in range(2 * TT):
                        t, f = n // 2, slice(n % 2 * T, n % 2 * T + T)
                        dve.wait_ge(summed, n + 1)
                        dve.tensor_tensor(k.xh[:, t, f], k.xh[:, t, f], k.ps[n][:, :], ALU.add)
                    return
                chain = Chain(dve, vec)
                dve.wait_ge(sq_done, 2 * TT)
                dve.tensor_tensor(stat[:, 0, :], halves[:, :, 0], halves[:, :, 1], ALU.add).then_inc(sums_done, 1)
                dve.wait_ge(rooted, 1)
                refined_rsqrt(chain, dve, stat[:, 2, :], stat[:, 1, :], stat[:, 0, :], stat[:, 3, :], 1.0 / D)
                dve.wait_ge(post_in, 16)
                for n in range(2 * TT):
                    t, f = n // 2, slice(n % 2 * T, n % 2 * T + T)
                    if n >= 2:
                        dve.wait_ge(added, n - 1)
                    dve.scalar_tensor_tensor(out=normed[:, n % 2, :], in0=k.ps[n][:, :], scalar=stat[:, 2, t:t + 1],
                                             in1=post_w[:, f], op0=ALU.mult, op1=ALU.mult).then_inc(normed_done, 1)
                    dve.wait_ge(normed_done, n + 1)
                    dve.tensor_tensor(k.xh[:, t, f], k.xh[:, t, f], normed[:, n % 2, :], ALU.add).then_inc(added, 1)

            @block.tensor
            def _(pe):
                for c in range(DC):
                    b = c % 2
                    pe.wait_ge(w_lo[b], c // 2 + 1)
                    for n in range(2 * TT):
                        t, f = n // 2, slice(n % 2 * T, n % 2 * T + T)
                        for x, w in ((hi, whi), (hi, wlo), (lo, whi)):
                            mm = pe.matmul(k.ps[n][:, :], x[:, c, t * P:(t + 1) * P], w[b][:, f],
                                           start=(c == 0 and x is hi and w is whi), stop=(c == DC - 1 and x is lo))
                        if c == DC - 1:
                            mm.then_inc(summed, 1)
                    if c < DC - 1:
                        mm.then_inc(used, 1)

            if post is not None:
                @block.scalar
                def _(act):
                    for n in range(2 * TT):
                        act.wait_ge(summed, n + 1)
                        if n >= 2:
                            act.wait_ge(sq_done, n - 1)
                        act.activation(junk[:, n % 2, :], k.ps[n][:, :], ACT.Square,
                                       accum_out=halves[:, n // 2, n % 2:n % 2 + 1]).then_inc(sq_done, 1)
                    act.wait_ge(sums_done, 1)
                    act.activation(stat[:, 1, :], stat[:, 0, :], ACT.Sqrt, scale=1.0 / D, bias=k.eps[:, 0:1]).then_inc(rooted, 1)


XA, VB, CB, BB, GA, MA, MB = range(7)
W_COLUMNS = {XA: 0, GA: 1, VB: 2, BB: 3, CB: 4, MA: 5, MB: 6}
ATANH_TERMS = 9


def mixers(nc, k, io, src, out):
    hi, lo = src
    mhi, mlo = out
    w_dram = io["w_in_2"][0].rearrange("(c p) n -> p c n", p=P)
    last = L_HEADS - 1
    with ExitStack() as st:
        raw, whi, wlo = ([k.sb(f"x_{n}{s}", [P, DC, P], dt, ctx=st) for s in range(7)]
                         for n, dt in (("raw", F32), ("whi", F32R), ("wlo", F32R)))
        w_gate = k.sb("x_w_gate", [P, 2, P], ctx=st)
        tile = lambda n: k.sb(f"x_{n}", [P, T], ctx=st)
        xc, r, ig, tau, den, e, a, mult, h, ge, vb, cv, yb, sa, sb_ = (
            tile(n) for n in ("xc", "r", "ig", "tau", "den", "e", "a", "mult", "h", "ge", "vb", "cv", "yb", "sa", "sb"))
        rate = k.sb("x_rate", [P, 4, L_HEADS], ctx=st)
        raw_in, w_hi, w_lo, product = (k.sems(f"x_{n}", 7) for n in ("raw_in", "w_hi", "w_lo", "product"))
        names = ("gate_in", "rate_act", "rate_done", "xc_done", "r_ready", "i_ready", "r_done", "i_done", "tau_done",
                 "sqrt_in", "mult_done", "vb_kept", "ge_done", "sa_done", "sb_done", "m_done", "hi_done", "lo_done", "vec")
        s = {n: k.sem(f"x_{n}") for n in names}
        lam0, nl = COLS["lam"]
        col = lambda name, i, j=0, per=L_HEADS: k.cols[:, bass.ds(i + (COLS[name][0] + j * per), 1)]
        VEC = 19

        k.credit()
        with nc.Block() as block:
            @block.sync
            def _(sp):
                def load(i, first):
                    for n in range(7):
                        if not first:
                            sp.wait_ge(w_lo[n], after(i))
                        sp.dma_start(raw[n][:, :, :], w_dram[:, :, bass.ds(i * P + W_COLUMNS[n] * D, P)]).then_inc(raw_in[n], 16)
                        if n == XA:
                            if not first:
                                sp.wait_ge(s["i_ready"], after(i))
                            for j, name in enumerate(("w_a_2", "w_x_2")):
                                sp.dma_start(w_gate[:, j, :], io[name][0, bass.ds(i, 1), :, :].rearrange("a i j -> (a i) j")
                                             ).then_inc(s["gate_in"], 16)
                load(0, True)
                with sp.Fori(1, L_HEADS) as i:
                    load(i, False)

            @block.vector
            def _(dve):
                def split(i, n, first=False):
                    dve.wait_ge(raw_in[n], after(i * 16 + 16))
                    if not first:
                        dve.wait_ge(product[n], after(i))
                    dve.tensor_copy(whi[n][:, :, :], raw[n][:, :, :]).then_inc(w_hi[n], 1)
                    dve.wait_ge(w_hi[n], after(i + 1))
                    dve.tensor_tensor(wlo[n][:, :, :], raw[n][:, :, :], whi[n][:, :, :].bitcast(F32), ALU.subtract).then_inc(w_lo[n], 1)

                for n in range(7):
                    split(0, n, True)
                order = Chain(dve, s["rate_done"], done=1)
                dve.wait_ge(s["rate_act"], after(2))
                order(dve.tensor_scalar(rate[:, 1, :], rate[:, 0, :], 2.0, None, ALU.add))
                order(dve.reciprocal(rate[:, 1, :], rate[:, 1, :]))
                order(dve.tensor_tensor(rate[:, 0, :], rate[:, 0, :], rate[:, 1, :], ALU.mult))
                order(dve.tensor_tensor(rate[:, 1, :], rate[:, 0, :], rate[:, 0, :], ALU.mult))
                order(dve.tensor_scalar(rate[:, 2, :], rate[:, 1, :], 1.0 / (2 * ATANH_TERMS - 1), 1.0 / (2 * ATANH_TERMS - 3), ALU.mult, ALU.add))
                for n in range(ATANH_TERMS - 3, -1, -1):
                    order(dve.tensor_tensor(rate[:, 2, :], rate[:, 2, :], rate[:, 1, :], ALU.mult))
                    order(dve.tensor_scalar(rate[:, 2, :], rate[:, 2, :], 1.0 / (2 * n + 1), None, ALU.add))
                order(dve.tensor_tensor(rate[:, 2, :], rate[:, 2, :], rate[:, 0, :], ALU.mult))
                order(dve.tensor_scalar(rate[:, 1, :], k.cols[:, lam0:lam0 + nl], -1.0, 0.0, ALU.mult, ALU.max))
                order(dve.tensor_scalar(rate[:, 2, :], rate[:, 2, :], -8.0, None, ALU.mult))
                order(dve.tensor_scalar(rate[:, 1, :], rate[:, 1, :], -4.0, None, ALU.mult))
                order(dve.tensor_tensor(rate[:, 3, :], rate[:, 2, :], rate[:, 1, :], ALU.add))
                rate_steps = order.n

                def head(i, more):
                    chain = Chain(dve, s["vec"], i, VEC, done=1)
                    nxt = (lambda n: split(i + 1, n)) if more else (lambda n: None)
                    dve.wait_ge(product[XA], after(i + 1))
                    dve.wait_ge(s["i_ready"], after(i))
                    p = k.ps[0]
                    chain(dve.tensor_scalar(xc[:, :], p[:, :], col("conv_a", i, 3), col("conv_a_b", i), ALU.mult, ALU.add))
                    for j in (2, 1, 0):
                        d = 3 - j
                        ins = dve.scalar_tensor_tensor(out=xc[:, d:T], in0=p[:, 0:T - d], scalar=col("conv_a", i, j),
                                                       in1=xc[:, d:T], op0=ALU.mult, op1=ALU.add)
                        if j:
                            chain(ins)
                        else:
                            ins.then_inc(s["xc_done"], 1)
                    nxt(XA)
                    dve.wait_ge(product[CB], after(i + 1))
                    dve.wait_ge(s["vb_kept"], after(i + 1))
                    chain(dve.tensor_tensor(cv[:, :], vb[:, :], k.ps[2][:, :], ALU.mult))
                    chain(dve.tensor_scalar(yb[:, :], cv[:, :], col("conv_b", i, 2), None, ALU.mult))
                    for j in (1, 0):
                        d = 2 - j
                        chain(dve.scalar_tensor_tensor(out=yb[:, d:T], in0=cv[:, 0:T - d], scalar=col("conv_b", i, j),
                                                       in1=yb[:, d:T], op0=ALU.mult, op1=ALU.add))
                    nxt(VB)
                    nxt(CB)
                    dve.wait_ge(product[BB], after(i + 1))
                    chain(dve.tensor_tensor(yb[:, :], yb[:, :], k.ps[3][:, :], ALU.mult))
                    nxt(BB)
                    dve.wait_ge(s["tau_done"], after(i + 1))
                    chain(dve.tensor_scalar(den[:, :], tau[:, :], -1.0, 1.0, ALU.mult, ALU.add))
                    chain(dve.reciprocal(den[:, :], den[:, :]))
                    chain(dve.scalar_tensor_tensor(out=e[:, :], in0=tau[:, :], scalar=2.0, in1=den[:, :], op0=ALU.mult, op1=ALU.mult))
                    dve.scalar_tensor_tensor(out=den[:, :], in0=e[:, :], scalar=2.0, in1=e[:, :], op0=ALU.add, op1=ALU.mult
                                             ).then_inc(s["sqrt_in"], 1)
                    chain(dve.tensor_scalar(a[:, :], e[:, :], 1.0, None, ALU.add))
                    dve.wait_ge(s["i_done"], after(i + 1))
                    chain(dve.tensor_tensor(ig[:, :], ig[:, :], xc[:, :], ALU.mult))
                    dve.wait_ge(s["mult_done"], after(i + 1))
                    chain(dve.tensor_tensor(ig[:, :], ig[:, :], mult[:, :], ALU.mult))
                    chain(dve.tensor_tensor_scan(h[:, :], a[:, :], ig[:, :], 0.0, ALU.mult, ALU.add))
                    nxt(GA)
                    dve.wait_ge(s["ge_done"], after(i + 1))
                    chain(dve.tensor_tensor(h[:, :], h[:, :], ge[:, :], ALU.mult))
                    dve.wait_ge(s["sa_done"], after(i + 1))
                    chain(dve.tensor_tensor(h[:, :], h[:, :], sa[:, :], ALU.mult))
                    nxt(MA)
                    if more:
                        nxt(MB)
                    dve.wait_ge(s["sb_done"], after(i + 1))
                    chain(dve.tensor_tensor(yb[:, :], yb[:, :], sb_[:, :], ALU.mult))
                    dve.tensor_tensor(h[:, :], h[:, :], yb[:, :], ALU.add).then_inc(s["m_done"], 1)
                    dve.wait_ge(s["hi_done"], after(i + 1))
                    chain(dve.tensor_tensor(mlo[:, i, :], h[:, :], mhi[:, i, :].bitcast(F32), ALU.subtract))
                    assert chain.n == VEC, chain.n

                with dve.Fori(0, last) as i:
                    head(i, True)
                head(last, False)

            @block.tensor
            def _(pe):
                def section(i, n):
                    pe.wait_ge(w_lo[n], after(i + 1))
                    for c in range(DC):
                        for w, x in ((whi, hi), (whi, lo), (wlo, hi)):
                            mm = pe.matmul(k.ps[n][:, :], w[n][:, c, :], x[:, c, :], start=(c == 0 and w is whi and x is hi),
                                           stop=(c == DC - 1 and w is wlo))
                    mm.then_inc(product[n], 1)

                with pe.Fori(0, L_HEADS) as i:
                    pe.wait_ge(s["i_done"], after(i))
                    section(i, XA)
                    pe.wait_ge(s["vb_kept"], after(i))
                    section(i, VB)
                    pe.wait_ge(s["m_done"], after(i))
                    section(i, CB)
                    section(i, BB)
                    pe.wait_ge(s["gate_in"], after(i * 32 + 32))
                    pe.wait_ge(s["xc_done"], after(i + 1))
                    pe.wait_ge(s["r_done"], after(i))
                    pe.matmul(k.ps[7][:, :], w_gate[:, 0, :], xc[:, :], start=True, stop=True).then_inc(s["r_ready"], 1)
                    pe.matmul(k.ps[0][:, :], w_gate[:, 1, :], xc[:, :], start=True, stop=True).then_inc(s["i_ready"], 1)
                    pe.wait_ge(s["ge_done"], after(i))
                    section(i, GA)
                    pe.wait_ge(s["sa_done"], after(i))
                    section(i, MA)
                    pe.wait_ge(s["sb_done"], after(i))
                    section(i, MB)

            @block.scalar
            def _(act):
                act.activation(rate[:, 3, :], k.cols[:, lam0:lam0 + nl], ACT.Abs).then_inc(s["rate_act"], 1)
                act.wait_ge(s["rate_act"], after(1))
                act.activation(rate[:, 0, :], rate[:, 3, :], ACT.Exp, scale=-1.0).then_inc(s["rate_act"], 1)
                act.wait_ge(s["rate_done"], after(4 + 1 + 2 * (ATANH_TERMS - 2) + 5))
                with act.Fori(0, L_HEADS) as i:
                    act.wait_ge(product[VB], after(i + 1))
                    act.wait_ge(s["m_done"], after(i))
                    act.activation(vb[:, :], k.ps[1][:, :], ACT.Copy).then_inc(s["vb_kept"], 1)
                    act.wait_ge(s["r_ready"], after(i + 1))
                    act.activation(r[:, :], k.ps[7][:, :], ACT.Sigmoid, bias=col("b_a", i)).then_inc(s["r_done"], 1)
                    act.wait_ge(s["i_ready"], after(i + 1))
                    act.activation(ig[:, :], k.ps[0][:, :], ACT.Sigmoid, bias=col("b_x", i)).then_inc(s["i_done"], 1)
                    act.wait_ge(s["r_done"], after(i + 1))
                    act.activation(tau[:, :], r[:, :], ACT.Tanh, scale=rate[:, 3, bass.ds(i, 1)]).then_inc(s["tau_done"], 1)
                    act.wait_ge(s["sqrt_in"], after(i + 1))
                    act.activation(mult[:, :], den[:, :], ACT.Sqrt, scale=-1.0).then_inc(s["mult_done"], 1)
                    act.wait_ge(product[GA], after(i + 1))
                    act.activation(ge[:, :], k.ps[4][:, :], ACT.Gelu_apprx_tanh).then_inc(s["ge_done"], 1)
                    act.wait_ge(product[MA], after(i + 1))
                    act.activation(sa[:, :], k.ps[5][:, :], ACT.Sigmoid).then_inc(s["sa_done"], 1)
                    act.wait_ge(product[MB], after(i + 1))
                    act.activation(sb_[:, :], k.ps[6][:, :], ACT.Sigmoid).then_inc(s["sb_done"], 1)
                    act.wait_ge(s["m_done"], after(i + 1))
                    act.activation(mhi[:, i, :], h[:, :], ACT.Copy).then_inc(s["hi_done"], 1)


def choose_experts(nc, k, io, src, chosen, residual, acts):
    H, K, LOW = PEER_HEADS, TOPK, -3.0e38
    hi, lo = src
    keys = io["peer_subkeys_2"][0].rearrange("h s n c -> n (h s) c")
    w_dram = io["peer_wq_2"][0].rearrange("(c p) n -> p c n", p=P)
    steps = 4
    per = GROUPS // steps
    heads = H // steps
    sections = 2 * steps
    pairs = TT * heads
    ROW0, MID, CAND = K, K + 7 * 8, K + 7 * 8 + 8
    with ExitStack() as st:
        raw = [k.sb(f"k_raw{b}", [P, DC, SEC], ctx=st) for b in range(2)]
        whi = [k.sb(f"k_whi{b}", [P, DC, SEC], F32R, ctx=st) for b in range(4)]
        wlo = [k.sb(f"k_wlo{b}", [P, DC, SEC], F32R, ctx=st) for b in range(4)]
        qt = k.sb("k_qt", [P, per, T], ctx=st)
        sc = [k.sb(f"k_sc{b}", [P, TT * per, NKEYS], ctx=st) for b in range(2)]
        kt = k.sb("k_t", [P, GROUPS, P], ctx=st)
        rest = k.sb("k_rest", [P, TT * per, NKEYS], ctx=st)
        top = k.sb("k_top", [P, TT * per, K], ctx=st)
        top_i = k.sb("k_top_i", [P, TT * per, K], U32, ctx=st)
        top_f = [k.sb(f"k_top_f{b}", [P, TT * per, K], ctx=st) for b in range(2)]
        cand = k.sb("k_cand", [P, pairs, CAND], ctx=st)
        rest2 = k.sb("k_rest2", [P, pairs, CAND], ctx=st)
        best = k.sb("k_best", [P, steps, pairs, K], ctx=st)
        largest = k.sb("k_largest", [P, steps, pairs], ctx=st)
        total = k.sb("k_total", [P, 2, steps, pairs], ctx=st)
        pos = k.sb("k_pos", [P, pairs, K], U32, ctx=st)
        part = k.sb("k_part", [P, 2, pairs, K], U32, ctx=st)
        eighth = k.sb("k_eighth", [P, 3, pairs, K], ctx=st)
        rank = k.sb("k_rank", [P, 2, pairs, K], ctx=st)
        flat = k.xh[:, :, :].rearrange("p t d -> p (t d)")
        eq = [flat[:, n * pairs * K * K:(n + 1) * pairs * K * K].rearrange("p (m a c) -> p m a c", m=pairs, a=K) for n in range(2)]
        sel = k.sb("k_sel", [P, 3, steps, pairs, K], ctx=st)
        u_dram = io["peer_u_2"][0].rearrange("(p c) d -> p c d", c=NKEYS)
        flat_half = lambda ap, n: ap[:, 4 * n:4 * n + 4, :].rearrange("p c n -> p (c n)")
        u_raw, u_turn = ([flat_half(r, n) for n in range(2)] for r in raw)
        u_hi, u_lo = ([flat_half(w, 0) for w in ws] for ws in (whi, wlo))
        u_act = [kt[:, 4 * n:4 * n + 4, :].rearrange("p g n -> p (g n)") for n in range(4)]
        u_in, u_out = k.sems("k_u_in", 2), k.sems("k_u_out", 4)
        u_turned, u_copied, u_low, u_product, u_made = (
            k.sem(f"k_{n}") for n in ("u_turned", "u_copied", "u_low", "u_product", "u_made"))
        raw_in, w_hi, w_lo = k.sems("k_raw_in", 2), k.sems("k_w_hi", 4), k.sems("k_w_lo", 4)
        product, q_kept, scored = k.sems("k_product", per), k.sems("k_q_kept", per), k.sems("k_scored", per)
        names = ("residual_out", "keys_in", "keys_turned", "sc_kept", "read", "vec", "matched",
                 "reduced", "shifted", "exped", "sel_done", "turned", "pool")
        s = {n: k.sem(f"k_{n}") for n in names}
        keys_of = lambda i: top_f[i % 2][:, :, :].rearrange("p (m s) a -> p s m a", s=2)

        def pick(eng, i, n):
            return eng.tensor_tensor(eq[n][:, :, :, :], eq[n][:, :, :, :],
                                     keys_of(i)[:, n, :, :].unsqueeze(2).to_broadcast([P, pairs, K, K]), ALU.mult)

        def low(eng, sec):
            b = sec % 4
            eng.wait_ge(w_hi[b], after(sec // 4 + 1))
            eng.tensor_tensor(wlo[b][:, :, :], raw[sec % 2][:, :, :], whi[b][:, :, :].bitcast(F32), ALU.subtract
                              ).then_inc(w_lo[b], 1)

        stat = k.sb("k_stat", [P, 4 * TT], ctx=st)
        k.credit()
        xs = [a[:, 8 * n:8 * n + 8, :].rearrange("p g n -> p (g n)") for a in (sc[0], rest) for n in range(2)]
        norm = NormAndTurn(nc, k, "k_norm", src, "norm2", xs, stat)
        with nc.Block() as block:
            @block.sync
            def _(sp):
                for sec in range(sections):
                    if sec >= 2:
                        sp.wait_ge(w_lo[(sec - 2) % 4], after((sec - 2) // 4 + 1))
                    sp.dma_start(raw[sec % 2][:, :, :], w_dram[:, :, sec * SEC:(sec + 1) * SEC]).then_inc(raw_in[sec % 2], 16)
                    if sec == 1:
                        sp.dma_start(sc[1][:, :, :], keys).then_inc(s["keys_in"], 16)
                        sp.dma_start(residual, k.xh[:, :, :]).then_inc(s["residual_out"], 16)
                def load(e):
                    if e >= EARLY:
                        return
                    if e >= 2:
                        sp.wait_ge(u_turned, after(e - 1))
                    sp.dma_start(u_raw[e % 2], u_dram[:, e, :]).then_inc(u_in[e % 2], 16)

                sp.wait_ge(w_lo[2], after(2))
                for e in range(4):
                    load(e)
                for e in range(EARLY):
                    sp.wait_ge(u_made, after(e + 1))
                    sp.dma_start(acts[e], u_act[e % 4]).then_inc(u_out[e % 4], 16)
                    load(e + 4)
                sp.wait_ge(s["residual_out"], after(16))
                for n in range(4):
                    sp.wait_ge(u_out[n], after(16 * (EARLY // 4)))

            @block.tensor
            def _(pe):
                def queries(pair, half, n):
                    b = 2 * half + n // 2
                    if n % 2 == 0:
                        pe.wait_ge(w_lo[b], after(pair + 1))
                    for c in range(DC):
                        for w, x in ((whi, hi), (whi, lo), (wlo, hi)):
                            mm = pe.matmul(k.ps[n][:, :], w[b][:, c, n % 2 * P:(n % 2 + 1) * P], x[:, c, :],
                                           start=(c == 0 and w is whi and x is hi), stop=(c == DC - 1 and w is wlo))
                    return mm

                def scores(i, n):
                    pe.wait_ge(q_kept[n], after(i + 1))
                    for t in range(TT):
                        mm = pe.matmul(k.ps[4 + t][:, n * P:(n + 1) * P], qt[:, n, t * P:(t + 1) * P],
                                       kt[:, i * per + n, :], start=True, stop=True)
                    mm.then_inc(scored[n], 1)

                norm.tensor(pe)
                pe.wait_ge(s["keys_in"], after(16))
                for g in range(GROUPS):
                    mm = pe.transpose(k.ps[4 + g // 4][:, g % 4 * P:(g % 4 + 1) * P], sc[1][:, g, :], k.ident[:, :])
                    if g % 4 == 3:
                        mm.then_inc(s["keys_turned"], 1)
                with pe.Fori(0, steps // 2) as pair:
                    for half in range(2):
                        i = pair * 2 + half
                        for n in range(per):
                            pe.wait_ge(q_kept[n], after(i))
                            queries(pair, half, n).then_inc(product[n], 1)
                            if n == 1:
                                pe.wait_ge(s["sc_kept"], after(i * 4 + 4))
                            if n:
                                scores(i, n - 1)
                        scores(i, per - 1)

                def turn(e):
                    if e >= EARLY:
                        return
                    pe.wait_ge(u_in[e % 2], after(16 * (e // 2 + 1)))
                    if e:
                        pe.wait_ge(u_copied, after(4 * e))
                    else:
                        pe.wait_ge(q_kept[0], after(steps))
                        pe.wait_ge(q_kept[1], after(steps))
                    for c in range(DC):
                        mm = pe.transpose(k.ps[c // 4][:, c % 4 * P:(c % 4 + 1) * P], u_raw[e % 2][:, c * P:(c + 1) * P],
                                          k.ident[:, :])
                    mm.then_inc(u_turned, 1)
                turn(0)
                turn(1)
                for e in range(EARLY):
                    turn(e + 2)
                    pe.wait_ge(u_low, after(e + 1))
                    if e >= 2:
                        pe.wait_ge(u_made, after(e - 1))
                    elif e == 0:
                        pe.wait_ge(s["sc_kept"], after(4 * (steps + 1)))
                    for c in range(DC):
                        for w, x in ((u_hi, hi), (u_hi, lo), (u_lo, hi)):
                            mm = pe.matmul(k.ps[6 + e % 2][:, :], w[e % 4][:, c * P:(c + 1) * P], x[:, c, :],
                                           start=(c == 0 and w is u_hi and x is hi), stop=(c == DC - 1 and w is u_lo))
                    mm.then_inc(u_product, 1)
                pe.wait_ge(s["sel_done"], after(1))
                for t in range(TT):
                    for n in range(3):
                        mm = pe.transpose(k.ps[t][:, n * P:(n + 1) * P],
                                          flat[:, (t * 3 + n) * P:(t * 3 + n + 1) * P], k.ident[:, :])
                    mm.then_inc(s["turned"], 1)

            @block.scalar
            def _(act):
                def high(sec):
                    b = sec % 4
                    act.wait_ge(raw_in[sec % 2], after(16 * (sec // 2 + 1)))
                    if sec >= 4:
                        act.wait_ge(product[2 * (sec % 2) + 1], after(sec // 2 - 1))
                    act.activation(whi[b][:, :, :], raw[sec % 2][:, :, :], ACT.Copy).then_inc(w_hi[b], 1)
                def copy(e):
                    if e >= EARLY:
                        return
                    act.wait_ge(u_turned, after(e + 1))
                    if e >= 2:
                        act.wait_ge(u_low, after(e - 1))
                    else:
                        act.wait_ge(w_lo[3], after(2))
                    if e >= 4:
                        act.wait_ge(u_product, after(e - 3))
                    for f in range(2):
                        half = slice(f * T, (f + 1) * T)
                        act.activation(u_turn[e % 2][:, half], k.ps[f][:, :], ACT.Copy).then_inc(u_copied, 1)
                        act.activation(u_hi[e % 4][:, half], k.ps[f][:, :], ACT.Copy).then_inc(u_copied, 1)
                norm.squares(act)
                high(0)
                high(1)
                norm.highs(act)
                for n in range(4):
                    act.wait_ge(s["keys_turned"], after(n + 1))
                    act.activation(kt[:, 4 * n:4 * n + 4, :].rearrange("p g n -> p (g n)"), k.ps[4 + n][:, :], ACT.Copy
                                   ).then_inc(s["sc_kept"], 1)
                high(2)
                high(3)
                for i in range(steps):
                    for n in range(per):
                        act.wait_ge(product[n], after(i + 1))
                        if i:
                            act.wait_ge(scored[n], after(i))
                        act.activation(qt[:, n, :], k.ps[n][:, :], ACT.Copy).then_inc(q_kept[n], 1)
                        if n % 2 and i + 2 < steps:
                            high(2 * (i + 2) + n // 2)
                    if i == steps - 1:
                        copy(0)
                    for n in range(per):
                        act.wait_ge(scored[n], after(i + 1))
                    if i >= 2:
                        act.wait_ge(s["read"], after(i - 1))
                    for t in range(TT):
                        act.activation(sc[i % 2][:, per * t:per * (t + 1), :].rearrange("p g n -> p (g n)"), k.ps[4 + t][:, :],
                                       ACT.Copy).then_inc(s["sc_kept"], 1)
                copy(1)
                for e in range(EARLY):
                    copy(e + 2)
                    if e == EARLY - 1:
                        act.wait_ge(s["shifted"], after(steps))
                        act.activation(best[:, :, :, :], best[:, :, :, :], ACT.Exp).then_inc(s["exped"], 1)
                    act.wait_ge(u_product, after(e + 1))
                    if e >= 4:
                        act.wait_ge(u_out[e % 4], after(16 * (e // 4)))
                    act.activation(u_act[e % 4], k.ps[6 + e % 2][:, :], ACT.Gelu_apprx_tanh).then_inc(u_made, 1)
                for t in range(TT):
                    act.wait_ge(s["turned"], after(t + 1))
                    act.activation(chosen[:, :, t * P:(t + 1) * P], k.ps[t][:, 0:3 * P].rearrange("p (n t) -> p n t", n=3), ACT.Copy)

            @block.gpsimd
            def _(pool):
                order = Chain(pool, s["pool"], done=1)

                def select(i, n):
                    pool.wait_ge(s["matched"], after(2 * i + n + 1))
                    order(pick(pool, i, n))
                    for w in (8, 4, 2):
                        order(pool.tensor_tensor(eq[n][:, :, :, 0:w], eq[n][:, :, :, 0:w], eq[n][:, :, :, w:2 * w], ALU.add))
                    pool.tensor_tensor(sel[:, n, i, :, :], eq[n][:, :, :, 0], eq[n][:, :, :, 1], ALU.add
                                       ).then_inc(s["reduced"], 1)
                low(pool, 4)
                low(pool, 5)
                low(pool, 6)
                select(0, 0)
                select(0, 1)
                low(pool, 7)
                select(1, 0)
                select(1, 1)

                def low_early(e):
                    pool.wait_ge(u_copied, after(4 * (e + 1)))
                    pool.tensor_tensor(u_lo[e % 4], u_turn[e % 2], u_hi[e % 4].bitcast(F32), ALU.subtract).then_inc(u_low, 1)
                for e in range(5):
                    low_early(e)
                select(2, 0)
                for e in range(5, EARLY - 1):
                    low_early(e)
                select(2, 1)
                low_early(EARLY - 1)

            @block.vector
            def _(dve):
                order = Chain(dve, s["vec"], done=1)

                norm.scale(dve)
                for sec in range(2):
                    low(dve, sec)
                norm.lows(dve)
                for sec in range(2, 4):
                    low(dve, sec)
                for i in range(steps):
                    b, tops = i % 2, top[:, :, :].rearrange("p (m s) a -> p s m a", s=2)
                    if i >= 2:
                        dve.wait_ge(s["reduced"], after(2 * (i - 1)))
                    for t in range(TT):
                        dve.wait_ge(s["sc_kept"], after(4 * (i + 1) + t + 1))
                        for g in range(per * t, per * (t + 1)):
                            order.add(dve.max(top[:, g, 0:8], sc[b][:, g, :]))
                    order.wait()
                    for g in range(TT * per):
                        order.add(dve.max_index(top_i[:, g, 0:8], top[:, g, 0:8], sc[b][:, g, :]))
                        order.add(dve.match_replace(rest[:, g, :], top[:, g, 0:8], sc[b][:, g, :], LOW))
                    order.wait()
                    dve.sem_inc(s["read"], 1)
                    for g in range(TT * per):
                        order.add(dve.max(top[:, g, 8:16], rest[:, g, :]))
                    order.wait()
                    for g in range(TT * per):
                        order.add(dve.max_index(top_i[:, g, 8:16], top[:, g, 8:16], rest[:, g, :]))
                    order.wait()
                    order.add(dve.tensor_copy(top_f[b][:, :, :], top_i[:, :, :]))
                    first = lambda a0, a1, n: tops[:, 0, :, a0:a1].unsqueeze(3).to_broadcast([P, pairs, a1 - a0, n])
                    second = lambda rows, n: tops[:, 1, :, 0:n].unsqueeze(2).to_broadcast([P, pairs, rows, n])
                    for at, a0, a1, n in ((0, 0, 1, K), (ROW0, 1, 8, 8), (MID, 8, K, 1)):
                        order.add(dve.tensor_tensor(cand[:, :, at:at + (a1 - a0) * n].rearrange("p m (a c) -> p m a c", c=n),
                                                    first(a0, a1, n), second(a1 - a0, n), ALU.add))
                    order.wait()
                    for m in range(pairs):
                        order.add(dve.max(best[:, i, m, 0:8], cand[:, m, :]))
                    order.wait()
                    for m in range(pairs):
                        order.add(dve.max_index(pos[:, m, 0:8], best[:, i, m, 0:8], cand[:, m, :]))
                        order.add(dve.match_replace(rest2[:, m, :], best[:, i, m, 0:8], cand[:, m, :], LOW))
                    order.wait()
                    for m in range(pairs):
                        order.add(dve.max(best[:, i, m, 8:16], rest2[:, m, :]))
                    order.wait()
                    for m in range(pairs):
                        order.add(dve.max_index(pos[:, m, 8:16], best[:, i, m, 8:16], rest2[:, m, :]))
                    order.wait()
                    order.add(dve.tensor_copy(largest[:, i, :], best[:, i, :, 0]))
                    order.add(dve.tensor_scalar(part[:, 0, :, :], pos[:, :, :], 3, None, ALU.logical_shift_right))
                    order(dve.tensor_scalar(part[:, 1, :, :], pos[:, :, :], 7, None, ALU.bitwise_and))
                    dve.tensor_tensor(best[:, i, :, :], best[:, i, :, :], largest[:, i, :].unsqueeze(2).to_broadcast([P, pairs, K]),
                                      ALU.subtract).then_inc(s["shifted"], 1)
                    order(dve.tensor_copy(eighth[:, 0:2, :, :], part[:, :, :, :]))
                    q, r, last = (eighth[:, n, :, :] for n in range(3))
                    order.add(dve.tensor_scalar(rank[:, 0, :, :], q, 1.0, 0.0, ALU.subtract, ALU.max))
                    order.add(dve.tensor_scalar(rank[:, 1, :, :], q, 1.0, 8.0, ALU.is_equal, ALU.mult))
                    order(dve.scalar_tensor_tensor(out=last, in0=q, scalar=float(MID // 8), in1=r, op0=ALU.is_equal, op1=ALU.mult))
                    order.add(dve.tensor_tensor(rank[:, 0, :, :], rank[:, 0, :, :], last, ALU.add))
                    order(dve.tensor_tensor(r, r, last, ALU.subtract))
                    order(dve.tensor_tensor(rank[:, 1, :, :], rank[:, 1, :, :], r, ALU.add))
                    if i:
                        dve.wait_ge(s["reduced"], after(2 * i))
                    else:
                        dve.wait_ge(s["residual_out"], after(16))
                    for n in range(2):
                        dve.tensor_tensor(eq[n][:, :, :, :], rank[:, n, :, :].unsqueeze(3).to_broadcast([P, pairs, K, K]),
                                          k.row[:, 0:K].unsqueeze(1).unsqueeze(1).to_broadcast([P, pairs, K, K]), ALU.is_equal
                                          ).then_inc(s["matched"], 1)
                for n in range(2):
                    dve.wait_ge(s["matched"], after(2 * steps - 1 + n))
                    order(pick(dve, steps - 1, n))
                    dve.tensor_reduce(sel[:, n, steps - 1, :, :], eq[n][:, :, :, :], AX_X, ALU.add).then_inc(s["reduced"], 1)
                dve.wait_ge(s["exped"], after(1))
                order(dve.tensor_reduce(total[:, 0, :, :], best[:, :, :, :], AX_X, ALU.add))
                order(dve.reciprocal(total[:, 1, :, :], total[:, 0, :, :]))
                order(dve.tensor_tensor(sel[:, 2, :, :, :].rearrange("p i m a -> p (i m) a"),
                                        best[:, :, :, :].rearrange("p i m a -> p (i m) a"),
                                        total[:, 1, :, :].rearrange("p i m -> p (i m)").unsqueeze(2).to_broadcast([P, steps * pairs, K]), ALU.mult))
                dve.wait_ge(s["reduced"], after(2 * steps))
                for t in range(TT):
                    for n in range(3):
                        ins = dve.tensor_copy(flat[:, (t * 3 + n) * P:(t * 3 + n + 1) * P].rearrange("p (i r) -> p i r", i=steps),
                                              sel[:, n, :, heads * t:heads * (t + 1), :].rearrange("p i h a -> p i (h a)"))
                        if t == TT - 1 and n == 2:
                            order.wait()
                            ins.then_inc(s["sel_done"], 1)
                        else:
                            order.add(ins)


PER = 4
TOK_TILE = T // EXPERT_TILES
CHUNK_TILES = P // TOK_TILE


def first_products(nc, k, io, src, chosen, acts, weights, spread):
    hi, lo = src
    u_dram = io["peer_u_2"][0].rearrange("(p c) d -> p c d", c=NKEYS)
    chunks = T // P
    pieces = 16
    with ExitStack() as st:
        raw = [k.xh[:, b, :] for b in range(2)]
        ga = [k.xh[:, 2, b * T:(b + 1) * T] for b in range(2)]
        one = k.sb("u_one", [P, TOK_TILE, P], F32R, ctx=st)
        two = k.sb("u_two", [P, TOK_TILE, 2, P], F32R, ctx=st)
        weight_hi = k.xh[:, 3, 0:T].bitcast(F32R)
        weight_lo = k.sb("u_weight_lo", [P, T], ctx=st)
        uhi = [k.sb(f"u_hi{s}", [P, DC, P], F32R, ctx=st) for s in range(2)]
        ulo = [k.sb(f"u_lo{s}", [P, DC, P], F32R, ctx=st) for s in range(2)]
        names = ("raw_in", "turned", "hi_done", "lo_done", "product", "ga_done", "ga_out", "stored")
        s = {n: k.sems(f"u_{n}", 2) for n in names}
        weight_split, one_done, spread_ready, high_kept, spread_kept = (
            k.sem(f"u_{n}") for n in ("weight_split", "one_done", "spread_ready", "high_kept", "spread_kept"))
        half = PER // 2
        extra = EARLY // 2
        SIX = PER + 2
        chunk_rounds = lambda c: (CHUNK_TILES * c - EARLY) // PER
        segments = [(0, 0, extra, SIX), (0, extra, chunk_rounds(1), PER)]
        segments += [(c, chunk_rounds(c), chunk_rounds(c + 1), PER) for c in range(1, chunks)]
        tiles = EXPERT_TILES - EARLY

        def loop(eng, body, chunk=lambda c: None):
            for c, first, last, steps in segments:
                chunk(c)
                with eng.Fori(first, last) as n:
                    body(n, c, steps)

        def spread_steps(n, u, steps):
            end = DC - 1
            if steps == SIX:
                return [(n * SIX + v, c) for v, c in (((0, 4),), ((1, 1), (2, end)), ((3, 4),), ((4, 1), (5, end)))[u]]
            return [(n * PER + (u + EARLY), end)]

        def place(n, u):
            return u % 2, n * half + u // 2

        def places(c, step, m):
            return (spread[:, c % 2, :, bass.ds(step * TOK_TILE + (2 * m - c * P), 2)],
                    k.ps[6 + m][:, :].rearrange("p (q h n) -> p h n q", q=2, h=2))

        k.credit()
        piece_out = k.sems("u_piece_out", 2)
        with nc.Block() as block:
            @block.sync
            def _(sp):
                def load(n, u):
                    b, before = place(n, u)
                    sp.wait_ge(s["turned"][b], after(before * 2))
                    sp.dma_start(raw[b], u_dram[:, bass.ds((n * PER + (u + EARLY)) % EXPERT_TILES, 1), :].rearrange("p a d -> p (a d)")
                                 ).then_inc(s["raw_in"][b], 16)

                def body(n, c, steps):
                    for u in range(PER):
                        load(n, u + 1)
                load(0, 0)
                loop(sp, body)

            @block.gpsimd
            def _(pool):
                step = NKEYS // pieces
                for parity in range(2):
                    pool.wait_ge(spread_kept, after((parity + 1) * CHUNK_TILES * 2))
                    for at in range(0, NKEYS, step):
                        pool.dma_start(weights[at:at + step, :, parity * P:(parity + 1) * P].rearrange("n p t -> p n t"),
                                       spread[:, parity, at:at + step, :]).then_inc(piece_out[parity], 16)
                    pool.wait_ge(piece_out[parity], 16 * pieces)
                    pool.sem_inc(s["stored"][parity], 1)

            @block.tensor
            def _(pe):
                def turn(n, u):
                    b, before = place(n, u)
                    pe.wait_ge(s["raw_in"][b], after(before * 16 + 16))
                    pe.wait_ge(s["lo_done"][b], after(before * 2))
                    for f in range(2):
                        for c in range(4 * f, 4 * f + 4):
                            mm = pe.transpose(k.ps[2 * b + f][:, c % 4 * P:(c % 4 + 1) * P], raw[b][:, c * P:(c + 1) * P], k.ident[:, :])
                        mm.then_inc(s["turned"][b], 1)

                def spread_tokens(step):
                    pe.wait_ge(one_done, after(step * (3 * TOK_TILE) + 3 * TOK_TILE))
                    pe.wait_ge(spread_kept, after(step * 2))
                    for q in range(TOK_TILE):
                        mm = pe.matmul(k.ps[6 + q // 2][:, q % 2 * 2 * P:(q % 2 + 1) * 2 * P], one[:, q, :],
                                       two[:, q, :, :].rearrange("p h n -> p (h n)"), start=True, stop=True)
                    mm.then_inc(spread_ready, 1)

                def multiply(n, u, steps):
                    b, before = place(n, u)
                    pe.wait_ge(s["ga_done"][b], after(before))
                    for c in range(DC):
                        if c % 4 == 0:
                            pe.wait_ge(s["lo_done"][b], after(before * 2 + (c // 4 + 1)))
                        for w, x in ((uhi, hi), (uhi, lo), (ulo, hi)):
                            mm = pe.matmul(k.ps[4 + b][:, :], w[b][:, c, :], x[:, c, :], start=(c == 0 and w is uhi and x is hi),
                                           stop=(c == DC - 1 and w is ulo))
                        if c == DC - 1:
                            mm.then_inc(s["product"][b], 1)
                        for step, at in spread_steps(n, u, steps):
                            if at == c:
                                spread_tokens(step)

                def body(n, c, steps):
                    for u in range(PER):
                        turn(n, u + 1)
                        multiply(n, u, steps)
                turn(0, 0)
                loop(pe, body)

            @block.vector
            def _(dve):
                def low(n, u):
                    b, before = place(n, u)
                    for f in range(2):
                        dve.wait_ge(s["hi_done"][b], after(before * 2 + (f + 1)))
                        dve.tensor_tensor(ulo[b][:, 4 * f:4 * f + 4, :], k.ps[2 * b + f][:, :].rearrange("p (c n) -> p c n", c=4),
                                          uhi[b][:, 4 * f:4 * f + 4, :].bitcast(F32), ALU.subtract).then_inc(s["lo_done"][b], 1)

                def onehots(step):
                    for q in range(TOK_TILE):
                        at = bass.ds((step * TOK_TILE + q) % T, 1)
                        dve.tensor_scalar(one[:, q, :], k.row[:, :], chosen[:, 0, at], None, ALU.is_equal).then_inc(one_done, 1)
                        for h, part in enumerate((chosen[:, 2, at], weight_lo[:, at])):
                            dve.tensor_scalar(two[:, q, h, :], k.row[:, :], chosen[:, 1, at], part,
                                              ALU.is_equal, ALU.mult).then_inc(one_done, 1)

                def keep(c, step):
                    for m in range(2):
                        dve.wait_ge(high_kept, after(step * 2 + (m + 1)))
                        to, parts = places(c, step, m)
                        dve.tensor_tensor(to, to, parts[:, 1, :, :], ALU.add).then_inc(spread_kept, 1)

                def body(n, c, steps):
                    for u in range(PER):
                        low(n, u + 1)
                        for step, _ in spread_steps(n, u, steps):
                            dve.wait_ge(spread_ready, after(step + 1))
                            onehots(step + 1)
                            keep(c, step)

                dve.tensor_copy(weight_hi, chosen[:, 2, :]).then_inc(weight_split, 1)
                dve.wait_ge(weight_split, after(1))
                dve.tensor_tensor(weight_lo[:, :], chosen[:, 2, :], weight_hi.bitcast(F32), ALU.subtract).then_inc(weight_split, 1)
                dve.wait_ge(weight_split, after(2))
                low(0, 0)
                onehots(0)
                loop(dve, body)

            @block.scalar
            def _(act):
                def high(n, u):
                    b, before = place(n, u)
                    act.wait_ge(s["product"][b], after(before))
                    for f in range(2):
                        act.wait_ge(s["turned"][b], after(before * 2 + (f + 1)))
                        act.activation(uhi[b][:, 4 * f:4 * f + 4, :], k.ps[2 * b + f][:, :].rearrange("p (c n) -> p c n", c=4),
                                       ACT.Copy).then_inc(s["hi_done"][b], 1)

                def spread_high(c, step):
                    act.wait_ge(spread_ready, after(step + 1))
                    for m in range(2):
                        to, parts = places(c, step, m)
                        act.activation(to, parts[:, 0, :, :], ACT.Copy).then_inc(high_kept, 1)

                def keep(n, u, c, steps):
                    b, before = place(n, u)
                    for step, at in spread_steps(n, u, steps):
                        if at < DC - 1:
                            spread_high(c, step)
                    act.wait_ge(s["product"][b], after(before + 1))
                    act.wait_ge(s["ga_out"][b], after(before * 16))
                    act.activation(ga[b], k.ps[4 + b][:, :], ACT.Gelu_apprx_tanh).then_inc(s["ga_done"][b], 1)
                    for step, at in spread_steps(n, u, steps):
                        if at == DC - 1:
                            spread_high(c, step)
                    act.wait_ge(s["ga_done"][b], after(before + 1))
                    act.dma_start(acts[bass.ds(n * PER + (u + EARLY), 1), :, :].rearrange("a p t -> (a p) t"), ga[b]
                                  ).then_inc(s["ga_out"][b], 16)

                def body(n, c, steps):
                    for u in range(PER):
                        high(n, u + 1)
                        keep(n, u, c, steps)

                def chunk(c):
                    if c >= 2:
                        act.wait_ge(s["stored"][c % 2], after(1))
                high(0, 0)
                loop(act, body, chunk)
                for b in range(2):
                    act.wait_ge(s["ga_out"][b], after(16 * tiles // 2))


def second_products(nc, k, io, src, acts, weights, spread, residual, out):
    out_t = out[0].rearrange("(t p) d -> t p d", p=P)
    v_dram = io["peer_v_2"][0].rearrange("(p c) d -> p c d", c=NKEYS)
    with ExitStack() as st:
        raw = [k.xh[:, u, :] for u in range(PER)]
        ga = [k.sb(f"v_ga{u}", [P, T], ctx=st) for u in range(PER)]
        gg = [k.sb(f"v_gg{u}", [P, T // 2], ctx=st) for u in range(PER)]
        h32 = [k.sb(f"v_h{b}", [P, T], ctx=st) for b in range(2)]
        vhi, vlo = ([x[:, 2 * b:2 * b + 2, :].rearrange("p c t -> p (c t)") for b in range(2)] for x in src)
        hhi, hlo = ([x[:, 4 + b, :] for b in range(2)] for x in src)
        zero = k.sb("v_zero", [P, T], ctx=st)
        v_in, ga_in, gg_in = (k.sems(f"v_{n}", PER) for n in ("in", "ga_in", "gg_in"))
        slot_v, slot_h = k.sems("v_split_slot", PER), k.sems("v_weighted_slot", PER)
        s = {n: k.sems(f"v_{n}", 2) for n in ("vhi_done", "hhi_done", "hlo_done", "used")}
        zeroed = k.sem("v_zeroed")
        rounds, half = EXPERT_TILES // PER, PER // 2
        place = lambda n, u: (u % 2, n * half + u // 2)
        tiles_at = lambda parity, at, n: spread[:, parity, at:at + DC * n, :].rearrange("p (t a) n -> p t (a n)", t=n)
        y, junk, gain = tiles_at(0, 0, TT), tiles_at(1, 0, 2), tiles_at(1, 2 * DC, 1)[:, 0, :]
        stat = k.sb("v_stat", [P, 4, TT], ctx=st)
        k.credit()
        gain_in, res_in, closed, added, squared, rooted, vec, done, stored = (
            k.sem(f"v_{n}") for n in ("gain_in", "res_in", "closed", "added", "squared", "rooted", "vec", "done", "stored"))
        with nc.Block() as block:
            @block.sync
            def _(sp):
                with sp.Fori(0, rounds) as n:
                    for u in range(PER):
                        at = bass.ds(n * PER + u, 1)
                        sp.wait_ge(slot_v[u], after(n))
                        sp.dma_start(raw[u], v_dram[:, at, :].rearrange("p a d -> p (a d)")).then_inc(v_in[u], 16)
                        sp.wait_ge(slot_h[u], after(n * 2))
                        sp.dma_start(ga[u][:, :], acts[at, :, :].rearrange("a p t -> (a p) t")).then_inc(ga_in[u], 16)
                        sp.dma_start(gg[u][:, :], weights[at, :, :].rearrange("a p t -> (a p) t")).then_inc(gg_in[u], 16)
                for u in range(PER):
                    sp.wait_ge(slot_v[u], after(rounds))
                    sp.wait_ge(slot_h[u], after(2 * rounds))
                sp.dma_start(k.xh[:, :, :], residual).then_inc(res_in, 16)
                sp.dma_start(gain, io["final_g_2"].partition_broadcast(P)).then_inc(gain_in, 16)
                for t in range(TT):
                    sp.wait_ge(done, t + 1)
                    sp.dma_start(out_t[t], y[:, t, :]).then_inc(stored, 16)
                sp.wait_ge(stored, 16 * TT)

            @block.vector
            def _(dve):
                dve.memset(zero[:, :], 0.0).then_inc(zeroed, 1)
                with dve.Fori(0, rounds) as n:
                    for u in range(PER):
                        b, before = place(n, u)
                        dve.wait_ge(ga_in[u], after(n * 16 + 16))
                        dve.wait_ge(gg_in[u], after(n * 16 + 16))
                        dve.wait_ge(s["hlo_done"][b], after(before))
                        dve.tensor_tensor(h32[b][:, 0:T // 2], ga[u][:, 0:T // 2], gg[u][:, :], ALU.mult).then_inc(slot_h[u], 1)
                        halves = lambda ap: ap[:, T // 2:T].rearrange("p (a t) -> p a t", a=2)
                        dve.tensor_tensor(halves(h32[b]), halves(ga[u]), spread[:, :, n * PER + u, :], ALU.mult
                                          ).then_inc(slot_h[u], 1)
                        dve.wait_ge(s["vhi_done"][b], after(before + 1))
                        dve.tensor_tensor(vlo[b], raw[u], vhi[b].bitcast(F32), ALU.subtract).then_inc(slot_v[u], 1)
                        dve.wait_ge(s["hhi_done"][b], after(before + 1))
                        dve.wait_ge(slot_h[u], after(n * 2 + 2))
                        dve.tensor_tensor(hlo[b], h32[b][:, :], hhi[b].bitcast(F32), ALU.subtract).then_inc(s["hlo_done"][b], 1)

                chain = Chain(dve, vec)

                def add(t):
                    dve.wait_ge(closed, t + 1)
                    for q in (2 * t, 2 * t + 1):
                        f = slice(q % 2 * T, q % 2 * T + T)
                        dve.tensor_tensor(k.xh[:, t, f], k.xh[:, t, f], k.ps[q][:, :], ALU.add).then_inc(added, 1)
                dve.wait_ge(res_in, 16)
                add(0)
                for t in range(TT):
                    if t + 1 < TT:
                        add(t + 1)
                    dve.wait_ge(rooted, t + 1)
                    total, root, inverse, tmp = (stat[:, n, t:t + 1] for n in range(4))
                    refined_rsqrt(chain, dve, inverse, root, total, tmp, 1.0 / D)
                    if t == 0:
                        dve.wait_ge(gain_in, 16)
                    dve.wait_ge(added, 2 * t + 2)
                    dve.scalar_tensor_tensor(out=y[:, t, :], in0=k.xh[:, t, :], scalar=inverse, in1=gain,
                                             op0=ALU.mult, op1=ALU.mult).then_inc(done, 1)

            @block.scalar
            def _(act):
                with act.Fori(0, rounds) as n:
                    for u in range(PER):
                        b, before = place(n, u)
                        act.wait_ge(v_in[u], after(n * 16 + 16))
                        act.wait_ge(s["used"][b], after(before))
                        act.activation(vhi[b], raw[u], ACT.Copy).then_inc(s["vhi_done"][b], 1)
                        act.wait_ge(slot_h[u], after(n * 2 + 2))
                        act.activation(hhi[b], h32[b][:, :], ACT.Copy).then_inc(s["hhi_done"][b], 1)
                for u in range(PER):
                    act.wait_ge(slot_h[u], after(2 * rounds))
                for t in range(TT):
                    act.wait_ge(added, 2 * t + 2)
                    if t >= 2:
                        act.wait_ge(squared, t - 1)
                    act.activation(junk[:, t % 2, :], k.xh[:, t, :], ACT.Square, accum_out=stat[:, 0, t:t + 1]).then_inc(squared, 1)
                    act.wait_ge(squared, t + 1)
                    act.activation(stat[:, 1, t:t + 1], stat[:, 0, t:t + 1], ACT.Sqrt, scale=1.0 / D, bias=k.eps[:, 0:1]
                                   ).then_inc(rooted, 1)

            @block.tensor
            def _(pe):
                pe.wait_ge(zeroed, after(1))
                for q in range(2 * TT):
                    pe.matmul(k.ps[q][:, :], zero[:, 0:P], zero[:, :], start=True, stop=False, skip_group_check=True)

                def multiply(b, q):
                    t, f = q // 2, slice(q % 2 * T, q % 2 * T + T)
                    for h, v in ((hhi, vhi), (hhi, vlo), (hlo, vhi)):
                        mm = pe.matmul(k.ps[q][:, :], h[b][:, t * P:(t + 1) * P], v[b][:, f], start=False, stop=False,
                                       skip_group_check=True)
                    return mm

                def ready(n, u):
                    b, before = place(n, u)
                    pe.wait_ge(slot_v[u], after(n + 1))
                    pe.wait_ge(s["hlo_done"][b], after(before + 1))
                    return b

                def tile(n, u):
                    b = ready(n, u)
                    for q in range(2 * TT):
                        mm = multiply(b, q)
                    mm.then_inc(s["used"][b], 1)

                with pe.Fori(0, rounds - 1) as n:
                    for u in range(PER):
                        tile(n, u)
                for u in range(PER - 2):
                    tile(rounds - 1, u)
                last = [ready(rounds - 1, u) for u in (PER - 2, PER - 1)]
                for t in range(TT):
                    for q in (2 * t, 2 * t + 1):
                        for b in last:
                            multiply(b, q)
                        mm = pe.matmul(k.ps[q][:, :], zero[:, 0:P], zero[:, :], start=False, stop=True, skip_group_check=True)
                    mm.then_inc(closed, 1)


def build(nc, io, out):
    with ExitStack() as ctx:
        k = Kit(nc, ctx)
        k.ps = [ctx.enter_context(nc.psum_tensor(f"bank{b}", [P, T], F32)) for b in range(8)]
        k.ident = k.sb("ident", [P, P])
        k.cols = k.sb("cols", [P, NCOLS])
        k.eps = k.sb("eps", [P, 1])
        k.row = k.sb("row", [P, NKEYS])
        k.xh = k.sb("xh", [P, TT, D])
        with ExitStack() as st:
            k.ones = k.sb("ones", [P, P], ctx=st)
            k.upto, k.later = k.sb("upto", [P, P], ctx=st), k.sb("later", [P, P], ctx=st)
            k.level = k.sb("level", [P, LEVELS, P], ctx=st)
            k.qk_scale = k.sb("qk_scale", [P, G_HEADS], ctx=st)
            w8 = k.sb("w8", [P, DC, BA], ctx=st)
            load_constants(nc, k, io, w8)
            k.end_stage()
            mixed = k.sb("mixed", [P, TT, D], ctx=st)
            proj = k.sb("proj", [P, PROJ, T], ctx=st)
            gates = (k.sb("beta", [P, TT, G_HEADS], ctx=st), k.sb("g", [P, TT, G_HEADS], ctx=st))
            with ExitStack() as st2:
                xt = (k.sb("xt_hi", [P, DC, T], F32R, ctx=st2), k.sb("xt_lo", [P, DC, T], F32R, ctx=st2))
                project_first(nc, k, io, xt, w8, proj, gates)
                k.end_stage()
            attention(nc, k, proj, mixed)
            k.end_stage()
            o = mixed[:, :, A_HEADS * A_DH:D]
            with ExitStack() as st2:
                qkv = proj[:, DQ0:DZ0, :]
                kept = {n: proj[:, at:at + TT, :].rearrange("p c (h n) -> p c h n", h=G_HEADS)
                        for n, at in (("intra", Q0), ("inv", K0), ("kdec", V0))}
                kept["v"] = k.sb("kept_v", [P, TT, G_HEADS, P], ctx=st2)
                kept["rates"] = k.sb("kept_rates", [P, TT, 2, G_HEADS], ctx=st2)
                delta_prepare(nc, k, qkv, gates, kept)
                k.end_stage()
                delta_scan(nc, k, gates, kept, qkv, o)
                k.end_stage()
            with ExitStack() as st2:
                xt = (k.sb("mt_hi", [P, DC, T], F32R, ctx=st2), k.sb("mt_lo", [P, DC, T], F32R, ctx=st2))
                gate_and_turn(nc, k, io, mixed, proj, xt)
                k.end_stage()
                project_out(nc, k, "o1", io["w_out"][0], xt, post=io["norm_post_w"][0])
                k.end_stage()
        with ExitStack() as st:
            mt = (k.sb("g_hi", [P, DC, T], F32R, ctx=st), k.sb("g_lo", [P, DC, T], F32R, ctx=st))
            with ExitStack() as st2:
                xt = (k.sb("xt2_hi", [P, DC, T], F32R, ctx=st2), k.sb("xt2_lo", [P, DC, T], F32R, ctx=st2))
                norm_and_turn(nc, k, "n2", xt, "norm1")
                k.end_stage()
                mixers(nc, k, io, xt, mt)
                k.end_stage()
            project_out(nc, k, "o2", io["w_out_2"][0], mt)
            k.end_stage()
        residual = nc.dram_tensor("residual", (P, TT, D), F32, kind="Internal").ap()
        acts = nc.dram_tensor("acts", (EXPERT_TILES, P, T), F32, kind="Internal").ap()
        weights = nc.dram_tensor("weights", (EXPERT_TILES, P, T // 2), F32, kind="Internal").ap()
        with ExitStack() as st:
            chosen = k.sb("chosen", [P, 3, T], ctx=st)
            xt = (k.sb("xt3_hi", [P, DC, T], F32R, ctx=st), k.sb("xt3_lo", [P, DC, T], F32R, ctx=st))
            choose_experts(nc, k, io, xt, chosen, residual, acts)
            k.end_stage()
            spread = k.sb("u_spread", [P, 2, NKEYS, P], ctx=st)
            first_products(nc, k, io, xt, chosen, acts, weights, spread)
            k.end_stage()
            second_products(nc, k, io, xt, acts, weights, spread, residual, out)
            k.end_stage()


_INS = ["x", "norm_pre_w", "w_in", "conv_w", "a_log", "dt_bias", "gdn_norm_w", "w_out", "norm_post_w", "norm1_g_2",
        "w_in_2", "conv_a_w_2", "conv_a_b_2", "w_a_2", "b_a_2", "w_x_2", "b_x_2", "lru_lambda_2", "conv_b_w_2",
        "w_out_2", "norm2_g_2", "peer_wq_2", "peer_subkeys_2", "peer_u_2", "peer_v_2", "final_g_2"]


def kernel(**inputs):
    import numpy as _np
    import concourse.bacc as _bacc
    from concourse.bass_utils import run_bass_kernel_spmd as _run

    nc = _bacc.Bacc("TRN2", target_bir_lowering=False, num_devices=1)
    arrays, io = {}, {}
    for name in _INS:
        a = _np.ascontiguousarray(inputs[name])
        arrays[f"in_{name}_dram"] = a
        io[name] = nc.dram_tensor(f"in_{name}_dram", a.shape, mybir.dt.from_np(a.dtype), kind="ExternalInput").ap()
    out = nc.dram_tensor("out_dram", (1, T, D), F32, kind="ExternalOutput").ap()
    build(nc, io, out)
    r = _run(nc, [arrays], core_ids=[0])
    return r.results[0]["out_dram"]
```
